# Optimizing a Trainium2 kernel written in Bass

```python
import math
import jax, jax.numpy as jnp
from jax import lax
import numpy as np

D_MODEL = 1024
BATCH = 1
SEQ = 256
DEPTH = 1

CHUNK = 64
Q_BLOCK = 128
MIX_WIDTH = D_MODEL
CONV_CH = MIX_WIDTH // 2
CONV_K = 31
N_HEADS = 8
V_HEAD_DIM = (MIX_WIDTH - CONV_CH) // N_HEADS
QK_NOPE_DIM = 64
QK_ROPE_DIM = 32
QK_HEAD_DIM = QK_NOPE_DIM + QK_ROPE_DIM
Q_LORA_RANK = D_MODEL // 4
KV_LORA_RANK = D_MODEL // 8
ROPE_THETA = 10000.0
IN_WIDTH = 2 * CONV_CH + Q_LORA_RANK + KV_LORA_RANK + QK_ROPE_DIM
N_GROUPS = 4
EXPERTS_PER_GROUP = 8
N_EXPERTS = N_GROUPS * EXPERTS_PER_GROUP
TOP_K = 2
D_EXPERT = D_MODEL // 4
EPS = 1e-6


def rms_norm(x, g):
    xf = x.astype(jnp.float32)
    y = xf * lax.rsqrt(jnp.mean(xf * xf, axis=-1, keepdims=True) + EPS)
    return (y * g.astype(jnp.float32)).astype(x.dtype)

def layer_norm(x, g, b):
    xf = x.astype(jnp.float32)
    mu = jnp.mean(xf, axis=-1, keepdims=True)
    var = jnp.mean(jnp.square(xf - mu), axis=-1, keepdims=True)
    y = (xf - mu) * lax.rsqrt(var + EPS)
    return (y * g.astype(jnp.float32) + b.astype(jnp.float32)).astype(x.dtype)

def apply_rope(x, cos, sin):
    x1, x2 = jnp.split(x, 2, axis=-1)
    cos = cos.astype(x.dtype)
    sin = sin.astype(x.dtype)
    return jnp.concatenate([x1 * cos - x2 * sin, x1 * sin + x2 * cos], axis=-1)

def conv_group(val, gate, conv_w, conv_b, ln_g, ln_b):
    u = val * jax.nn.sigmoid(gate)
    kern = conv_w[:, None, :].astype(u.dtype)
    dw = lax.conv_general_dilated(
        u, kern, window_strides=(1,), padding=[(CONV_K - 1, 0)],
        dimension_numbers=("NWC", "WIO", "NWC"),
        feature_group_count=CONV_CH) + conv_b.astype(u.dtype)
    return jax.nn.silu(layer_norm(dw, ln_g, ln_b))

def mla_group(c_q, c_kv, k_rope, cos, sin, q_a_norm, w_q_b, kv_a_norm, w_kv_b,
              q_norm, k_norm):
    b, s, _ = c_q.shape
    q = (rms_norm(c_q, q_a_norm) @ w_q_b).reshape(b, s, N_HEADS, QK_HEAD_DIM)
    kv = (rms_norm(c_kv, kv_a_norm) @ w_kv_b).reshape(b, s, N_HEADS, QK_NOPE_DIM + V_HEAD_DIM)
    k_nope, v = kv[..., :QK_NOPE_DIM], kv[..., QK_NOPE_DIM:]
    k_r = jnp.broadcast_to(k_rope[:, :, None, :], (b, s, N_HEADS, QK_ROPE_DIM))
    k = jnp.concatenate([k_nope, k_r], axis=-1)
    q = rms_norm(q, q_norm)
    k = rms_norm(k, k_norm)
    cos_h, sin_h = cos[:, :, None, :], sin[:, :, None, :]
    q = jnp.concatenate([q[..., :QK_NOPE_DIM], apply_rope(q[..., QK_NOPE_DIM:], cos_h, sin_h)], axis=-1)
    k = jnp.concatenate([k[..., :QK_NOPE_DIM], apply_rope(k[..., QK_NOPE_DIM:], cos_h, sin_h)], axis=-1)

    n_blk = s // Q_BLOCK
    key_chunk = jnp.arange(s) // CHUNK
    scale = QK_HEAD_DIM ** -0.5
    q_blocks = q.reshape(b, n_blk, Q_BLOCK, N_HEADS, QK_HEAD_DIM).swapaxes(0, 1)

    def block_attn(args):
        qb, blk = args
        sc = jnp.einsum("bqhd,bkhd->bhqk", qb, k).astype(jnp.float32) * scale
        q_chunk = (blk * Q_BLOCK + jnp.arange(Q_BLOCK)) // CHUNK
        mask = key_chunk[None, :] <= q_chunk[:, None]
        sc = jnp.where(mask[None, None], sc, -jnp.inf)
        p = jax.nn.softmax(sc, axis=-1).astype(v.dtype)
        return jnp.einsum("bhqk,bkhd->bqhd", p, v)

    out = lax.map(block_attn, (q_blocks, jnp.arange(n_blk)))
    return out.swapaxes(0, 1).reshape(b, s, N_HEADS * V_HEAD_DIM)

def hier_moe(h, w_group, b_group, w_expert, b_expert, w_gate_e, w_up_e, w_down_e):
    n = h.shape[0]
    g_logits = (h @ w_group).astype(jnp.float32) + b_group.astype(jnp.float32)
    g_prob = jax.nn.softmax(g_logits, axis=-1)
    g_top, g_idx = lax.top_k(g_prob, 1)
    e_logits = ((h @ w_expert).astype(jnp.float32) + b_expert.astype(jnp.float32)
                ).reshape(n, N_GROUPS, EXPERTS_PER_GROUP)
    sel = jnp.broadcast_to(g_idx[:, :, None], (n, 1, EXPERTS_PER_GROUP))
    e_in = jnp.take_along_axis(e_logits, sel, axis=1)[:, 0]
    e_prob = jax.nn.softmax(e_in, axis=-1)
    e_top, e_idx = lax.top_k(e_prob, TOP_K)
    w = g_top * e_top / jnp.sum(e_top, axis=-1, keepdims=True)
    glob_idx = g_idx * EXPERTS_PER_GROUP + e_idx
    gates = jnp.sum(jax.nn.one_hot(glob_idx, N_EXPERTS, dtype=jnp.float32) * w[..., None],
                    axis=1).astype(h.dtype)
    y = jnp.zeros_like(h)
    for e in range(N_EXPERTS):
        a = jax.nn.silu(h @ w_gate_e[e]) * (h @ w_up_e[e])
        y = y + gates[:, e:e + 1] * (a @ w_down_e[e])
    return y

def hybrid_layer(x, c, cos, sin, w_ada, b_ada, norm_mix, w_in, conv_w, conv_b,
                 conv_ln_g, conv_ln_b, q_a_norm, w_q_b, kv_a_norm, w_kv_b, q_norm,
                 k_norm, w_out, norm_ffn, w_group, b_group, w_expert, b_expert,
                 w_gate_e, w_up_e, w_down_e):
    b, s, d = x.shape
    mod = jax.nn.silu(c) @ w_ada + b_ada
    sh_a, sc_a, g_a, sh_f, sc_f, g_f = jnp.split(mod, 6, axis=-1)

    h = rms_norm(x, norm_mix) * (1 + sc_a[:, None]) + sh_a[:, None]
    proj = h @ w_in
    o1 = CONV_CH
    o2 = o1 + CONV_CH
    o3 = o2 + Q_LORA_RANK
    o4 = o3 + KV_LORA_RANK
    conv_val, conv_gate, c_q, c_kv, k_rope = jnp.split(proj, [o1, o2, o3, o4], axis=-1)
    y_conv = conv_group(conv_val, conv_gate, conv_w, conv_b, conv_ln_g, conv_ln_b)
    y_attn = mla_group(c_q, c_kv, k_rope, cos, sin, q_a_norm, w_q_b, kv_a_norm,
                       w_kv_b, q_norm, k_norm)
    mixed = jnp.concatenate([y_conv, y_attn], axis=-1) @ w_out
    x = x + g_a[:, None] * mixed

    h2 = rms_norm(x, norm_ffn) * (1 + sc_f[:, None]) + sh_f[:, None]
    y = hier_moe(h2.reshape(b * s, d), w_group, b_group, w_expert, b_expert,
                 w_gate_e, w_up_e, w_down_e).reshape(b, s, d)
    return x + g_f[:, None] * y

def first_inputs(seed: int = 0) -> dict:
    key = jax.random.key(seed)
    ks = jax.random.split(key, 32)
    f32 = jnp.float32

    def nrm(k, shape, scale):
        return jax.random.normal(k, shape, f32) * scale

    def gain(k, n):
        return 1.0 + 0.01 * jax.random.normal(k, (DEPTH, n), f32)

    positions = (jax.random.randint(ks[2], (BATCH, 1), 0, 4096, dtype=jnp.int32)
                 + jnp.arange(SEQ, dtype=jnp.int32)[None, :])
    return {
        "x": nrm(ks[0], (BATCH, SEQ, D_MODEL), 1.0),
        "c": nrm(ks[1], (BATCH, D_MODEL), 1.0),
        "positions": positions,
        "w_ada": nrm(ks[3], (DEPTH, D_MODEL, 6 * D_MODEL), 0.5 * D_MODEL ** -0.5),
        "b_ada": nrm(ks[4], (DEPTH, 6 * D_MODEL), 0.01),
        "norm_mix": gain(ks[5], D_MODEL),
        "w_in": nrm(ks[6], (DEPTH, D_MODEL, IN_WIDTH), D_MODEL ** -0.5),
        "conv_w": nrm(ks[7], (DEPTH, CONV_K, CONV_CH), CONV_K ** -0.5),
        "conv_b": nrm(ks[8], (DEPTH, CONV_CH), 0.01),
        "conv_ln_g": gain(ks[9], CONV_CH),
        "conv_ln_b": nrm(ks[10], (DEPTH, CONV_CH), 0.01),
        "q_a_norm": gain(ks[11], Q_LORA_RANK),
        "w_q_b": nrm(ks[12], (DEPTH, Q_LORA_RANK, N_HEADS * QK_HEAD_DIM), Q_LORA_RANK ** -0.5),
        "kv_a_norm": gain(ks[13], KV_LORA_RANK),
        "w_kv_b": nrm(ks[14], (DEPTH, KV_LORA_RANK, N_HEADS * (QK_NOPE_DIM + V_HEAD_DIM)), KV_LORA_RANK ** -0.5),
        "q_norm": gain(ks[15], QK_HEAD_DIM),
        "k_norm": gain(ks[16], QK_HEAD_DIM),
        "w_out": nrm(ks[17], (DEPTH, MIX_WIDTH, D_MODEL), MIX_WIDTH ** -0.5),
        "norm_ffn": gain(ks[18], D_MODEL),
        "w_group": nrm(ks[19], (DEPTH, D_MODEL, N_GROUPS), D_MODEL ** -0.5),
        "b_group": nrm(ks[20], (DEPTH, N_GROUPS), 0.01),
        "w_expert": nrm(ks[21], (DEPTH, D_MODEL, N_EXPERTS), D_MODEL ** -0.5),
        "b_expert": nrm(ks[22], (DEPTH, N_EXPERTS), 0.01),
        "w_gate_e": nrm(ks[23], (DEPTH, N_EXPERTS, D_MODEL, D_EXPERT), D_MODEL ** -0.5),
        "w_up_e": nrm(ks[24], (DEPTH, N_EXPERTS, D_MODEL, D_EXPERT), D_MODEL ** -0.5),
        "w_down_e": nrm(ks[25], (DEPTH, N_EXPERTS, D_EXPERT, D_MODEL), D_EXPERT ** -0.5),
    }

def first_block(x, c, positions, w_ada, b_ada, norm_mix, w_in, conv_w, conv_b,
              conv_ln_g, conv_ln_b, q_a_norm, w_q_b, kv_a_norm, w_kv_b, q_norm,
              k_norm, w_out, norm_ffn, w_group, b_group, w_expert, b_expert,
              w_gate_e, w_up_e, w_down_e):
    inv_freq = ROPE_THETA ** (-jnp.arange(0, QK_ROPE_DIM, 2, dtype=jnp.float32) / QK_ROPE_DIM)
    ang = positions.astype(jnp.float32)[..., None] * inv_freq
    cos, sin = jnp.cos(ang), jnp.sin(ang)
    for l in range(DEPTH):
        x = hybrid_layer(x, c, cos, sin, w_ada[l], b_ada[l], norm_mix[l], w_in[l],
                         conv_w[l], conv_b[l], conv_ln_g[l], conv_ln_b[l],
                         q_a_norm[l], w_q_b[l], kv_a_norm[l], w_kv_b[l], q_norm[l],
                         k_norm[l], w_out[l], norm_ffn[l], w_group[l], b_group[l],
                         w_expert[l], b_expert[l], w_gate_e[l], w_up_e[l], w_down_e[l])
    return x


DEPTH_2 = 2

N_MIXERS = 2
N_LRU_LAYERS = (DEPTH_2 + 1) // 2
N_POOL_LAYERS = DEPTH_2 // 2
D_FF = 11 * D_MODEL // 4
D_RNN = 5 * D_MODEL // 4
LRU_HEADS = 16
LRU_HEAD_DIM = D_RNN // LRU_HEADS
CONV_WIDTH = 4
LRU_C = 8.0
POOL_WINDOWS = (2, 4, 8, 16)
POOL_GROUPS = len(POOL_WINDOWS)
POOL_GROUP_DIM = D_MODEL // POOL_GROUPS
PLE_DIM = 256
RMS_EPS = 1e-6


def rms_norm_2(x, g):
    xf = x.astype(jnp.float32)
    y = xf * lax.rsqrt(jnp.mean(xf * xf, axis=-1, keepdims=True) + RMS_EPS)
    return (y * g.astype(jnp.float32)).astype(x.dtype)

def swiglu(x, w_gate, w_up, w_down):
    return (jax.nn.silu(x @ w_gate) * (x @ w_up)) @ w_down

def _lin_combine(c1, c2):
    a1, b1 = c1
    a2, b2 = c2
    return a1 * a2, a2 * b1 + b2

def rglru_mixer(x, w_in, conv_w, conv_b, w_a, b_a, w_x, b_x, a_param, w_out):
    B, S, _ = x.shape
    z = x @ w_in
    gate_branch, xb = z[..., :D_RNN], z[..., D_RNN:]
    xp = jnp.pad(xb, ((0, 0), (CONV_WIDTH - 1, 0), (0, 0)))
    xc = conv_b + conv_w[0] * xp[:, 0:S]
    for k in range(1, CONV_WIDTH):
        xc = xc + conv_w[k] * xp[:, k:k + S]
    xh = xc.reshape(B, S, LRU_HEADS, LRU_HEAD_DIM)
    r = jax.nn.sigmoid(jnp.einsum('bshi,hij->bshj', xh, w_a).reshape(B, S, D_RNN) + b_a)
    ig = jax.nn.sigmoid(jnp.einsum('bshi,hij->bshj', xh, w_x).reshape(B, S, D_RNN) + b_x)
    log_a = -LRU_C * r.astype(jnp.float32) * jax.nn.softplus(-a_param.astype(jnp.float32))
    a = jnp.exp(log_a)
    mult = jnp.sqrt(-jnp.expm1(2.0 * log_a))
    bterm = mult * (ig * xc).astype(jnp.float32)
    _, h = lax.associative_scan(_lin_combine, (a, bterm), axis=1)
    y = h.astype(x.dtype) * jax.nn.gelu(gate_branch)
    return y @ w_out

def pool_mixer(x, w, b, scale):
    B, S, _ = x.shape
    xf = x.astype(jnp.float32)
    cs = jnp.cumsum(xf, axis=1)
    t = jnp.arange(S)
    outs = []
    for g, win in enumerate(POOL_WINDOWS):
        lo, hi = g * POOL_GROUP_DIM, (g + 1) * POOL_GROUP_DIM
        c = cs[..., lo:hi]
        prev = jnp.pad(c[:, :S - win], ((0, 0), (win, 0), (0, 0)))
        count = jnp.minimum(t + 1, win).astype(jnp.float32)[None, :, None]
        outs.append((c - prev) / count - xf[..., lo:hi])
    u = jnp.stack(outs, axis=2).astype(x.dtype)
    y = jnp.einsum('bsgc,gcd->bsgd', u, w).reshape(B, S, D_MODEL)
    return (y + b) * scale

def second_inputs(seed: int = 0) -> dict:
    key = jax.random.key(seed)
    ks = iter(jax.random.split(key, 40))

    def nrm(shape, scale):
        return scale * jax.random.normal(next(ks), shape, jnp.float32)

    D, F, L = D_MODEL, D_FF, DEPTH_2
    NL, NP = N_LRU_LAYERS, N_POOL_LAYERS
    x = nrm((BATCH, SEQ, D), 1.0)
    p = nrm((DEPTH_2, BATCH, SEQ, PLE_DIM), 1.0)
    ffn1_norm = 1.0 + nrm((L, D), 0.1)
    ffn1_w_gate = nrm((L, D, F), D ** -0.5)
    ffn1_w_up = nrm((L, D, F), D ** -0.5)
    ffn1_w_down = nrm((L, F, D), F ** -0.5)
    mix_norm = 1.0 + nrm((L, D), 0.1)
    lru_w_in = nrm((NL, D, 2 * D_RNN), D ** -0.5)
    lru_conv_w = nrm((NL, CONV_WIDTH, D_RNN), CONV_WIDTH ** -0.5)
    lru_conv_b = nrm((NL, D_RNN), 0.01)
    lru_w_a = nrm((NL, LRU_HEADS, LRU_HEAD_DIM, LRU_HEAD_DIM), LRU_HEAD_DIM ** -0.5)
    lru_b_a = nrm((NL, D_RNN), 0.01)
    lru_w_x = nrm((NL, LRU_HEADS, LRU_HEAD_DIM, LRU_HEAD_DIM), LRU_HEAD_DIM ** -0.5)
    lru_b_x = nrm((NL, D_RNN), 0.01)
    u = jax.random.uniform(next(ks), (NL, D_RNN), jnp.float32, minval=0.9, maxval=0.999)
    a0 = u ** (1.0 / LRU_C)
    lru_a_param = jnp.log(a0) - jnp.log1p(-a0)
    lru_w_out = nrm((NL, D_RNN, D), D_RNN ** -0.5)
    pool_w = nrm((NP, POOL_GROUPS, POOL_GROUP_DIM, POOL_GROUP_DIM), POOL_GROUP_DIM ** -0.5)
    pool_b = nrm((NP, D), 0.01)
    pool_scale = 1.0 + nrm((NP, D), 0.1)
    ffn2_norm = 1.0 + nrm((L, D), 0.1)
    ffn2_w_gate = nrm((L, D, F), D ** -0.5)
    ffn2_w_up = nrm((L, D, F), D ** -0.5)
    ffn2_w_down = nrm((L, F, D), F ** -0.5)
    ple_norm = 1.0 + nrm((L, D), 0.1)
    ple_w_gate = nrm((L, D, D), D ** -0.5)
    ple_w_proj = nrm((L, PLE_DIM, D), PLE_DIM ** -0.5)
    final_norm = 1.0 + nrm((D,), 0.1)
    return {"x": x, "p": p,
            "ffn1_norm": ffn1_norm, "ffn1_w_gate": ffn1_w_gate, "ffn1_w_up": ffn1_w_up, "ffn1_w_down": ffn1_w_down,
            "mix_norm": mix_norm,
            "lru_w_in": lru_w_in, "lru_conv_w": lru_conv_w, "lru_conv_b": lru_conv_b,
            "lru_w_a": lru_w_a, "lru_b_a": lru_b_a, "lru_w_x": lru_w_x, "lru_b_x": lru_b_x,
            "lru_a_param": lru_a_param, "lru_w_out": lru_w_out,
            "pool_w": pool_w, "pool_b": pool_b, "pool_scale": pool_scale,
            "ffn2_norm": ffn2_norm, "ffn2_w_gate": ffn2_w_gate, "ffn2_w_up": ffn2_w_up, "ffn2_w_down": ffn2_w_down,
            "ple_norm": ple_norm, "ple_w_gate": ple_w_gate, "ple_w_proj": ple_w_proj,
            "final_norm": final_norm}

def second_block(x, p, ffn1_norm, ffn1_w_gate, ffn1_w_up, ffn1_w_down, mix_norm,
              lru_w_in, lru_conv_w, lru_conv_b, lru_w_a, lru_b_a, lru_w_x, lru_b_x, lru_a_param, lru_w_out,
              pool_w, pool_b, pool_scale,
              ffn2_norm, ffn2_w_gate, ffn2_w_up, ffn2_w_down,
              ple_norm, ple_w_gate, ple_w_proj, final_norm):
    h = x
    for i in range(DEPTH_2):
        h = h + 0.5 * swiglu(rms_norm_2(h, ffn1_norm[i]), ffn1_w_gate[i], ffn1_w_up[i], ffn1_w_down[i])
        hn = rms_norm_2(h, mix_norm[i])
        j = i // N_MIXERS
        if i % N_MIXERS == 0:
            m = rglru_mixer(hn, lru_w_in[j], lru_conv_w[j], lru_conv_b[j], lru_w_a[j], lru_b_a[j],
                            lru_w_x[j], lru_b_x[j], lru_a_param[j], lru_w_out[j])
        else:
            m = pool_mixer(hn, pool_w[j], pool_b[j], pool_scale[j])
        h = h + m
        h = h + 0.5 * swiglu(rms_norm_2(h, ffn2_norm[i]), ffn2_w_gate[i], ffn2_w_up[i], ffn2_w_down[i])
        gate = jax.nn.sigmoid(rms_norm_2(h, ple_norm[i]) @ ple_w_gate[i])
        h = h + gate * (p[i].astype(h.dtype) @ ple_w_proj[i])
    return rms_norm_2(h, final_norm)


def setup_inputs(seed=0):
    out = dict(first_inputs(seed))
    for name, value in second_inputs(seed + 1).items():
        if name != "x":
            out[name + "_2"] = value
    return out


def reference(
    x, c, positions, w_ada, b_ada, norm_mix, w_in, conv_w, conv_b, conv_ln_g, conv_ln_b,
    q_a_norm, w_q_b, kv_a_norm, w_kv_b, q_norm, k_norm, w_out, norm_ffn, w_group, b_group,
    w_expert, b_expert, w_gate_e, w_up_e, w_down_e, p_2, ffn1_norm_2, ffn1_w_gate_2,
    ffn1_w_up_2, ffn1_w_down_2, mix_norm_2, lru_w_in_2, lru_conv_w_2, lru_conv_b_2, lru_w_a_2,
    lru_b_a_2, lru_w_x_2, lru_b_x_2, lru_a_param_2, lru_w_out_2, pool_w_2, pool_b_2,
    pool_scale_2, ffn2_norm_2, ffn2_w_gate_2, ffn2_w_up_2, ffn2_w_down_2, ple_norm_2,
    ple_w_gate_2, ple_w_proj_2, final_norm_2,
):
    x = first_block(
        x, c, positions, w_ada, b_ada, norm_mix, w_in, conv_w, conv_b, conv_ln_g, conv_ln_b,
        q_a_norm, w_q_b, kv_a_norm, w_kv_b, q_norm, k_norm, w_out, norm_ffn, w_group, b_group,
        w_expert, b_expert, w_gate_e, w_up_e, w_down_e,
    )
    return second_block(
        x, p_2, ffn1_norm_2, ffn1_w_gate_2, ffn1_w_up_2, ffn1_w_down_2, mix_norm_2, lru_w_in_2,
        lru_conv_w_2, lru_conv_b_2, lru_w_a_2, lru_b_a_2, lru_w_x_2, lru_b_x_2, lru_a_param_2,
        lru_w_out_2, pool_w_2, pool_b_2, pool_scale_2, ffn2_norm_2, ffn2_w_gate_2, ffn2_w_up_2,
        ffn2_w_down_2, ple_norm_2, ple_w_gate_2, ple_w_proj_2, final_norm_2,
    )


_drawn_inputs = setup_inputs


def setup_inputs(seed=0):
    import zlib

    import numpy as np

    out = dict(_drawn_inputs(seed))
    spreads = {}
    factors = {'b_ada': 4.516,
     'norm_mix': 8.0,
     'conv_b': 8.0,
     'conv_ln_g': 8.0,
     'conv_ln_b': 8.0,
     'q_a_norm': 8.0,
     'kv_a_norm': 8.0,
     'q_norm': 8.0,
     'k_norm': 8.0,
     'norm_ffn': 7.681,
     'b_group': 8.0,
     'b_expert': 8.0,
     'lru_conv_b_2': 171.584,
     'lru_b_a_2': 200.0,
     'lru_b_x_2': 200.0,
     'pool_b_2': 61.557,
     'ple_norm_2': 175.296,
     'ffn1_norm_2': 8.0,
     'mix_norm_2': 5.638,
     'lru_w_a_2': 46.48,
     'lru_w_x_2': 25.64,
     'lru_a_param_2': 41.112,
     'pool_scale_2': 6.896,
     'ffn2_norm_2': 8.0,
     'lru_w_in_2': 8.0,
     'lru_conv_w_2': 8.0,
     'lru_w_out_2': 8.0,
     'ple_w_gate_2': 2.951}
    for name, (base, spread) in spreads.items():
        noise = np.random.default_rng([zlib.crc32(name.encode()), seed]).standard_normal(out[name].shape)
        drawn = base * np.exp(spread * noise) if base else spread * noise
        out[name] = __import__('jax').numpy.asarray(drawn.astype(out[name].dtype))
    for name, factor in factors.items():
        out[name] = (out[name] * factor).astype(out[name].dtype)
    return out
```

```python
from contextlib import ExitStack

import concourse.bass as bass
from concourse import mybir

F32 = mybir.dt.float32
F32R = mybir.dt.float32r
I32 = mybir.dt.int32
ALU = mybir.AluOpType
ACT = mybir.ActivationFunctionType
AX = mybir.AxisListType.X

P = 128
T = 256
TT = T // P
D = 1024
KD = D // P
SLOT = 2048
CW = SLOT // KD
RW = SLOT // D
N_RAW = 6
N_SPLIT = 3
AHEAD = N_SPLIT - 1
EPS = 1e-6
ARENA = 12832

CONV_CH, CONV_K = 512, 31
KC = CONV_CH // P
HEADS, NOPE, ROPE, VD = 8, 64, 32, 64
QK = NOPE + ROPE
GROUPS, PER_GROUP = 4, 8
EXPERTS = GROUPS * PER_GROUP
CHUNK = 64
D_FF = 2816
D_RNN = 1280
KR = D_RNN // P
LRU_HEADS, LRU_DIM = 16, 80
LRU_C = 8.0
WINDOWS = (2, 4, 8, 16)
PAD = 32
TW = PAD + T

C_IDENT = 0
C_ROT = C_IDENT + P
C_MASK = C_ROT + QK
C_FREQ = C_MASK + P
C_COUNT = C_FREQ + 1
C_DESC = C_COUNT + len(WINDOWS) * 16
C_SHIFT = C_DESC + EXPERTS
C_END = C_SHIFT + QK

VEC_A = [("b_ada", 48), ("norm_mix", 8), ("norm_ffn", 8), ("c", 8), ("conv_b", 4),
         ("conv_ln_g", 4), ("conv_ln_b", 4), ("q_a_norm", 2), ("kv_a_norm", 1)]
VEC_B = [("ffn1_norm_2", 16), ("mix_norm_2", 16), ("ffn2_norm_2", 16), ("ple_norm_2", 16),
         ("final_norm_2", 8), ("pool_b_2", 8), ("pool_scale_2", 8)]
VEC_C = [("conv_w", CONV_K * KC)]
VEC_D = [("lru_conv_w_2", 4 * KR), ("lru_conv_b_2", KR), ("lru_b_a_2", KR), ("lru_b_x_2", KR),
         ("lru_a_param_2", KR)]


class Lane:

    def __init__(self, engine, semaphore):
        self.engine, self.semaphore, self.count, self.seen = engine, semaphore, 0, {}

    def mark(self, instruction):
        instruction.then_inc(self.semaphore, 1)
        self.count += 1
        return self.semaphore, self.count

    @property
    def last(self):
        return self.semaphore, self.count

    def wait(self, *points):
        for semaphore, value in points:
            if value > self.seen.get(id(semaphore), 0):
                self.engine.wait_ge(semaphore, value)
                self.seen[id(semaphore)] = value


def build(nc, a, consts, out):
    ctx = ExitStack()
    with ctx:
        def sb(name, shape, dt=F32):
            return ctx.enter_context(nc.sbuf_tensor(name, shape, dt))

        def sem(name):
            return ctx.enter_context(nc.semaphore(name))

        pe, act = Lane(nc.tensor, sem("pe")), Lane(nc.scalar, sem("act"))
        dve, pool = Lane(nc.vector, sem("dve")), Lane(nc.gpsimd, sem("pool"))
        sp = Lane(nc.sync, sem("sp"))
        T_, V, S, G, L = nc.tensor, nc.vector, nc.scalar, nc.gpsimd, nc.sync

        bank = [ctx.enter_context(nc.psum_tensor(f"bank{b}", [P, 512], F32)) for b in range(8)]
        bank_free = [[] for _ in range(8)]

        def pair(b):
            return bank[b][:, :].rearrange("p (c t) -> p c t", c=2)

        raw = [sb(f"raw{i}", [P, SLOT]) for i in range(N_RAW)]
        w_hi = [sb(f"w_hi{i}", [P, SLOT], F32R) for i in range(N_SPLIT)]
        w_lo = [sb(f"w_lo{i}", [P, SLOT], F32R) for i in range(N_SPLIT)]
        xT = sb("xT", [P, KD, T])
        normed = sb("normed", [P, KR, T])
        a_hi = sb("a_hi", [P, KR, T], F32R)
        a_lo = sb("a_lo", [P, KR, T], F32R)
        hid = sb("hid", [P, 2, 2 * T])
        h_hi = sb("h_hi", [P, 2, 2 * T], F32R)
        h_lo = sb("h_lo", [P, 2, 2 * T], F32R)
        stat = sb("stat", [P, 5, T])
        cst = sb("cst", [P, C_END])
        ones = sb("ones", [P, P])
        eps = sb("eps", [P, 1])
        vec = sb("vec", [P, 4, P])
        mod = sb("mod", [P, 48])
        gmod = sb("gmod", [P, 2, KD])
        small = sb("small", [P, 96])
        arena = sb("arena", [P, ARENA])
        rows = arena[:, TT * D:TT * D + 4 * P].rearrange("p (n c) -> p n c", n=4)

        ident = cst[:, C_IDENT:C_IDENT + P]
        rstd, var, tmp_a, tmp_b, mean = (stat[:, i, :] for i in range(5))

        vec_at = {}
        for n, group in enumerate((VEC_A, VEC_B, VEC_C, VEC_D)):
            at = 0
            for name, count in group:
                vec_at[name] = (n, at, count)
                at += count

        def col(name, j):
            n, at, _ = vec_at[name]
            return vec[:, n, at + j:at + j + 1]

        s_small, s_x = sem("s_small"), sem("s_x")
        n_small = 0

        def load_small(dst, src, semaphore=None):
            nonlocal n_small
            S.dma_start(dst, src).then_inc(s_small, 16)
            n_small += 16
            return s_small, n_small

        L.dma_start(arena[:, 0:TT * D].rearrange("p (t d) -> p t d", t=TT),
                    a["x"].rearrange("(t p) d -> p t d", p=P)).then_inc(s_x, 16)
        load_small(cst[:, :], consts)
        for n, group in enumerate((VEC_A, VEC_B, VEC_C, VEC_D)):
            for name, count in group:
                _, at, _ = vec_at[name]
                src = a[name]
                if name in ("conv_w", "lru_conv_w_2"):
                    src = src.rearrange("k (c p) -> (k c) p", p=P)
                elif len(src.shape) == 2:
                    src = src.rearrange("l (c p) -> (l c) p", p=P)
                else:
                    src = src.rearrange("(c p) -> c p", p=P)
                load_small(rows[at:at + count, n, :], src)
        qk_gain = small[0:QK, 0:2]
        load_small(qk_gain[:, 0:1], a["q_norm"].rearrange("(d o) -> d o", o=1))
        load_small(qk_gain[:, 1:2], a["k_norm"].rearrange("(d o) -> d o", o=1))
        bias_row = small[0:1, 4:4 + GROUPS + EXPERTS]
        load_small(bias_row[:, 0:GROUPS], a["b_group"].rearrange("(o n) -> o n", o=1))
        load_small(bias_row[:, GROUPS:], a["b_expert"].rearrange("(o n) -> o n", o=1))
        pos_i = arena[0:1, TT * D + 4 * P:TT * D + 4 * P + T].bitcast(I32)
        load_small(pos_i, a["positions"])
        w_route = sb("w_route", [P, KD, GROUPS + EXPERTS])
        load_small(w_route[:, :, 0:GROUPS], a["w_group"].rearrange("(k p) n -> p k n", p=P))
        small_loaded = load_small(w_route[:, :, GROUPS:],
                                  a["w_expert"].rearrange("(k p) n -> p k n", p=P))

        entries = []

        def columns(name, c0, width=CW, split=True, index=None):
            w = a[name] if index is None else a[name][index]
            entries.append((w[:, c0:c0 + width].rearrange("(k p) n -> p k n", p=P),
                            w.shape[0] // P, width, split))

        def row_block(name, r0, split=True, index=None):
            w = a[name] if index is None else a[name][index]
            entries.append((w[r0:r0 + RW * P, :].rearrange("(k p) n -> p k n", p=P), RW, D, split))

        def units(names, n, per_expert, index=None):
            gate, up, down = names
            for u in range(n):
                i, c0 = (u, 0) if per_expert else (index, u * CW)
                columns(gate, c0, index=i)
                columns(up, c0, index=i)
                if u:
                    j, r0 = (u - 1, 0) if per_expert else (index, (u - 1) * CW)
                    row_block(down, r0, index=j)
            j, r0 = (n - 1, 0) if per_expert else (index, (n - 1) * CW)
            row_block(down, r0, index=j)

        def ple_entries(i):
            row_block("ple_w_proj_2", 0, index=i)
            for c0 in range(0, D, CW):
                columns("ple_w_gate_2", c0, index=i)

        for c0 in range(0, 2 * D, CW):
            columns("w_ada", c0, split=False)
        columns("w_in", 1024)
        columns("w_in", 1280, width=160)
        entries.append((a["w_q_b"].rearrange("(k p) n -> p k n", p=P), 2, HEADS * QK, False))
        entries.append((a["w_kv_b"].rearrange("(k p) n -> p k n", p=P), 1, HEADS * 128, False))
        for c0 in range(0, 1024, CW):
            columns("w_in", c0)
        for c0 in range(2 * D, 6 * D, CW):
            columns("w_ada", c0, split=False)
        for c0 in range(0, D, CW):
            columns("w_out", c0)
        units(("w_gate_e", "w_up_e", "w_down_e"), EXPERTS, True)
        for i in range(2):
            units(("ffn1_w_gate_2", "ffn1_w_up_2", "ffn1_w_down_2"), D_FF // CW, False, i)
            if i == 0:
                for c0 in range(0, 2 * D_RNN, CW):
                    columns("lru_w_in_2", c0)
                for r0 in range(0, D_RNN, RW * P):
                    row_block("lru_w_out_2", r0)
            else:
                entries.append((a["pool_w_2"].rearrange("g (k p) n -> p (g k) n", p=P), 8, CW,
                                True))
            units(("ffn2_w_gate_2", "ffn2_w_up_2", "ffn2_w_down_2"), D_FF // CW, False, i)
            ple_entries(i)

        s_raw = [sem(f"s_raw{i}") for i in range(N_RAW)]
        n_loaded = n_split = n_taken = 0
        raw_free = [[] for _ in range(N_RAW)]
        split_free = [None] * N_SPLIT
        where = {}
        ready = {}
        n_splits = 0

        released = [False] * len(entries)

        def load_more():
            nonlocal n_loaded
            while n_loaded < len(entries) and (n_loaded < N_RAW or released[n_loaded - N_RAW]):
                src, k, width, _ = entries[n_loaded]
                slot = n_loaded % N_RAW
                sp.wait(*raw_free[slot])
                L.dma_start(raw[slot][:, 0:k * width].rearrange("p (k n) -> p k n", k=k),
                            src).then_inc(s_raw[slot], 16)
                n_loaded += 1

        def release(i, points):
            raw_free[i % N_RAW] = points
            released[i] = True
            load_more()

        def loaded(i):
            return s_raw[i % N_RAW], 16 * (i // N_RAW + 1)

        def split_next():
            nonlocal n_split, n_splits
            i = n_split
            n_split += 1
            _, k, width, split = entries[i]
            load_more()
            assert n_loaded > i
            if not split:
                ready[i] = [loaded(i)]
                return
            s, n, size = i % N_RAW, n_splits % N_SPLIT, k * width
            n_splits += 1
            where[i] = n
            act.wait(loaded(i))
            if split_free[n]:
                act.wait(split_free[n])
                dve.wait(split_free[n])
            hi = act.mark(S.activation(w_hi[n][:, 0:size], raw[s][:, 0:size], ACT.Copy))
            dve.wait(loaded(i), hi)
            lo = dve.mark(V.tensor_tensor(w_lo[n][:, 0:size], raw[s][:, 0:size],
                                          w_hi[n][:, 0:size].bitcast(F32), ALU.subtract))
            ready[i] = [hi, lo]
            release(i, [hi, lo])

        def take():
            nonlocal n_taken
            i = n_taken
            n_taken += 1
            while n_split <= i:
                split_next()
            pe.wait(*ready[i])
            return i

        def look_ahead(i):
            while n_split < n_loaded and n_split <= i + AHEAD:
                split_next()

        def give_back(i, point):
            if entries[i][3]:
                split_free[where[i]] = point
            else:
                release(i, [point])
            look_ahead(i)

        def weights(i):
            _, k, width, split = entries[i]
            if not split:
                return raw[i % N_RAW][:, 0:k * width].rearrange("p (k n) -> p k n", k=k)
            n = where[i]
            return tuple(w[n][:, 0:k * width].rearrange("p (k n) -> p k n", k=k)
                         for w in (w_hi, w_lo))

        def product3(dst, w, x, first, last, check=True):
            (wh, wl), (xh, xl) = w, x
            T_.matmul(dst, wh, xh, start=first, stop=False, skip_group_check=not check)
            T_.matmul(dst, wh, xl, start=False, stop=False, skip_group_check=not check)
            return T_.matmul(dst, wl, xh, start=False, stop=last, skip_group_check=not check)

        def column_product(b, x_ready, chunks=KD, width=CW, x0=0):
            i = take()
            wh, wl = weights(i)
            pe.wait(*bank_free[b])
            m0 = 0
            while m0 < width:
                m = min(P, width - m0)
                for k in range(chunks):
                    if x_ready and m0 == 0:
                        pe.wait(x_ready[k])
                    last = product3(pair(b)[0:m, m0 // P, :],
                                    (wh[:, k, m0:m0 + m], wl[:, k, m0:m0 + m]),
                                    (a_hi[:, x0 + k, :], a_lo[:, x0 + k, :]),
                                    k == 0, k == chunks - 1)
                m0 += m
            point = pe.mark(last)
            give_back(i, point)
            return point

        def row_product(x_hi, x_lo, first, last, x_ready):
            i = take()
            wh, wl = weights(i)
            pe.wait(*x_ready)
            if first:
                for b in range(4, 8):
                    pe.wait(*bank_free[b])
            for m in range(KD):
                for k in range(RW):
                    ins = product3(pair(4 + m // 2)[:, m % 2, :],
                                   (wh[:, k, m * P:(m + 1) * P], wl[:, k, m * P:(m + 1) * P]),
                                   (x_hi[k], x_lo[k]),
                                   first and k == 0 and m % 2 == 0, last and k == RW - 1, False)
            point = pe.mark(ins)
            give_back(i, point)
            return point

        operand_free = [None]

        def split_operand(k, src, src_ready):
            act.wait(*src_ready)
            if operand_free[0]:
                act.wait(operand_free[0])
                dve.wait(operand_free[0])
            hi = act.mark(S.activation(a_hi[:, k, :], src, ACT.Copy))
            dve.wait(hi, *src_ready)
            return dve.mark(V.tensor_tensor(a_lo[:, k, :], src, a_hi[:, k, :].bitcast(F32),
                                            ALU.subtract))

        def inverse_root(total, n, p=P, width=T, dst=None):
            r, v = (rstd, var) if dst is None else dst
            r, v, ta, tb = (x[0:p, 0:width] for x in (r, v, tmp_a, tmp_b))
            dve.mark(V.tensor_scalar(v, total, 1.0 / n, EPS, ALU.mult, ALU.add))
            act.wait(dve.last)
            act.mark(S.activation(ta, v, ACT.Sqrt))
            dve.wait(act.last)
            dve.mark(V.reciprocal(tb, ta))
            dve.wait(dve.last)
            dve.mark(V.tensor_tensor(r, tb, tb, ALU.mult))
            dve.wait(dve.last)
            dve.mark(V.tensor_tensor(r, r, v, ALU.mult))
            dve.wait(dve.last)
            dve.mark(V.tensor_scalar(r, r, -0.5, 1.5, ALU.mult, ALU.add))
            dve.wait(dve.last)
            return dve.mark(V.tensor_tensor(r, r, tb, ALU.mult))

        def rms_statistics(src, n_chunks, b, x_ready, squares=None):
            sq = normed if squares is None else squares
            act.wait(dve.last, pe.last)
            for k in range(n_chunks):
                act.wait(x_ready[k])
                done = act.mark(S.activation(sq[:, k, :], src[:, k, :], ACT.Square))
                if k == 0:
                    pe.wait(*bank_free[b])
                pe.wait(done, consts_ready)
                last = T_.matmul(pair(b)[:, 0, :], ones[:, :], sq[:, k, :], start=k == 0,
                                 stop=k == n_chunks - 1)
            dve.wait(pe.mark(last))
            point = inverse_root(pair(b)[:, 0, :], n_chunks * P)
            bank_free[b] = [point]
            return point

        def rms_norm(gain, x_ready, shift=None):
            rms_statistics(xT, KD, 0, x_ready)
            points = []
            for k in range(KD):
                dve.wait(dve.last)
                done = dve.mark(V.scalar_tensor_tensor(normed[:, k, :], xT[:, k, :], gain(k),
                                                       rstd, ALU.mult, ALU.mult))
                if shift is not None:
                    dve.wait(done)
                    done = dve.mark(V.tensor_scalar(normed[:, k, :], normed[:, k, :], shift(k),
                                                    None, ALU.add))
                points.append(split_operand(k, normed[:, k, :], [done]))
            return points

        def gated_units(n, x_ready, expert_gates=None):
            hidden = [None] * n
            down_done = [None] * n

            def down(u):
                s = u % 2
                hi, lo = (h[:, s, :].rearrange("p (c t) -> p c t", c=2) for h in (h_hi, h_lo))
                down_done[u] = row_product([hi[:, 0, :], hi[:, 1, :]], [lo[:, 0, :], lo[:, 1, :]],
                                           u == 0, u == n - 1, [hidden[u]])

            for u in range(n):
                s = u % 2
                gate_b, up_b = 2 * s, 2 * s + 1
                gate_done = column_product(gate_b, x_ready if u == 0 else None)
                up_done = column_product(up_b, None)
                act.wait(gate_done)
                if u >= 1:
                    act.wait(hidden[u - 1])
                act.mark(S.activation(hid[:, s, :], bank[gate_b][:, :], ACT.Silu))
                dve.wait(act.last, up_done)
                dve.mark(V.tensor_tensor(hid[:, s, :], hid[:, s, :], bank[up_b][:, :], ALU.mult))
                bank_free[gate_b], bank_free[up_b] = [act.last], [dve.last]
                if expert_gates is not None:
                    for c in range(2):
                        dve.wait(dve.last)
                        dve.mark(V.tensor_tensor(hid[:, s, c * T:(c + 1) * T],
                                                 hid[:, s, c * T:(c + 1) * T],
                                                 expert_gates[:, u, :], ALU.mult))
                act.wait(dve.last)
                if u >= 2:
                    act.wait(down_done[u - 2])
                    dve.wait(down_done[u - 2])
                act.mark(S.activation(h_hi[:, s, :], hid[:, s, :], ACT.Copy))
                dve.wait(act.last)
                hidden[u] = dve.mark(V.tensor_tensor(h_lo[:, s, :], hid[:, s, :],
                                                     h_hi[:, s, :].bitcast(F32), ALU.subtract))
                if u:
                    down(u - 1)
            down(n - 1)
            operand_free[0] = pe.last
            return down_done[n - 1]

        def add_banks(factor, done):
            dve.wait(done)
            points = []
            for m in range(KD):
                f = factor(m) if callable(factor) else factor
                points.append(dve.mark(V.scalar_tensor_tensor(
                    xT[:, m, :], pair(4 + m // 2)[:, m % 2, :], f, xT[:, m, :],
                    ALU.mult, ALU.add)))
            for b in range(4, 8):
                bank_free[b] = [dve.last]
            return points

        pool.mark(G.memset(ones[:, :], 1.0))
        pool.mark(G.memset(eps[:, :], EPS))
        consts_ready = pool.last
        pe.wait(small_loaded)
        for n, group in enumerate((VEC_A, VEC_B, VEC_C, VEC_D)):
            r = sum(count for _, count in group)
            last = T_.transpose(bank[0][:, n * P:n * P + r], rows[0:r, n, :], ident[0:r, 0:r])
        dve.wait(pe.mark(last))
        for n, group in enumerate((VEC_A, VEC_B, VEC_C, VEC_D)):
            r = sum(count for _, count in group)
            vectors = dve.mark(V.tensor_copy(vec[:, n, 0:r], bank[0][:, n * P:n * P + r]))
        bank_free[0] = [vectors]
        pos_row = stat[0:1, 4, :]
        dve.wait(small_loaded)
        pos_ready = dve.mark(V.tensor_copy(pos_row, pos_i))

        x_tok = arena[:, 0:TT * D].rearrange("p (t d) -> p t d", t=TT)
        pe.wait((s_x, 16))
        x_points = []
        for k in range(KD):
            b = 1 + k // 2
            for t in range(TT):
                last = T_.transpose(pair(b)[:, k % 2, t * P:(t + 1) * P],
                                    x_tok[:, t, k * P:(k + 1) * P], ident)
            if k % 2:
                dve.wait(pe.mark(last))
                x_points += 2 * [dve.mark(V.tensor_copy(xT[:, k - 1:k + 1, :], pair(b)))]
                bank_free[b] = [dve.last]

        c_act = small[:, 40:40 + KD]
        n, at, _ = vec_at["c"]
        act.wait(vectors)
        c_ready = act.mark(S.activation(c_act, vec[:, n, at:at + KD], ACT.Silu))

        def modulation(first, count):
            pe.wait(c_ready, *bank_free[7])
            for j in range(first, first + count):
                i = take()
                w = weights(i)
                for m in range(2):
                    for k in range(KD):
                        last = T_.matmul(bank[7][:, 2 * j + m:2 * j + m + 1],
                                         w[:, k, m * P:(m + 1) * P], c_act[:, k:k + 1],
                                         start=k == 0, stop=k == KD - 1)
                give_back(i, pe.mark(last))
            dve.wait(pe.last, vectors)
            nb, ab, _ = vec_at["b_ada"]
            lo, hi = 2 * first, 2 * (first + count)
            dve.mark(V.tensor_tensor(mod[:, lo:hi], bank[7][:, lo:hi], vec[:, nb, ab + lo:ab + hi],
                                     ALU.add))
            bank_free[7] = [dve.last]
            return dve.last

        def scaled_gain(row, name, at_scale):
            nn, an, _ = vec_at[name]
            dve.wait(dve.last)
            dve.mark(V.scalar_tensor_tensor(gmod[:, row, :], mod[:, at_scale:at_scale + KD], 1.0,
                                            vec[:, nn, an:an + KD], ALU.add, ALU.mult))
            dve.wait(dve.last)

        modulation(0, 8)
        scaled_gain(0, "norm_mix", KD)
        h_points = rms_norm(lambda k: gmod[:, 0, k:k + 1], x_points, lambda k: mod[:, k:k + 1])

        at = [0]

        def scratch(size, shape=None):
            x = arena[:, at[0]:at[0] + size]
            at[0] += size
            assert at[0] <= ARENA
            return x

        u_pad = scratch(KC * TW).rearrange("p (c t) -> p c t", c=KC)
        qk = scratch(2 * HEADS * T).rearrange("p (s h t) -> p s h t", s=2, h=HEADS)
        v_tok = scratch(TT * HEADS * VD).rearrange("p (t n) -> p t n", t=TT)
        cosT, sinT = normed[:, KD, :], normed[:, KD + 1, :]
        wide = scratch(HEADS * T + HEADS * P)
        p_t = scratch(3 * HEADS * P)
        cq = p_t[:, 0:2 * T].rearrange("p (c t) -> p c t", c=2)
        ckv = p_t[:, 2 * T:3 * T].rearrange("p (c t) -> p c t", c=1)
        conv = hid[:, :, :].rearrange("p s (c t) -> p (s c) t", c=2)
        dve.wait(pe.last)

        cq_done = column_product(1, h_points)
        kv_done = column_product(2, None, width=160)
        act.wait(cq_done)
        act.mark(S.activation(cq[:, :, :], pair(1)[:, :, :], ACT.Copy))
        bank_free[1] = [act.last]
        act.wait(kv_done)
        act.mark(S.activation(ckv[:, 0, :], pair(2)[:, 0, :], ACT.Copy))
        k_rope = p_t[0:ROPE, 3 * T:4 * T]
        kv_ready = act.mark(S.activation(k_rope, pair(2)[0:ROPE, 1, :], ACT.Copy))
        bank_free[2] = [act.last]

        def small_norm(src, n_chunks, gains, ready_point):
            rms_statistics(src, n_chunks, 0, [ready_point] * n_chunks, squares=normed)
            dve.wait(dve.last)
            for k in range(n_chunks):
                done = dve.mark(V.scalar_tensor_tensor(src[:, k, :], src[:, k, :], gains(k), rstd,
                                                       ALU.mult, ALU.mult))
            return done

        cq_ready = small_norm(cq, 2, lambda k: col("q_a_norm", k), kv_ready)
        ckv_ready = small_norm(ckv, 1, lambda k: col("kv_a_norm", k), kv_ready)

        pe.wait(pos_ready, *bank_free[3])
        last = T_.matmul(pair(3)[0:QK, 0, :], ones[0:1, 0:QK], pos_row, start=True, stop=True)
        dve.wait(pe.mark(last))
        ang = cosT[0:QK, :]
        turn = tmp_a[0:QK, :]
        dve.mark(V.tensor_scalar(ang, pair(3)[0:QK, 0, :], cst[0:QK, C_FREQ:C_FREQ + 1], None,
                                 ALU.mult))
        bank_free[3] = [dve.last]
        MAGIC = 12582912.0
        PARTS = two_pi_parts()
        for scalar, op in ((1.0 / 6.283185307179586, ALU.mult), (MAGIC, ALU.add),
                           (-MAGIC, ALU.add)):
            dve.wait(dve.last)
            dve.mark(V.tensor_scalar(turn, ang if op == ALU.mult else turn, scalar, None, op))
        for part in PARTS:
            dve.wait(dve.last)
            dve.mark(V.scalar_tensor_tensor(ang, turn, -part, ang, ALU.mult, ALU.add))
        PI = 3.1415925
        dve.wait(dve.last)
        dve.mark(V.tensor_scalar(ang, ang, PI, -PI, ALU.min, ALU.max))
        act.wait(dve.last)
        act.mark(S.activation(sinT[0:QK, :], ang, ACT.Sin))
        dve.wait(dve.last)
        dve.mark(V.tensor_scalar(turn, ang, -1.0, None, ALU.mult))
        dve.wait(dve.last)
        dve.mark(V.tensor_tensor(turn, turn, ang, ALU.max))
        dve.wait(dve.last)
        dve.mark(V.tensor_scalar(turn, turn, -1.0, 1.5707963267948966, ALU.mult, ALU.add))
        act.wait(dve.last, act.last)
        rope_ready = act.mark(S.activation(cosT[0:QK, :], turn, ACT.Sin))

        i = take()
        w = weights(i)
        pe.wait(cq_ready)
        qT, kT = qk[:, 0, :, :], qk[:, 1, :, :]
        for h in range(HEADS):
            b = 3 + h // 2
            if h % 2 == 0:
                pe.wait(*bank_free[b])
            for k in range(2):
                last = T_.matmul(pair(b)[0:QK, h % 2, :], w[:, k, h * QK:(h + 1) * QK],
                                 cq[:, k, :], start=k == 0, stop=k == 1)
            if h % 2:
                act.wait(pe.mark(last))
                act.mark(S.activation(qT[0:QK, h - 1:h + 1, :], pair(b)[0:QK, :, :], ACT.Copy))
                bank_free[b] = [act.last]
        give_back(i, pe.last)
        q_raw = act.last
        i = take()
        w = weights(i)
        pe.wait(ckv_ready, kv_ready)
        last = T_.matmul(pair(7)[0:QK, 1, :], cst[0:ROPE, C_SHIFT:C_SHIFT + QK],
                         k_rope, start=True, stop=True)
        rope_rows = pe.mark(last)
        act.wait(rope_rows)
        for h in range(HEADS):
            act.mark(S.activation(kT[NOPE:QK, h, :], pair(7)[NOPE:QK, 1, :], ACT.Copy))
        bank_free[7] = [act.last]
        for h in range(HEADS):
            b = (1, 2, 3, 4)[h // 2]
            if h % 2 == 0:
                pe.wait(*bank_free[b])
            last = T_.matmul(pair(b)[0:NOPE, h % 2, :], w[:, 0, h * 128:h * 128 + NOPE],
                             ckv[:, 0, :], start=True, stop=True)
            if h % 2:
                act.wait(pe.mark(last))
                act.mark(S.activation(kT[0:NOPE, h - 1:h + 1, :], pair(b)[0:NOPE, :, :],
                                      ACT.Copy))
                bank_free[b] = [act.last]
        k_raw = act.last
        wv = w[:, 0, :].rearrange("p (h s) -> p h s", s=128)[:, :, NOPE:128]
        for t in range(TT):
            pe.wait(*bank_free[5 + t])
            last = T_.matmul(bank[5 + t][:, :], ckv[:, 0, t * P:(t + 1) * P], wv, start=True,
                             stop=True)
            act.wait(pe.mark(last))
            v_ready = act.mark(S.activation(v_tok[:, t, :], bank[5 + t][:, :], ACT.Copy))
            bank_free[5 + t] = [act.last]
        give_back(i, pe.last)

        def heads_ready(side, raw_ready):
            x = qk[0:QK, side, :, :]
            sq = normed[0:QK, 0:HEADS, :]
            act.wait(raw_ready, dve.last, pe.last)
            act.mark(S.activation(sq, x, ACT.Square))
            pe.wait(act.last)
            for j in range(4):
                b = 1 + j
                pe.wait(*bank_free[b])
                last = T_.matmul(pair(b)[0:QK, :, :], ones[0:QK, 0:QK], sq[:, 2 * j:2 * j + 2, :],
                                 start=True, stop=True)
                dve.wait(pe.mark(last))
                inverse_root(pair(b)[0:QK, 0, :], QK, QK)
                for c in range(2):
                    if c:
                        dve.wait(dve.last)
                        inverse_root(pair(b)[0:QK, 1, :], QK, QK)
                    dve.wait(dve.last)
                    dve.mark(V.scalar_tensor_tensor(x[:, 2 * j + c, :], x[:, 2 * j + c, :],
                                                    qk_gain[:, side:side + 1], rstd[0:QK, :],
                                                    ALU.mult, ALU.mult))
                bank_free[b] = [dve.last]
            pe.wait(dve.last)
            for j in range(4):
                b = 1 + j
                pe.wait(*bank_free[b])
                last = T_.matmul(pair(b)[0:QK, :, :], cst[0:QK, C_ROT:C_ROT + QK],
                                 x[:, 2 * j:2 * j + 2, :], start=True, stop=True)
                pe.mark(last)
            for j in range(4):
                b = 1 + j
                dve.wait(pe.last, rope_ready)
                for c in range(2):
                    h = 2 * j + c
                    dve.mark(V.tensor_tensor(sq[:, h, :], pair(b)[0:QK, c, :], sinT[0:QK, :],
                                             ALU.mult))
                    dve.mark(V.tensor_tensor(x[:, h, :], x[:, h, :], cosT[0:QK, :], ALU.mult))
                    dve.wait(dve.last)
                    dve.mark(V.tensor_tensor(x[:, h, :], x[:, h, :], sq[:, h, :], ALU.add))
                bank_free[b] = [dve.last]
            return dve.last

        q_ready = heads_ready(0, q_raw)
        k_ready = heads_ready(1, k_raw)

        pool.wait(dve.last, pe.last)
        pad_ready = pool.mark(G.memset(u_pad[:, :, 0:PAD], 0.0))
        conv_banks = []
        for b in (5, 6, 7, 0):
            conv_banks.append(column_product(b, None))
        operand_free[0] = pe.last
        for j in range(2):
            act.wait(conv_banks[2 + j])
            act.mark(S.activation(conv[:, 2 * j:2 * j + 2, :], pair((7, 0)[j]), ACT.Sigmoid))
            bank_free[(7, 0)[j]] = [act.last]
            dve.wait(act.last)
            dve.mark(V.tensor_tensor(u_pad[:, 2 * j:2 * j + 2, PAD:], pair(5 + j),
                                     conv[:, 2 * j:2 * j + 2, :], ALU.mult))
            bank_free[5 + j] = [dve.last]

        s1 = wide[:, 0:HEADS * T].rearrange("p (h t) -> p h t", h=HEADS)
        s0 = wide[:, HEADS * T:].rearrange("p (h t) -> p h t", h=HEADS)
        mask = cst[:, C_MASK:C_MASK + P]
        top, negative, total = small[:, 48:56], small[:, 56:64], small[:, 64:72]
        scale = float(QK) ** -0.5
        pe.wait(q_ready, k_ready)
        for t, s in ((0, s0), (1, s1)):
            keys = (t + 1) * P
            for h in range(HEADS):
                b, c = 1 + h // 2, h % 2
                if c == 0:
                    pe.wait(*bank_free[b])
                last = T_.matmul(pair(b)[:, c, 0:keys], qT[0:QK, h, t * P:(t + 1) * P],
                                 kT[0:QK, h, 0:keys], start=True, stop=True)
                if c == 0:
                    continue
                dve.wait(pe.mark(last))
                for hh in (h - 1, h):
                    dve.mark(V.tensor_tensor(s[:, hh, keys - P:keys],
                                             pair(b)[:, hh % 2, keys - P:keys], mask, ALU.add))
                if t:
                    dve.mark(V.tensor_copy(s[:, h - 1:h + 1, 0:P], pair(b)[:, :, 0:P]))
                bank_free[b] = [dve.last]
            dve.wait(dve.last, act.last)
            dve.mark(V.tensor_reduce(top, s, AX, ALU.max))
            dve.wait(dve.last)
            dve.mark(V.tensor_scalar(negative, top, -scale, None, ALU.mult))
            act.wait(dve.last)
            for h in range(HEADS):
                act.mark(S.activation(s[:, h, :], s[:, h, :], ACT.Exp, bias=negative[:, h:h + 1],
                                      scale=scale, accum_out=total[:, h:h + 1]))
            dve.wait(act.last)
            dve.mark(V.reciprocal(total, total))
            dve.wait(dve.last)
            for h in range(HEADS):
                dve.mark(V.tensor_scalar(s[:, h, :], s[:, h, :], total[:, h:h + 1], None,
                                         ALU.mult))
            pe.wait(dve.last)
            for kt in range(t + 1):
                block = 0 if t == 0 else 1 + kt
                for half in range(2):
                    b = 1 + (2 * kt + half) % 4
                    pe.wait(*bank_free[b])
                    for h in range(4 * half, 4 * half + 4):
                        last = T_.transpose(bank[b][:, (h % 4) * P:(h % 4 + 1) * P],
                                            s[:, h, kt * P:(kt + 1) * P], ident)
                    act.wait(pe.mark(last), k_ready)
                    at0 = (block * HEADS + 4 * half) * P
                    act.mark(S.activation(p_t[:, at0:at0 + 4 * P], bank[b][:, :], ACT.Copy))
                    bank_free[b] = [act.last]
        pt = p_t.rearrange("p (b h t) -> p b h t", b=3, h=HEADS)

        pe.wait(act.last, v_ready)
        y_points = [None] * KD
        for pair_h in range(HEADS // 2):
            b = 1 + pair_h
            pe.wait(*bank_free[b])
            for c in range(2):
                h = 2 * pair_h + c
                dst = pair(b)[c * VD:(c + 1) * VD, 0, :]
                v0, v1 = (v_tok[:, t, h * VD:(h + 1) * VD] for t in range(TT))
                T_.matmul(dst[:, 0:P], v0, pt[:, 0, h, :], start=True, stop=True,
                          skip_group_check=True)
                T_.matmul(dst[:, P:T], v0, pt[:, 1, h, :], start=False, stop=False,
                          skip_group_check=True)
                last = T_.matmul(dst[:, P:T], v1, pt[:, 2, h, :], start=False, stop=True,
                                 skip_group_check=True)
            dve.wait(pe.mark(last))
            done = dve.mark(V.tensor_copy(normed[:, KC + pair_h, :], pair(b)[:, 0, :]))
            bank_free[b] = [done]
            y_points[KC + pair_h] = split_operand(KC + pair_h, normed[:, KC + pair_h, :], [done])

        dve.wait(pad_ready)
        for k in range(CONV_K):
            for c in range(KC):
                tap = u_pad[:, c, PAD - (CONV_K - 1) + k:PAD - (CONV_K - 1) + k + T]
                if k:
                    dve.wait((dve.semaphore, dve.count - KC + 1))
                    dve.mark(V.scalar_tensor_tensor(conv[:, c, :], tap, col("conv_w", k * KC + c),
                                                    conv[:, c, :], ALU.mult, ALU.add))
                else:
                    dve.wait(dve.last)
                    dve.mark(V.tensor_scalar(conv[:, c, :], tap, col("conv_w", c),
                                             col("conv_b", c), ALU.mult, ALU.add))
        pe.wait(dve.last, *bank_free[5])
        for c in range(KC):
            last = T_.matmul(pair(5)[:, 0, :], ones[:, :], conv[:, c, :], start=c == 0,
                             stop=c == KC - 1)
        dve.wait(pe.mark(last), dve.last)
        dve.mark(V.tensor_scalar(mean, pair(5)[:, 0, :], 1.0 / CONV_CH, None, ALU.mult))
        bank_free[5] = [dve.last]
        for c in range(KC):
            dve.wait(dve.last)
            dve.mark(V.tensor_tensor(conv[:, c, :], conv[:, c, :], mean, ALU.subtract))
        rms_statistics(conv, KC, 6, [dve.last] * KC)
        for c in range(KC):
            dve.wait(dve.last)
            dve.mark(V.scalar_tensor_tensor(conv[:, c, :], conv[:, c, :], col("conv_ln_g", c),
                                            rstd, ALU.mult, ALU.mult))
            dve.wait(dve.last)
            dve.mark(V.tensor_scalar(conv[:, c, :], conv[:, c, :], col("conv_ln_b", c), None,
                                     ALU.add))
            act.wait(dve.last)
            done = act.mark(S.activation(conv[:, c, :], conv[:, c, :], ACT.Silu))
            y_points[c] = split_operand(c, conv[:, c, :], [done])

        modulation(8, 16)
        dve.wait(dve.last)
        x_points = []
        for j in range(4):
            done = column_product(1 + j, y_points if j == 0 else None)
            dve.wait(done)
            for c in range(2):
                m = 2 * j + c
                x_points.append(dve.mark(V.scalar_tensor_tensor(
                    xT[:, m, :], pair(1 + j)[:, c, :], mod[:, 2 * KD + m:2 * KD + m + 1],
                    xT[:, m, :], ALU.mult, ALU.add)))
            bank_free[1 + j] = [dve.last]
        operand_free[0] = pe.last

        scaled_gain(1, "norm_ffn", 4 * KD)
        h_points = rms_norm(lambda k: gmod[:, 1, k:k + 1], x_points,
                            lambda k: mod[:, 3 * KD + k:3 * KD + k + 1])
        at[0] = 0
        gate_all = scratch(EXPERTS * T).rearrange("p (e t) -> p e t", e=EXPERTS)
        gates_t = scratch(T)
        r_at = at[0]
        NR = GROUPS + EXPERTS
        pe.wait(dve.last, *bank_free[1])
        for t in range(TT):
            dst = bank[1][:, t * 64:t * 64 + NR]
            for k in range(KD):
                T_.matmul(dst, normed[:, k, t * P:(t + 1) * P], w_route[:, k, :], start=k == 0,
                          stop=False)
            last = T_.matmul(dst, ones[0:1, 0:P], bias_row, start=False, stop=True)
        dve.wait(pe.mark(last))
        desc = cst[:, C_DESC:C_DESC + EXPERTS]

        def one_hot_of_top(dst, values, n, scr, best):
            dve.wait(dve.last)
            dve.mark(V.tensor_reduce(best, values, AX, ALU.max))
            dve.wait(dve.last)
            dve.mark(V.tensor_scalar(scr, values, best, None, ALU.is_equal))
            dve.wait(dve.last)
            dve.mark(V.tensor_tensor(scr, scr, desc[:, EXPERTS - n:], ALU.mult))
            dve.wait(dve.last)
            dve.mark(V.tensor_reduce(dst[:, 0:1], scr, AX, ALU.max))
            dve.wait(dve.last)
            dve.mark(V.tensor_scalar(scr, desc[:, EXPERTS - n:], dst[:, 0:1], None,
                                     ALU.is_equal))
            dve.wait(dve.last)
            dve.mark(V.tensor_copy(dst, scr))
            dve.wait(dve.last)

        for t in range(TT):
            lg, le, hot_g, hot1, hot2, scr, pr = (
                scratch(n) for n in (GROUPS, EXPERTS, GROUPS, EXPERTS, EXPERTS, EXPERTS, EXPERTS))
            best, neg, s_g, p2, den = (scratch(1) for _ in range(5))
            dve.wait(act.last, pe.last)
            dve.mark(V.tensor_copy(lg, bank[1][:, t * 64:t * 64 + GROUPS]))
            dve.mark(V.tensor_copy(le, bank[1][:, t * 64 + GROUPS:t * 64 + NR]))
            one_hot_of_top(hot_g, lg, GROUPS, scr[:, 0:GROUPS], best)
            dve.mark(V.tensor_scalar(neg, best, -1.0, None, ALU.mult))
            act.wait(dve.last)
            act.mark(S.activation(scr[:, 0:GROUPS], lg, ACT.Exp, bias=neg, accum_out=s_g))
            dve.wait(act.last)
            dve.mark(V.tensor_scalar(hot_g, hot_g, -1.0, 1e30, ALU.add, ALU.mult))
            dve.wait(dve.last)
            for g in range(GROUPS):
                dve.mark(V.tensor_scalar(le[:, g * PER_GROUP:(g + 1) * PER_GROUP],
                                         le[:, g * PER_GROUP:(g + 1) * PER_GROUP],
                                         hot_g[:, g:g + 1], None, ALU.add))
            dve.wait(dve.last)
            dve.mark(V.tensor_reduce(best, le, AX, ALU.max))
            dve.wait(dve.last)
            dve.mark(V.tensor_scalar(neg, best, -1.0, None, ALU.mult))
            act.wait(dve.last)
            act.mark(S.activation(pr, le, ACT.Exp, bias=neg))
            dve.wait(act.last)
            one_hot_of_top(hot1, pr, EXPERTS, scr, best)
            dve.mark(V.scalar_tensor_tensor(pr, hot1, -2.0, pr, ALU.mult, ALU.add))
            one_hot_of_top(hot2, pr, EXPERTS, scr, p2)
            dve.mark(V.tensor_tensor(den, best, p2, ALU.add))
            dve.mark(V.tensor_scalar(hot1, hot1, best, None, ALU.mult))
            dve.wait(dve.last)
            dve.mark(V.tensor_tensor(den, den, s_g, ALU.mult))
            dve.mark(V.scalar_tensor_tensor(hot1, hot2, p2, hot1, ALU.mult, ALU.add))
            dve.wait(dve.last)
            dve.mark(V.reciprocal(den, den))
            dve.wait(dve.last)
            dve.mark(V.tensor_scalar(hot1, hot1, den, None, ALU.mult))
            pe.wait(dve.last, *bank_free[2])
            last = T_.transpose(bank[2][0:EXPERTS, t * P:(t + 1) * P], hot1, ident)
            pe.mark(last)
        bank_free[1] = [dve.last]
        dve.wait(pe.last)
        dve.mark(V.tensor_copy(gates_t[0:EXPERTS, :], bank[2][0:EXPERTS, 0:T]))
        bank_free[2] = [dve.last]
        pe.wait(dve.last)
        for j in range(EXPERTS // 2):
            b = 4 + j % 4
            pe.wait(*bank_free[b])
            for c in range(2):
                e = 2 * j + c
                last = T_.matmul(pair(b)[:, c, :],
                                 cst[0:EXPERTS, C_IDENT + e:C_IDENT + e + 1].to_broadcast(
                                     [EXPERTS, P]),
                                 gates_t[0:EXPERTS, :], start=True, stop=True)
            pe.mark(last)
            lane, eng = (act, S) if j % 2 else (dve, V)
            lane.wait(pe.last)
            dst = gate_all[:, 2 * j:2 * j + 2, :]
            if j % 2:
                act.mark(S.activation(dst, pair(b), ACT.Copy))
            else:
                dve.mark(V.tensor_copy(dst, pair(b)))
            bank_free[b] = [lane.last]
        dve.wait(act.last)

        done = gated_units(EXPERTS, h_points, gate_all)
        x_points = add_banks(lambda m: mod[:, 5 * KD + m:5 * KD + m + 1], done)

        BAND = 3 * P
        at[0] = 0
        s_band = sem("s_band")
        bands = []
        n_band = 0
        pool.wait(dve.last, pe.last, act.last)
        for name in ("lru_w_a_2", "lru_w_x_2"):
            band = scratch(KR * BAND).rearrange("p (c n) -> p c n", c=KR)
            bands.append(band)
            pool.mark(G.memset(band, 0.0))
            pool.wait(pool.last)
            for h in range(LRU_HEADS):
                r = h * LRU_DIM
                while r < (h + 1) * LRU_DIM:
                    c = r // P
                    end = min((h + 1) * LRU_DIM, (c + 1) * P)
                    c0 = h * LRU_DIM - (c - 1) * P
                    G.dma_start(band[r - c * P:end - c * P, c, c0:c0 + LRU_DIM],
                                a[name][h, r - h * LRU_DIM:end - h * LRU_DIM, :]
                                ).then_inc(s_band, 16)
                    n_band += 16
                    r = end
        bands_ready = (s_band, n_band)

        def ffn(which, layer, x_points):
            h = rms_norm(lambda k: col(f"{which}_norm_2", layer * KD + k), x_points)
            return add_banks(0.5, gated_units(D_FF // CW, h))

        s_p = sem("s_p")

        def per_layer_embedding(layer, x_points):
            tok = arena[:, 0:TT * 256].rearrange("p (t d) -> p t d", t=TT)
            pT = arena[:, TT * 256:TT * 256 + 2 * T].rearrange("p (k t) -> p k t", k=2)
            sg = arena[:, 1024:1024 + D * TT].rearrange("p (m t) -> p m t", m=KD)
            pool.wait(dve.last, act.last, pe.last)
            G.dma_start(tok, a["p_2"][layer].rearrange("(t p) d -> p t d", p=P)
                        ).then_inc(s_p, 16)
            pe.wait((s_p, 16 * (layer + 1)), *bank_free[1], *bank_free[0])
            for k in range(2):
                for t in range(TT):
                    last = T_.transpose(pair(1)[:, k, t * P:(t + 1) * P],
                                        tok[:, t, k * P:(k + 1) * P], ident)
            dve.wait(pe.mark(last), act.last)
            done = dve.mark(V.tensor_copy(pT, pair(1)))
            bank_free[1] = [done]
            p_points = [split_operand(KD + k, pT[:, k, :], [done]) for k in range(2)]
            h = rms_norm(lambda k: col("ple_norm_2", layer * KD + k), x_points)
            proj = row_product([a_hi[:, KD, :], a_hi[:, KD + 1, :]],
                               [a_lo[:, KD, :], a_lo[:, KD + 1, :]], True, True, p_points)
            points = []
            for j in range(4):
                done = column_product(j, h if j == 0 else None)
                act.wait(done)
                act.mark(S.activation(sg[:, 2 * j:2 * j + 2, :], pair(j), ACT.Sigmoid))
                bank_free[j] = [act.last]
                dve.wait(act.last, proj)
                dve.mark(V.tensor_tensor(sg[:, 2 * j:2 * j + 2, :], sg[:, 2 * j:2 * j + 2, :],
                                         pair(4 + j), ALU.mult))
                bank_free[4 + j] = [dve.last]
                dve.wait(dve.last)
                for c in range(2):
                    points.append(dve.mark(V.tensor_tensor(
                        xT[:, 2 * j + c, :], xT[:, 2 * j + c, :], sg[:, 2 * j + c, :], ALU.add)))
            operand_free[0] = pe.last
            return points

        def lru(x_points):
            base = at[0]
            h = rms_norm(lambda k: col("mix_norm_2", k), x_points)
            nn, an, _ = vec_at["lru_a_param_2"]
            v, e, z, z2, sp_ = (small[:, 40 + i * KR:40 + (i + 1) * KR] for i in range(5))
            dve.wait(act.last)
            dve.mark(V.tensor_scalar(v, vec[:, nn, an:an + KR], -1.0, None, ALU.mult))
            dve.wait(dve.last)
            dve.mark(V.tensor_tensor(e, v, vec[:, nn, an:an + KR], ALU.max))
            act.wait(dve.last)
            act.mark(S.activation(e, e, ACT.Exp, scale=-1.0))
            dve.wait(act.last)
            dve.mark(V.tensor_scalar(z, e, 2.0, None, ALU.add))
            dve.wait(dve.last)
            dve.mark(V.reciprocal(z, z))
            dve.wait(dve.last)
            dve.mark(V.tensor_tensor(z, z, e, ALU.mult))
            dve.wait(dve.last)
            dve.mark(V.tensor_tensor(z2, z, z, ALU.mult))
            dve.wait(dve.last)
            dve.mark(V.tensor_scalar(sp_, z2, 1.0 / 17, 1.0 / 15, ALU.mult, ALU.add))
            for n in (13, 11, 9, 7, 5, 3, 1):
                dve.wait(dve.last)
                dve.mark(V.tensor_tensor(sp_, sp_, z2, ALU.mult))
                dve.wait(dve.last)
                dve.mark(V.tensor_scalar(sp_, sp_, 1.0 / n, None, ALU.add))
            dve.wait(dve.last)
            dve.mark(V.tensor_tensor(sp_, sp_, z, ALU.mult))
            dve.wait(dve.last)
            dve.mark(V.tensor_scalar(v, v, 0.0, None, ALU.max))
            dve.wait(dve.last)
            dve.mark(V.scalar_tensor_tensor(sp_, sp_, 2.0, v, ALU.mult, ALU.add))
            dve.wait(dve.last)
            dve.mark(V.tensor_scalar(sp_, sp_, -LRU_C, None, ALU.mult))
            gelu = scratch(KR * T).rearrange("p (c t) -> p c t", c=KR)
            xb = normed
            for j in range(KR):
                b = j % 4
                done = column_product(b, h if j == 0 else None)
                if j < KR // 2:
                    act.wait(done, dve.last)
                    act.mark(S.activation(gelu[:, 2 * j:2 * j + 2, :], pair(b), ACT.Copy))
                    bank_free[b] = [act.last]
                else:
                    jj = 2 * j - KR
                    act.wait(done, dve.last)
                    act.mark(S.activation(xb[:, jj:jj + 2, :], pair(b), ACT.Copy))
                    bank_free[b] = [act.last]
            operand_free[0] = pe.last
            for c in range(KR):
                g, w1 = gelu[:, c, :], (tmp_a, tmp_b)[c % 2]
                dve.wait(act.last, dve.last)
                dve.mark(V.tensor_tensor(w1, g, g, ALU.mult))
                dve.wait(dve.last)
                dve.mark(V.tensor_scalar(w1, w1, 0.044715, 1.0, ALU.mult, ALU.add))
                dve.wait(dve.last)
                dve.mark(V.tensor_tensor(w1, w1, g, ALU.mult))
                act.wait(dve.last)
                act.mark(S.activation(w1, w1, ACT.Tanh, scale=0.7978845608028654))
                dve.wait(act.last)
                dve.mark(V.tensor_scalar(w1, w1, 1.0, 0.5, ALU.add, ALU.mult))
                dve.wait(dve.last)
                dve.mark(V.tensor_tensor(g, g, w1, ALU.mult))
            xcs = sb_xc
            for c in range(KR):
                dve.wait(dve.last, act.last)
                dve.mark(V.tensor_scalar(xcs[:, c, :], xb[:, c, :], col("lru_conv_w_2", 3 * KR + c),
                                         col("lru_conv_b_2", c), ALU.mult, ALU.add))
                for k in range(3):
                    sh = 3 - k
                    dve.wait(dve.last)
                    dve.mark(V.scalar_tensor_tensor(
                        xcs[:, c, sh:], xb[:, c, 0:T - sh], col("lru_conv_w_2", k * KR + c),
                        xcs[:, c, sh:], ALU.mult, ALU.add))
            pe.wait(dve.last, bands_ready)
            y_points = []
            for c in range(KR):
                half = c // (KR // 2) * (KR // 2)
                source = [i for i in (c - 1, c, c + 1) if half <= i < half + KR // 2]
                b = c % 4
                pe.wait(*bank_free[b])
                for n in range(2):
                    for i in source:
                        w = bands[n][:, i, (c - i + 1) * P:(c - i + 2) * P]
                        last = T_.matmul(pair(b)[:, n, :], w, xcs[:, i, :],
                                         start=i == source[0], stop=i == source[-1])
                act.wait(pe.mark(last), dve.last)
                act.mark(S.activation(rstd, pair(b)[:, 0, :], ACT.Sigmoid,
                                      bias=col("lru_b_a_2", c)))
                act.mark(S.activation(var, pair(b)[:, 1, :], ACT.Sigmoid,
                                      bias=col("lru_b_x_2", c)))
                bank_free[b] = [act.last]
                dve.wait(act.last)
                dve.mark(V.tensor_scalar(rstd, rstd, sp_[:, c:c + 1], None, ALU.mult))
                act.wait(dve.last)
                act.mark(S.activation(tmp_a, rstd, ACT.Exp))
                act.mark(S.activation(tmp_b, rstd, ACT.Tanh, scale=-1.0))
                dve.wait(act.last)
                dve.mark(V.tensor_scalar(mean, tmp_b, 1.0, None, ALU.add))
                dve.mark(V.tensor_tensor(var, var, xcs[:, c, :], ALU.mult))
                dve.wait(dve.last)
                dve.mark(V.reciprocal(mean, mean))
                dve.wait(dve.last)
                dve.mark(V.scalar_tensor_tensor(tmp_b, tmp_b, 2.0, mean, ALU.mult, ALU.mult))
                act.wait(dve.last)
                act.mark(S.activation(tmp_b, tmp_b, ACT.Sqrt))
                dve.wait(act.last)
                dve.mark(V.tensor_tensor(var, var, tmp_b, ALU.mult))
                dve.wait(dve.last)
                dve.mark(V.tensor_tensor_scan(mean, tmp_a, var, 0.0, ALU.mult, ALU.add))
                dve.wait(dve.last)
                done = dve.mark(V.tensor_tensor(gelu[:, c, :], gelu[:, c, :], mean, ALU.mult))
                y_points.append(split_operand(c, gelu[:, c, :], [done]))
            for j in range(KR // 2):
                done = row_product([a_hi[:, 2 * j + c, :] for c in range(2)],
                                   [a_lo[:, 2 * j + c, :] for c in range(2)],
                                   j == 0, j == KR // 2 - 1, y_points[2 * j:2 * j + 2])
            operand_free[0] = pe.last
            return add_banks(1.0, done)

        def pooling(x_points):
            rms_norm(lambda k: col("mix_norm_2", KD + k), x_points)
            padded = arena[:, 0:3 * 2 * TW].rearrange("p (b c t) -> p b c t", b=3, c=2)
            pool.wait(dve.last, act.last, pe.last)
            pool.mark(G.memset(padded[:, :, :, 0:PAD], 0.0))
            points = []
            for g, win in enumerate(WINDOWS):
                x, s, s_next = padded[:, 0], padded[:, 1], padded[:, 2]
                dve.wait(pool.last, dve.last, act.last)
                dve.mark(V.tensor_copy(x[:, :, PAD:], normed[:, 2 * g:2 * g + 2, :]))
                src, step = x, 1
                while step < win:
                    dst = s if src is not s else s_next
                    dve.wait(dve.last)
                    dve.mark(V.tensor_tensor(dst[:, :, PAD:], src[:, :, PAD:],
                                             src[:, :, PAD - step:TW - step], ALU.add))
                    src, step = dst, 2 * step
                first = cst[:, C_COUNT + 16 * g:C_COUNT + 16 * g + 16]
                dve.wait(dve.last)
                for c in range(2):
                    dve.mark(V.tensor_tensor(src[:, c, PAD:PAD + 16], src[:, c, PAD:PAD + 16],
                                             first, ALU.mult))
                dve.mark(V.tensor_scalar(src[:, :, PAD + 16:], src[:, :, PAD + 16:], 1.0 / win,
                                         None, ALU.mult))
                dve.wait(dve.last)
                for c in range(2):
                    done = dve.mark(V.tensor_tensor(normed[:, 2 * g + c, :], src[:, c, PAD:],
                                                    x[:, c, PAD:], ALU.subtract))
                for c in range(2):
                    points.append(split_operand(2 * g + c, normed[:, 2 * g + c, :], [done]))
            i = take()
            wh, wl = weights(i)
            out_points = []
            for g in range(len(WINDOWS)):
                pe.wait(*bank_free[g])
                for m in range(2):
                    for k in range(2):
                        j = 2 * g + k
                        pe.wait(points[j])
                        last = product3(pair(g)[:, m, :],
                                        (wh[:, j, m * P:(m + 1) * P], wl[:, j, m * P:(m + 1) * P]),
                                        (a_hi[:, j, :], a_lo[:, j, :]), k == 0, k == 1)
                dve.wait(pe.mark(last), dve.last)
                for m in range(2):
                    c = 2 * g + m
                    dve.mark(V.tensor_scalar(tmp_a, pair(g)[:, m, :], col("pool_b_2", c),
                                             col("pool_scale_2", c), ALU.add, ALU.mult))
                    dve.wait(dve.last)
                    out_points.append(dve.mark(V.tensor_tensor(xT[:, c, :], xT[:, c, :], tmp_a,
                                                               ALU.add)))
                    dve.wait(dve.last)
                bank_free[g] = [dve.last]
            give_back(i, pe.last)
            operand_free[0] = pe.last
            return out_points

        sb_xc = arena[:, 7680 + KR * T:7680 + 2 * KR * T].rearrange("p (c t) -> p c t", c=KR)
        x_points = ffn("ffn1", 0, x_points)
        x_points = lru(x_points)
        x_points = ffn("ffn2", 0, x_points)
        x_points = per_layer_embedding(0, x_points)
        x_points = ffn("ffn1", 1, x_points)
        x_points = pooling(x_points)
        x_points = ffn("ffn2", 1, x_points)
        x_points = per_layer_embedding(1, x_points)

        rms_statistics(xT, KD, 0, x_points)
        y_tok = arena[:, 0:TT * D].rearrange("p (t d) -> p t d", t=TT)
        s_out = sem("s_out")
        for k in range(KD):
            dve.wait(dve.last)
            dve.mark(V.scalar_tensor_tensor(normed[:, k, :], xT[:, k, :], col("final_norm_2", k),
                                            rstd, ALU.mult, ALU.mult))
        pe.wait(dve.last)
        for t in range(TT):
            for half in range(2):
                b = 1 + 2 * t + half
                pe.wait(*bank_free[b])
                for k in range(4):
                    last = T_.transpose(bank[b][:, k * P:(k + 1) * P],
                                        normed[:, 4 * half + k, t * P:(t + 1) * P], ident)
                act.wait(pe.mark(last), dve.last)
                act.mark(S.activation(y_tok[:, t, half * 512:(half + 1) * 512], bank[b][:, :],
                                      ACT.Copy))
            sp.wait(act.last)
            L.dma_start(out[t * P:(t + 1) * P, :], y_tok[:, t, :]).then_inc(s_out, 16)
        L.wait_ge(s_out, 16 * TT)
        assert n_taken == len(entries)


def two_pi_parts():
    import math
    rest, parts = 2 * math.pi, []
    for bits in (8, 8, 8):
        exponent = math.floor(math.log2(rest)) + 1
        unit = 2.0 ** (exponent - bits)
        part = math.floor(rest / unit) * unit
        parts.append(part)
        rest -= part
    return parts + [rest]


def constants():
    import numpy as np
    c = np.zeros((P, C_END), np.float32)
    c[:, C_IDENT:C_IDENT + P] = np.eye(P, dtype=np.float32)
    half = ROPE // 2
    for j in range(half):
        c[NOPE + half + j, C_ROT + NOPE + j] = -1.0
        c[NOPE + j, C_ROT + NOPE + half + j] = 1.0
    c[0:CHUNK, C_MASK + CHUNK:C_MASK + P] = -1e30
    freq = 10000.0 ** (-np.arange(0, ROPE, 2) / ROPE)
    c[NOPE:NOPE + half, C_FREQ] = freq
    c[NOPE + half:QK, C_FREQ] = freq
    for g, win in enumerate(WINDOWS):
        for t in range(16):
            c[:, C_COUNT + 16 * g + t] = 1.0 / min(t + 1, win)
    c[:, C_DESC:C_DESC + EXPERTS] = np.arange(EXPERTS, 0, -1)
    c[0:ROPE, C_SHIFT + NOPE:C_SHIFT + QK] = np.eye(ROPE)
    return c


NAMES = ["x", "c", "positions", "w_ada", "b_ada", "norm_mix", "w_in", "conv_w", "conv_b",
         "conv_ln_g", "conv_ln_b", "q_a_norm", "w_q_b", "kv_a_norm", "w_kv_b", "q_norm", "k_norm",
         "w_out", "norm_ffn", "w_group", "b_group", "w_expert", "b_expert", "w_gate_e", "w_up_e",
         "w_down_e", "p_2", "ffn1_norm_2", "ffn1_w_gate_2", "ffn1_w_up_2", "ffn1_w_down_2",
         "mix_norm_2", "lru_w_in_2", "lru_conv_w_2", "lru_conv_b_2", "lru_w_a_2", "lru_b_a_2",
         "lru_w_x_2", "lru_b_x_2", "lru_a_param_2", "lru_w_out_2", "pool_w_2", "pool_b_2",
         "pool_scale_2", "ffn2_norm_2", "ffn2_w_gate_2", "ffn2_w_up_2", "ffn2_w_down_2",
         "ple_norm_2", "ple_w_gate_2", "ple_w_proj_2", "final_norm_2"]
KEEP_LEADING = {"positions", "final_norm_2", "p_2", "ffn1_norm_2", "ffn2_norm_2", "mix_norm_2",
                "ple_norm_2", "ffn1_w_gate_2", "ffn1_w_up_2", "ffn1_w_down_2", "ffn2_w_gate_2",
                "ffn2_w_up_2", "ffn2_w_down_2", "ple_w_gate_2", "ple_w_proj_2"}


def kernel(**inputs):
    import numpy as np
    import concourse.bacc as bacc
    from concourse.bass_utils import run_bass_kernel_spmd

    nc = bacc.Bacc("TRN2", target_bir_lowering=False, num_devices=1)
    arrays, aps = {}, {}
    for name in NAMES:
        array = np.ascontiguousarray(inputs[name])
        if name not in KEEP_LEADING:
            array = array.reshape(array.shape[1:])
        if name == "p_2":
            array = array.reshape(2, T, 256)
        arrays["in_" + name] = array
        aps[name] = nc.dram_tensor("in_" + name, array.shape, mybir.dt.from_np(array.dtype),
                                   kind="ExternalInput").ap()
    arrays["in_constants"] = constants()
    consts = nc.dram_tensor("in_constants", (P, C_END), F32, kind="ExternalInput").ap()
    out = nc.dram_tensor("out", (T, D), F32, kind="ExternalOutput").ap()
    build(nc, aps, consts, out)
    result = run_bass_kernel_spmd(nc, [arrays], core_ids=[0])
    return result.results[0]["out"].reshape(1, T, D)
```

```python
from contextlib import ExitStack

import concourse.bass as bass
from concourse import mybir

F32 = mybir.dt.float32
F32R = mybir.dt.float32r
I32 = mybir.dt.int32
ALU = mybir.AluOpType
ACT = mybir.ActivationFunctionType
AX = mybir.AxisListType.X

P = 128
T = 256
TT = T // P
D = 1024
KD = D // P
SLOT = 2048
CW = SLOT // KD
RW = SLOT // D
N_RAW = 4
N_SPLIT = 4
AHEAD = N_SPLIT - 1
EPS = 1e-6
ARENA = 12832

CONV_CH, CONV_K = 512, 31
KC = CONV_CH // P
HEADS, NOPE, ROPE, VD = 8, 64, 32, 64
QK = NOPE + ROPE
GROUPS, PER_GROUP = 4, 8
EXPERTS = GROUPS * PER_GROUP
CHUNK = 64
D_FF = 2816
D_RNN = 1280
KR = D_RNN // P
LRU_HEADS, LRU_DIM = 16, 80
LRU_C = 8.0
WINDOWS = (2, 4, 8, 16)
PAD = 32
TW = PAD + T

C_IDENT = 0
C_ROT = C_IDENT + P
C_MASK = C_ROT + QK
C_FREQ = C_MASK + P
C_COUNT = C_FREQ + 1
C_DESC = C_COUNT + len(WINDOWS) * 16
C_SHIFT = C_DESC + EXPERTS
C_END = C_SHIFT + QK

VEC_A = [("b_ada", 48), ("norm_mix", 8), ("norm_ffn", 8), ("c", 8), ("conv_b", 4),
         ("conv_ln_g", 4), ("conv_ln_b", 4), ("q_a_norm", 2), ("kv_a_norm", 1)]
VEC_B = [("ffn1_norm_2", 16), ("mix_norm_2", 16), ("ffn2_norm_2", 16), ("ple_norm_2", 16),
         ("final_norm_2", 8), ("pool_b_2", 8), ("pool_scale_2", 8),
         ("q_norm", 1), ("k_norm", 1)]
VEC_C = [("conv_w", CONV_K * KC)]
VEC_D = [("lru_conv_w_2", 4 * KR), ("lru_conv_b_2", KR), ("lru_b_a_2", KR), ("lru_b_x_2", KR),
         ("lru_a_param_2", KR)]


class Lane:

    def __init__(self, engine, semaphore):
        self.engine, self.semaphore, self.count, self.seen = engine, semaphore, 0, {}

    def mark(self, instruction):
        instruction.then_inc(self.semaphore, 1)
        self.count += 1
        return self.semaphore, self.count

    @property
    def last(self):
        return self.semaphore, self.count

    def wait(self, *points):
        for semaphore, value in points:
            if value > self.seen.get(id(semaphore), 0):
                self.engine.wait_ge(semaphore, value)
                self.seen[id(semaphore)] = value


def build(nc, a, consts, out):
    ctx = ExitStack()
    with ctx:
        def sb(name, shape, dt=F32):
            return ctx.enter_context(nc.sbuf_tensor(name, shape, dt))

        def sem(name):
            return ctx.enter_context(nc.semaphore(name))

        pe, act = Lane(nc.tensor, sem("pe")), Lane(nc.scalar, sem("act"))
        dve, pool = Lane(nc.vector, sem("dve")), Lane(nc.gpsimd, sem("pool"))
        sp = Lane(nc.sync, sem("sp"))
        T_, V, S, G, L = nc.tensor, nc.vector, nc.scalar, nc.gpsimd, nc.sync

        bank = [ctx.enter_context(nc.psum_tensor(f"bank{b}", [P, 512], F32)) for b in range(8)]
        bank_free = [[] for _ in range(8)]

        def pair(b):
            return bank[b][:, :].rearrange("p (c t) -> p c t", c=2)

        raw = [sb(f"raw{i}", [P, SLOT]) for i in range(N_RAW)]
        w_hi = [sb(f"w_hi{i}", [P, SLOT], F32R) for i in range(N_SPLIT)]
        w_lo = [sb(f"w_lo{i}", [P, SLOT], F32R) for i in range(N_SPLIT)]
        xT = sb("xT", [P, KD, T])
        normed = sb("normed", [P, KR, T])
        a_hi = sb("a_hi", [P, KR, T], F32R)
        a_lo = sb("a_lo", [P, KR, T], F32R)
        hid = sb("hid", [P, 2, 2 * T])
        h_hi = sb("h_hi", [P, 2, 2 * T], F32R)
        h_lo = sb("h_lo", [P, 2, 2 * T], F32R)
        stat = sb("stat", [P, 5, T])
        cst = sb("cst", [P, C_END])
        ones = sb("ones", [P, P])
        eps = sb("eps", [P, 1])
        vec = sb("vec", [P, 4, P])
        mod = sb("mod", [P, 48])
        gmod = sb("gmod", [P, 2, KD])
        small = sb("small", [P, 96])
        arena = sb("arena", [P, ARENA])
        rows = arena[:, TT * D:TT * D + 4 * P].rearrange("p (n c) -> p n c", n=4)

        cols = vec[:, 3, 80:128]
        roots2, roots16 = vec[:, 0, 88:90], vec[:, 0, 90:106]
        ident = cst[:, C_IDENT:C_IDENT + P]
        rstd, var, tmp_a, tmp_b, mean = (stat[:, i, :] for i in range(5))
        rstd2 = stat[:, 0:1, :].to_broadcast([P, 2, T])
        squares = arena[:, ARENA - KD * T:].rearrange("p (c t) -> p c t", c=KD)

        vec_at = {}
        for n, group in enumerate((VEC_A, VEC_B, VEC_C, VEC_D)):
            at = 0
            for name, count in group:
                vec_at[name] = (n, at, count)
                at += count

        def col(name, j):
            n, at, _ = vec_at[name]
            return vec[:, n, at + j:at + j + 1]

        s_vec, s_pos, s_route, s_x = sem("s_vec"), sem("s_pos"), sem("s_route"), sem("s_x")
        L.dma_start(arena[:, 0:TT * D].rearrange("p (t d) -> p t d", t=TT),
                    a["x"].rearrange("(t p) d -> p t d", p=P)).then_inc(s_x, 16)
        pos_i = arena[0:1, TT * D + 4 * P:TT * D + 4 * P + T].bitcast(I32)
        bias_row = small[0:1, 4:4 + GROUPS + EXPERTS]
        w_route = sb("w_route", [P, KD, GROUPS + EXPERTS])
        S.dma_start(rows, a["vectors"]).then_inc(s_vec, 16)
        S.dma_start(cst[:, :], consts).then_inc(s_vec, 16)
        S.dma_start(pos_i, a["positions"]).then_inc(s_pos, 16)
        S.dma_start(w_route[:, :, :], a["w_route"].rearrange("(k p) n -> p k n", p=P)
                    ).then_inc(s_route, 16)
        S.dma_start(bias_row, a["b_route"]).then_inc(s_route, 16)

        entries = []

        def columns(name, c0, width=CW, split=True, index=None):
            w = a[name] if index is None else a[name][index]
            entries.append((w[:, c0:c0 + width].rearrange("(k p) n -> p k n", p=P),
                            w.shape[0] // P, width, split))

        def row_block(name, r0, split=True, index=None):
            w = a[name] if index is None else a[name][index]
            entries.append((w[r0:r0 + RW * P, :].rearrange("(k p) n -> p k n", p=P), RW, D, split))

        def units(names, n, per_expert, index=None):
            gate, up, down = names
            for u in range(n):
                i, c0 = (u, 0) if per_expert else (index, u * CW)
                columns(gate, c0, index=i)
                columns(up, c0, index=i)
                if u:
                    j, r0 = (u - 1, 0) if per_expert else (index, (u - 1) * CW)
                    row_block(down, r0, index=j)
            j, r0 = (n - 1, 0) if per_expert else (index, (n - 1) * CW)
            row_block(down, r0, index=j)

        def ple_entries(i):
            row_block("ple_w_proj_2", 0, index=i)
            for c0 in range(0, D, CW):
                columns("ple_w_gate_2", c0, index=i)

        for c0 in range(0, 2 * D, CW):
            columns("w_ada", c0, split=False)
        columns("w_in", 1024)
        columns("w_in", 0)
        columns("w_in", 1280, width=160)
        for c0 in range(CW, 1024, CW):
            columns("w_in", c0)
        entries.append((a["w_q_b"].rearrange("(k p) n -> p k n", p=P), 2, HEADS * QK, False))
        entries.append((a["w_kv_b"].rearrange("(k p) n -> p k n", p=P), 1, HEADS * 128, False))
        for c0 in range(2 * D, 6 * D, CW):
            columns("w_ada", c0, split=False)
        for c0 in range(0, D, CW):
            columns("w_out", c0)
        units(("w_gate_e", "w_up_e", "w_down_e"), EXPERTS, True)
        for i in range(2):
            units(("ffn1_w_gate_2", "ffn1_w_up_2", "ffn1_w_down_2"), D_FF // CW, False, i)
            if i == 0:
                for c0 in list(range(D_RNN, 2 * D_RNN, CW)) + list(range(0, D_RNN, CW)):
                    columns("lru_w_in_2", c0)
                for r0 in range(0, D_RNN, RW * P):
                    row_block("lru_w_out_2", r0)
            else:
                entries.append((a["pool_w_2"].rearrange("g (k p) n -> p (g k) n", p=P), 8, CW,
                                True))
            units(("ffn2_w_gate_2", "ffn2_w_up_2", "ffn2_w_down_2"), D_FF // CW, False, i)
            ple_entries(i)

        s_raw = [sem(f"s_raw{i}") for i in range(N_RAW)]
        n_loaded = n_split = n_taken = 0
        raw_free = [[] for _ in range(N_RAW)]
        split_free = [None] * N_SPLIT
        where = {}
        ready = {}
        n_splits = n_returned = 0

        released = [False] * len(entries)

        def load_more():
            nonlocal n_loaded
            while n_loaded < len(entries) and (n_loaded < N_RAW or released[n_loaded - N_RAW]):
                src, k, width, _ = entries[n_loaded]
                slot = n_loaded % N_RAW
                sp.wait(*raw_free[slot])
                L.dma_start(raw[slot][:, 0:k * width].rearrange("p (k n) -> p k n", k=k),
                            src).then_inc(s_raw[slot], 16)
                n_loaded += 1

        def release(i, points):
            raw_free[i % N_RAW] = points
            released[i] = True
            load_more()

        def loaded(i):
            return s_raw[i % N_RAW], 16 * (i // N_RAW + 1)

        def split_next():
            nonlocal n_split, n_splits
            i = n_split
            n_split += 1
            _, k, width, split = entries[i]
            load_more()
            assert n_loaded > i
            if not split:
                ready[i] = [loaded(i)]
                return
            s, n, size = i % N_RAW, n_splits % N_SPLIT, k * width
            n_splits += 1
            where[i] = n
            act.wait(loaded(i))
            if split_free[n]:
                act.wait(split_free[n])
                dve.wait(split_free[n])
            hi = act.mark(S.activation(w_hi[n][:, 0:size], raw[s][:, 0:size], ACT.Copy))
            dve.wait(loaded(i), hi)
            lo = dve.mark(V.tensor_tensor(w_lo[n][:, 0:size], raw[s][:, 0:size],
                                          w_hi[n][:, 0:size].bitcast(F32), ALU.subtract))
            ready[i] = [hi, lo]
            release(i, [hi, lo])

        def take():
            nonlocal n_taken
            i = n_taken
            n_taken += 1
            while n_split <= i:
                split_next()
            look_ahead(i)
            pe.wait(*ready[i])
            return i

        def look_ahead(i):
            while (n_split < n_loaded and n_split <= i + AHEAD
                   and (not entries[n_split][3] or n_splits - n_returned < N_SPLIT)):
                split_next()

        def give_back(i, point):
            nonlocal n_returned
            if entries[i][3]:
                split_free[where[i]] = point
                n_returned += 1
            else:
                release(i, [point])
            look_ahead(i)

        def weights(i):
            _, k, width, split = entries[i]
            if not split:
                return raw[i % N_RAW][:, 0:k * width].rearrange("p (k n) -> p k n", k=k)
            n = where[i]
            return tuple(w[n][:, 0:k * width].rearrange("p (k n) -> p k n", k=k)
                         for w in (w_hi, w_lo))

        def product3(dst, w, x, first, last, check=True):
            (wh, wl), (xh, xl) = w, x
            T_.matmul(dst, wh, xh, start=first, stop=False, skip_group_check=not check)
            T_.matmul(dst, wh, xl, start=False, stop=False, skip_group_check=not check)
            return T_.matmul(dst, wl, xh, start=False, stop=last, skip_group_check=not check)

        def column_product(b, x_ready, chunks=KD, width=CW, x0=0):
            i = take()
            wh, wl = weights(i)
            pe.wait(*bank_free[b])
            m0 = 0
            while m0 < width:
                m = min(P, width - m0)
                for k in range(chunks):
                    if x_ready and m0 == 0:
                        pe.wait(x_ready[k])
                    last = product3(pair(b)[0:m, m0 // P, :],
                                    (wh[:, k, m0:m0 + m], wl[:, k, m0:m0 + m]),
                                    (a_hi[:, x0 + k, :], a_lo[:, x0 + k, :]),
                                    k == 0, k == chunks - 1)
                m0 += m
            point = pe.mark(last)
            give_back(i, point)
            return point

        def row_product(x_hi, x_lo, first, last, x_ready):
            i = take()
            wh, wl = weights(i)
            pe.wait(*x_ready)
            if first:
                for b in range(4, 8):
                    pe.wait(*bank_free[b])
            points = []
            for m in range(KD):
                for k in range(RW):
                    ins = product3(pair(4 + m // 2)[:, m % 2, :],
                                   (wh[:, k, m * P:(m + 1) * P], wl[:, k, m * P:(m + 1) * P]),
                                   (x_hi[k], x_lo[k]),
                                   first and k == 0 and m % 2 == 0, last and k == RW - 1, False)
                if last and m % 2:
                    points.append(pe.mark(ins))
            give_back(i, pe.last if last else pe.mark(ins))
            return points or [pe.last]

        operand_free = [None]

        def split_operand(k, src, src_ready):
            act.wait(*src_ready)
            if operand_free[0]:
                act.wait(operand_free[0])
                dve.wait(operand_free[0])
            hi = act.mark(S.activation(a_hi[:, k, :], src, ACT.Copy))
            dve.wait(hi, *src_ready)
            return dve.mark(V.tensor_tensor(a_lo[:, k, :], src, a_hi[:, k, :].bitcast(F32),
                                            ALU.subtract))

        squares_free, squares_ready = [None], [None]

        def square(src, k, x_ready):
            act.wait(x_ready)
            if k == 0 and squares_free[0]:
                act.wait(squares_free[0])
            done = act.mark(S.activation(squares[:, k, :], src[:, k, :], ACT.Square))
            pool.wait(done)
            if k > 1:
                pool.wait(pool.last)
            if k:
                done = pool.mark(G.tensor_tensor(squares[:, 0, :], squares[:, 0, :],
                                                 squares[:, k, :], ALU.add))
            squares_ready[0] = done

        def token_roots(total, n, roots):
            w = total.shape[-1]
            v, ta, tb = (cols[:, 16 * i:16 * i + w] for i in range(3))
            dve.wait(dve.last)
            dve.mark(V.tensor_scalar(v, total, 1.0 / n, EPS, ALU.mult, ALU.add))
            act.wait(dve.last)
            act.mark(S.activation(ta, v, ACT.Sqrt))
            dve.wait(act.last)
            dve.mark(V.reciprocal(tb, ta))
            dve.wait(dve.last)
            dve.mark(V.tensor_tensor(roots, tb, tb, ALU.mult))
            dve.wait(dve.last)
            dve.mark(V.tensor_tensor(roots, roots, v, ALU.mult))
            dve.wait(dve.last)
            dve.mark(V.tensor_scalar(roots, roots, -0.5, 1.5, ALU.mult, ALU.add))
            dve.wait(dve.last)
            return dve.mark(V.tensor_tensor(roots, roots, tb, ALU.mult))

        def as_diagonals(values, dst):
            for t in range(TT):
                dve.wait(dve.last)
                done = dve.mark(V.tensor_scalar(dst[:, t * P:(t + 1) * P], ident,
                                                values[:, t:t + 1], None, ALU.mult))
            return done

        def sum_squares_start(n_chunks, b, at=0, roots=roots2, diagonals=tmp_a):
            pe.wait(consts_ready, *bank_free[b])
            pe.wait(squares_ready[0])
            for t in range(TT):
                last = T_.matmul(bank[b][:, t:t + 1], squares[:, at, t * P:(t + 1) * P],
                                 ones[:, 0:1], start=True, stop=True)
            dve.wait(pe.mark(last))
            squares_free[0] = pe.last
            token_roots(bank[b][:, 0:TT], n_chunks * P, roots)
            bank_free[b] = [dve.last]
            return as_diagonals(roots, diagonals)

        def sum_squares_end(b, ready, diagonals=tmp_a, dst=rstd):
            pe.wait(ready, *bank_free[b])
            dve.wait(pe.mark(T_.matmul(pair(b)[:, 0, :], ones[:, :], diagonals, start=True,
                                       stop=True)), dve.last, act.last)
            point = dve.mark(V.tensor_copy(dst, pair(b)[:, 0, :]))
            bank_free[b] = [point]
            return point

        def sum_squares(n_chunks, b):
            return sum_squares_end(b, sum_squares_start(n_chunks, b))

        def rms_statistics(src, n_chunks, b, x_ready):
            for k in range(n_chunks):
                square(src, k, x_ready[k])
            return sum_squares(n_chunks, b)

        def rms_norm(gain, x_ready, shift=None):
            rms_statistics(xT, KD, 0, x_ready)
            points = []
            for k in range(KD):
                dve.wait(dve.last)
                done = dve.mark(V.scalar_tensor_tensor(normed[:, k, :], xT[:, k, :], gain(k),
                                                       rstd, ALU.mult, ALU.mult))
                if shift is not None:
                    dve.wait(done)
                    done = dve.mark(V.tensor_scalar(normed[:, k, :], normed[:, k, :], shift(k),
                                                    None, ALU.add))
                points.append(split_operand(k, normed[:, k, :], [done]))
            return points

        def scaled(gain, x_ready):
            points = []
            for k in range(KD):
                dve.wait(x_ready[k])
                done = dve.mark(V.tensor_scalar(normed[:, k, :], xT[:, k, :], gain(k), None,
                                                ALU.mult))
                points.append(split_operand(k, normed[:, k, :], [done]))
                square(xT, k, x_ready[k])
            return points

        def two_column_products(b0, b1, x_ready):
            entries_ = [take(), take()]
            ws = [weights(i) for i in entries_]
            pe.wait(*bank_free[b0], *bank_free[b1])
            for k in range(KD):
                pe.wait(x_ready[k])
                for b, (wh, wl) in zip((b0, b1), ws):
                    for m in range(2):
                        last = product3(pair(b)[:, m, :],
                                        (wh[:, k, m * P:(m + 1) * P], wl[:, k, m * P:(m + 1) * P]),
                                        (a_hi[:, k, :], a_lo[:, k, :]), k == 0 and m == 0,
                                        k == KD - 1, False)
            point = pe.mark(last)
            for i in entries_:
                give_back(i, point)
            return point

        def gated_units(n, x_ready, statistics=False, after_second=None, expert_gates=None,
                        before_last=None):
            hidden = [None] * n
            down_done = [None] * n
            products = [None] * n

            def product(u):
                s = u % 2
                if u == 0:
                    products[u] = two_column_products(0, 1, x_ready)
                else:
                    if u == 1 and statistics:
                        diagonals = sum_squares_start(KD, 4)
                    column_product(2 * s, None)
                    if u == 1 and statistics:
                        sum_squares_end(4, diagonals)
                        hide(0)
                    products[u] = column_product(2 * s + 1, None)

            def hide(u):
                s = u % 2
                gate_b, up_b = 2 * s, 2 * s + 1
                h = hid[:, s, :].rearrange("p (c t) -> p c t", c=2)
                act.wait(products[u])
                if u >= 2:
                    act.wait(hidden[u - 2])
                    dve.wait(hidden[u - 2])
                if expert_gates is None:
                    dve.wait(products[u], dve.last)
                    dve.mark(V.tensor_tensor(h, pair(gate_b), rstd2, ALU.mult))
                    act.wait(dve.last)
                    act.mark(S.activation(h, h, ACT.Silu))
                    bank_free[gate_b] = [dve.last]
                else:
                    act.mark(S.activation(h, pair(gate_b), ACT.Silu))
                    bank_free[gate_b] = [act.last]
                dve.wait(act.last, products[u])
                dve.mark(V.tensor_tensor(h, h, pair(up_b), ALU.mult))
                bank_free[up_b] = [dve.last]
                dve.wait(dve.last)
                scale = rstd2 if expert_gates is None else expert_gates[:, u:u + 1, :].to_broadcast(
                    [P, 2, T])
                dve.mark(V.tensor_tensor(h, h, scale, ALU.mult))
                act.wait(dve.last)
                if u >= 2:
                    act.wait(*down_done[u - 2])
                    dve.wait(*down_done[u - 2])
                act.mark(S.activation(h_hi[:, s, :], hid[:, s, :], ACT.Copy))
                dve.wait(act.last)
                hidden[u] = dve.mark(V.tensor_tensor(h_lo[:, s, :], hid[:, s, :],
                                                     h_hi[:, s, :].bitcast(F32), ALU.subtract))

            def down(u):
                s = u % 2
                hi, lo = (h[:, s, :].rearrange("p (c t) -> p c t", c=2) for h in (h_hi, h_lo))
                down_done[u] = row_product([hi[:, 0, :], hi[:, 1, :]], [lo[:, 0, :], lo[:, 1, :]],
                                           u == 0, u == n - 1, [hidden[u]])

            product(0)
            if after_second:
                product(1)
                after_second()
                hide(0)
                hide(1)
                down(0)
            else:
                product(1)
                hide(1)
                down(0)
            for u in range(2, n):
                product(u)
                hide(u)
                down(u - 1)
            if before_last:
                before_last()
            down(n - 1)
            operand_free[0] = pe.last
            return down_done[n - 1]

        def add_banks(factor, done):
            points = []
            for m in range(KD):
                dve.wait(done[m // 2])
                f = factor(m) if callable(factor) else factor
                points.append(dve.mark(V.scalar_tensor_tensor(
                    xT[:, m, :], pair(4 + m // 2)[:, m % 2, :], f, xT[:, m, :],
                    ALU.mult, ALU.add)))
                bank_free[4 + m // 2] = [dve.last]
            return points

        pool.mark(G.memset(ones[:, :], 1.0))
        consts_ready = pool.last

        def turn_vectors(groups, b):
            pe.wait((s_vec, 32), *bank_free[b])
            sizes = [sum(count for _, count in (VEC_A, VEC_B, VEC_C, VEC_D)[n]) for n in groups]
            for n, r in zip(groups, sizes):
                last = T_.transpose(bank[b][:, n * P:n * P + r], rows[0:r, n, :],
                                    ident[0:r, 0:r])
            dve.wait(pe.mark(last))
            for n, r in zip(groups, sizes):
                done = dve.mark(V.tensor_copy(vec[:, n, 0:r], bank[b][:, n * P:n * P + r]))
            bank_free[b] = [done]
            return done

        vectors = turn_vectors((0,), 0)
        c_act = small[:, 40:40 + KD]
        n, at, _ = vec_at["c"]
        act.wait(vectors)
        c_ready = act.mark(S.activation(c_act, vec[:, n, at:at + KD], ACT.Silu))

        x_tok = arena[:, 0:TT * D].rearrange("p (t d) -> p t d", t=TT)
        pe.wait((s_x, 16))
        x_points = []
        for k in range(KD):
            b = 1 + k // 2
            for t in range(TT):
                last = T_.transpose(pair(b)[:, k % 2, t * P:(t + 1) * P],
                                    x_tok[:, t, k * P:(k + 1) * P], ident)
            if k % 2:
                dve.wait(pe.mark(last))
                x_points += 2 * [dve.mark(V.tensor_copy(xT[:, k - 1:k + 1, :], pair(b)))]
                bank_free[b] = [dve.last]
                square(xT, k - 1, dve.last)
                square(xT, k, dve.last)
        sum_squares(KD, 0)
        for k in range(0, KD, 2):
            dve.wait(dve.last)
            dve.mark(V.tensor_tensor(normed[:, k:k + 2, :], xT[:, k:k + 2, :], rstd2, ALU.mult))

        def modulation_slots(first, count):
            pe.wait(c_ready, *bank_free[7])
            for j in range(first, first + count):
                i = take()
                w = weights(i)
                for m in range(2):
                    for k in range(KD):
                        last = T_.matmul(bank[7][:, 2 * j + m:2 * j + m + 1],
                                         w[:, k, m * P:(m + 1) * P], c_act[:, k:k + 1],
                                         start=k == 0, stop=k == KD - 1)
                give_back(i, pe.mark(last))

        def modulation_end(first, count):
            dve.wait(pe.last, vectors)
            nb, ab, _ = vec_at["b_ada"]
            lo, hi = 2 * first, 2 * (first + count)
            dve.mark(V.tensor_tensor(mod[:, lo:hi], bank[7][:, lo:hi], vec[:, nb, ab + lo:ab + hi],
                                     ALU.add))
            bank_free[7] = [dve.last]

        def scaled_gain(row, name, at_scale):
            nn, an, _ = vec_at[name]
            dve.wait(dve.last)
            dve.mark(V.scalar_tensor_tensor(gmod[:, row, :], mod[:, at_scale:at_scale + KD], 1.0,
                                            vec[:, nn, an:an + KD], ALU.add, ALU.mult))
            dve.wait(dve.last)

        cosT, sinT = normed[:, KD, :], normed[:, KD + 1, :]
        pos_row = stat[0:1, 4, :]
        dve.wait((s_pos, 16))
        dve.mark(V.tensor_copy(pos_row, pos_i))
        pe.wait(dve.last, *bank_free[6])
        last = T_.matmul(pair(6)[0:QK, 0, :], ones[0:1, 0:QK], pos_row, start=True, stop=True)
        dve.wait(pe.mark(last))
        ang = cosT[0:QK, :]
        turn = tmp_a[0:QK, :]
        dve.mark(V.tensor_scalar(ang, pair(6)[0:QK, 0, :], cst[0:QK, C_FREQ:C_FREQ + 1], None,
                                 ALU.mult))
        bank_free[6] = [dve.last]
        MAGIC = 12582912.0
        for scalar, op in ((1.0 / 6.283185307179586, ALU.mult), (MAGIC, ALU.add),
                           (-MAGIC, ALU.add)):
            dve.wait(dve.last)
            dve.mark(V.tensor_scalar(turn, ang if op == ALU.mult else turn, scalar, None, op))
        for part in two_pi_parts():
            dve.wait(dve.last)
            dve.mark(V.scalar_tensor_tensor(ang, turn, -part, ang, ALU.mult, ALU.add))
        PI = 3.1415925
        dve.wait(dve.last)
        dve.mark(V.tensor_scalar(ang, ang, PI, -PI, ALU.min, ALU.max))
        act.wait(dve.last)
        act.mark(S.activation(sinT[0:QK, :], ang, ACT.Sin))
        dve.wait(dve.last)
        dve.mark(V.tensor_scalar(turn, ang, -1.0, None, ALU.mult))
        dve.wait(dve.last)
        dve.mark(V.tensor_tensor(turn, turn, ang, ALU.max))
        dve.wait(dve.last)
        dve.mark(V.tensor_scalar(turn, turn, -1.0, 1.5707963267948966, ALU.mult, ALU.add))
        act.wait(dve.last, act.last)
        rope_ready = act.mark(S.activation(cosT[0:QK, :], turn, ACT.Sin))

        modulation_slots(0, 8)
        modulation_end(0, 8)
        scaled_gain(0, "norm_mix", KD)
        h_points = []
        for k in range(KD):
            done = dve.mark(V.tensor_scalar(normed[:, k, :], normed[:, k, :], gmod[:, 0, k:k + 1],
                                            mod[:, k:k + 1], ALU.mult, ALU.add))
            h_points.append(split_operand(k, normed[:, k, :], [done]))

        at = [0]

        def scratch(size, shape=None):
            x = arena[:, at[0]:at[0] + size]
            at[0] += size
            assert at[0] <= ARENA
            return x

        u_pad = scratch(KC * TW).rearrange("p (c t) -> p c t", c=KC)
        qk = scratch(2 * HEADS * T).rearrange("p (s h t) -> p s h t", s=2, h=HEADS)
        v_tok = scratch(TT * HEADS * VD).rearrange("p (t n) -> p t n", t=TT)
        wide = scratch(HEADS * T + HEADS * P)
        p_t = scratch(3 * HEADS * P)
        cq = p_t[:, 0:2 * T].rearrange("p (c t) -> p c t", c=2)
        ckv = p_t[:, 2 * T:3 * T].rearrange("p (c t) -> p c t", c=1)
        k_rope, k_rope_sq = p_t[0:ROPE, 3 * T:4 * T], p_t[0:ROPE, 4 * T:5 * T]
        conv = hid[:, :, :].rearrange("p s (c t) -> p (s c) t", c=2)
        qT, kT = qk[:, 0, :, :], qk[:, 1, :, :]

        turn_vectors((1, 2, 3), 6)
        vectors_ready = dve.last
        pool.wait(pe.last, dve.last)
        pad_ready = pool.mark(G.memset(u_pad[:, :, 0:PAD], 0.0))
        cq_done = two_column_products(1, 5, h_points)
        kv_done = column_product(2, None, width=160)
        act.wait(cq_done, squares_free[0], vectors_ready)
        act.mark(S.activation(cq[:, :, :], pair(1), ACT.Copy))
        bank_free[1] = [act.last]
        act.wait(act.last)
        cq_sq = act.mark(S.activation(squares[:, 0:2, :], cq[:, :, :], ACT.Square))
        pool.wait(cq_sq)
        squares_ready[0] = pool.mark(G.tensor_tensor(squares[:, 0, :], squares[:, 0, :],
                                                     squares[:, 1, :], ALU.add))
        act.wait(kv_done)
        act.mark(S.activation(ckv[:, 0, :], pair(2)[:, 0, :], ACT.Copy))
        kv_ready = act.mark(S.activation(k_rope, pair(2)[0:ROPE, 1, :], ACT.Copy))
        bank_free[2] = [kv_ready]
        act.wait(kv_ready)
        act.mark(S.activation(squares[:, 2, :], ckv[:, 0, :], ACT.Square))
        ckv_sq = act.mark(S.activation(k_rope_sq, k_rope, ACT.Square))

        val23 = column_product(6, None)
        cq_diagonals = sum_squares_start(2, 3)
        squares_ready[0] = ckv_sq
        ckv_diagonals = sum_squares_start(1, 4, 2, roots16[:, 0:TT], tmp_b)
        gate01 = column_product(7, None)
        sum_squares_end(3, cq_diagonals)
        sum_squares_end(4, ckv_diagonals, tmp_b, var)
        for k in range(2):
            dve.wait(dve.last)
            cq_ready = dve.mark(V.scalar_tensor_tensor(cq[:, k, :], cq[:, k, :],
                                                       col("q_a_norm", k), rstd,
                                                       ALU.mult, ALU.mult))
        ckv_ready = dve.mark(V.scalar_tensor_tensor(ckv[:, 0, :], ckv[:, 0, :],
                                                    col("kv_a_norm", 0), var,
                                                    ALU.mult, ALU.mult))
        gate23 = column_product(0, None)
        operand_free[0] = pe.last

        q_sq = normed[:, 0:HEADS, :]
        k_sq = wide[:, 0:HEADS * T].rearrange("p (h t) -> p h t", h=HEADS)
        i = take()
        w = weights(i)
        pe.wait(cq_ready)
        for h in range(HEADS):
            b = (1, 2, 3, 1)[h // 2]
            if h % 2 == 0:
                pe.wait(*bank_free[b])
            for k in range(2):
                last = T_.matmul(pair(b)[0:QK, h % 2, :], w[:, k, h * QK:(h + 1) * QK],
                                 cq[:, k, :], start=k == 0, stop=k == 1)
            if h % 2:
                act.wait(pe.mark(last))
                act.mark(S.activation(q_sq[0:QK, h - 1:h + 1, :], pair(b)[0:QK], ACT.Square))
                act.mark(S.activation(qT[0:QK, h - 1:h + 1, :], pair(b)[0:QK], ACT.Copy,
                                      scale=col("q_norm", 0)[0:QK]))
                bank_free[b] = [act.last]
        give_back(i, pe.last)
        q_ready = act.last

        for j, gate_done in enumerate((gate01, gate23)):
            act.wait(gate_done)
            act.mark(S.activation(conv[:, 2 * j:2 * j + 2, :], pair((7, 0)[j]), ACT.Sigmoid))
            bank_free[(7, 0)[j]] = [act.last]
            dve.wait(act.last, cq_done if j == 0 else val23)
            dve.mark(V.tensor_tensor(u_pad[:, 2 * j:2 * j + 2, PAD:], pair(5 + j),
                                     conv[:, 2 * j:2 * j + 2, :], ALU.mult))
            bank_free[5 + j] = [dve.last]
        dve.wait(dve.last, pad_ready)
        pe.wait(dve.last, pad_ready)

        i = take()
        w = weights(i)
        pe.wait(ckv_ready)
        for h in range(HEADS):
            b = (2, 3, 5, 6)[h // 2]
            if h % 2 == 0:
                pe.wait(*bank_free[b])
            last = T_.matmul(pair(b)[0:NOPE, h % 2, :], w[:, 0, h * 128:h * 128 + NOPE],
                             ckv[:, 0, :], start=True, stop=True)
            if h % 2:
                act.wait(pe.mark(last))
                act.mark(S.activation(k_sq[0:NOPE, h - 1:h + 1, :], pair(b)[0:NOPE], ACT.Square))
                act.mark(S.activation(kT[0:NOPE, h - 1:h + 1, :], pair(b)[0:NOPE], ACT.Copy,
                                      scale=col("k_norm", 0)[0:NOPE]))
                bank_free[b] = [act.last]
        k_ready = act.last
        wv = w[:, 0, :].rearrange("p (h s) -> p h s", s=128)[:, :, NOPE:128]
        for t in range(TT):
            pe.wait(*bank_free[1 + t])
            last = T_.matmul(bank[1 + t][:, :], ckv[:, 0, t * P:(t + 1) * P], wv, start=True,
                             stop=True)
            act.wait(pe.mark(last))
            v_ready = act.mark(S.activation(v_tok[:, t, :], bank[1 + t][:, :], ACT.Copy))
            bank_free[1 + t] = [act.last]
        give_back(i, pe.last)

        ring = [conv[:, 2 + n // 2, (n % 2) * P:(n % 2 + 1) * P] for n in range(4)]
        ring_free = [None] * 4

        def convolution():
            for k in range(CONV_K):
                def tap(c):
                    start = PAD - (CONV_K - 1) + k
                    return u_pad[:, c, start:start + T]

                diagonals = []
                for c in (2, 3):
                    n = (2 * k + c) % 4
                    if ring_free[n]:
                        dve.wait(ring_free[n])
                    diagonals.append(dve.mark(V.tensor_scalar(
                        ring[n], ident, col("conv_w", k * KC + c), None, ALU.mult)))
                for c in (0, 1):
                    if k:
                        dve.wait(taps[c])
                        taps[c] = dve.mark(V.scalar_tensor_tensor(
                            conv[:, c, :], tap(c), col("conv_w", k * KC + c), conv[:, c, :],
                            ALU.mult, ALU.add))
                    else:
                        taps[c] = dve.mark(V.tensor_scalar(
                            conv[:, c, :], tap(c), col("conv_w", c), col("conv_b", c),
                            ALU.mult, ALU.add))
                if k == 0:
                    pe.wait(*bank_free[0])
                pe.wait(diagonals[1])
                for c in (2, 3):
                    n = (2 * k + c) % 4
                    last = T_.matmul(pair(0)[:, c - 2, :], ring[n], tap(c),
                                     start=k == 0 and c == 2, stop=k == CONV_K - 1,
                                     skip_group_check=True)
                ring_free[(2 * k + 2) % 4] = ring_free[(2 * k + 3) % 4] = pe.mark(last)
                if k % 2 == 0:
                    modulation_slots(8 + k // 2, 1)
                yield

        taps = {}
        steps = convolution()

        def background(n):
            for _ in range(n):
                next(steps, None)

        kr = mean[0:QK, :]
        pe.wait(kv_ready, *bank_free[3])
        last = T_.matmul(pair(3)[0:QK, 0, :], cst[0:ROPE, C_SHIFT:C_SHIFT + QK], k_rope,
                         start=True, stop=True)
        dve.wait(pe.mark(last))
        dve.mark(V.tensor_scalar(kr, pair(3)[0:QK, 0, :], col("k_norm", 0)[0:QK], None, ALU.mult))
        pe.wait(q_ready, k_ready, consts_ready, *bank_free[4])
        for t in range(TT):
            for h in range(HEADS):
                c = t * HEADS + h
                last = T_.matmul(bank[4][:, c:c + 1], q_sq[0:QK, h, t * P:(t + 1) * P],
                                 ones[0:QK, 0:1], start=True, stop=True)
        q_sums = pe.mark(last)
        pe.wait(dve.last)
        last = T_.matmul(pair(3)[0:QK, 1, :], cst[0:QK, C_ROT:C_ROT + QK], kr, start=True,
                         stop=True)
        kr_turned = pe.mark(last)
        pe.wait(*bank_free[5])
        for t in range(TT):
            for h in range(HEADS):
                c = t * HEADS + h
                T_.matmul(bank[5][:, c:c + 1], k_sq[0:NOPE, h, t * P:(t + 1) * P],
                          ones[0:NOPE, 0:1], start=True, stop=False)
                last = T_.matmul(bank[5][:, c:c + 1], k_rope_sq[:, t * P:(t + 1) * P],
                                 ones[0:ROPE, 0:1], start=False, stop=True)
        k_sums = pe.mark(last)
        background(2)
        dve.wait(kr_turned, rope_ready, dve.last)
        dve.mark(V.tensor_tensor(tmp_a[0:QK, :], pair(3)[0:QK, 1, :], sinT[0:QK, :], ALU.mult))
        bank_free[3] = [dve.last]
        dve.mark(V.tensor_tensor(kr, kr, cosT[0:QK, :], ALU.mult))
        dve.wait(dve.last)
        dve.mark(V.tensor_tensor(kr, kr, tmp_a[0:QK, :], ALU.add))
        dve.wait(dve.last)
        kr_ready = dve.mark(V.tensor_copy(
            kT[NOPE:QK, :, :], stat[NOPE:QK, 4:5, :].to_broadcast([ROPE, HEADS, T])))
        roots_k = small[:, 72:88]
        dve.wait(q_sums)
        token_roots(bank[4][:, 0:2 * HEADS], QK, roots16)
        bank_free[4] = [dve.last]
        dve.wait(k_sums)
        token_roots(bank[5][:, 0:2 * HEADS], QK, roots_k)
        bank_free[5] = [dve.last]
        for j in range(HEADS // 2):
            dve.wait(dve.last, squares_free[0])
            for h in (2 * j, 2 * j + 1):
                for t in range(TT):
                    c = t * HEADS + h
                    dve.mark(V.tensor_scalar(squares[:, h, t * P:(t + 1) * P], ident,
                                             roots_k[:, c:c + 1], None, ALU.mult))
            b = (1, 2)[j % 2]
            pe.wait(dve.last, *bank_free[b])
            spread = pe.mark(T_.matmul(pair(b)[0:QK], ones[:, 0:QK],
                                       squares[:, 2 * j:2 * j + 2, :], start=True, stop=True))
            b2 = (3, 4)[j % 2]
            pe.wait(*bank_free[b2])
            qj = qT[0:QK, 2 * j:2 * j + 2, :]
            turned = pe.mark(T_.matmul(pair(b2)[0:QK], cst[0:QK, C_ROT:C_ROT + QK], qj,
                                       start=True, stop=True))
            pool.wait(turned, rope_ready)
            pool.mark(G.tensor_tensor(qj, qj, normed[0:QK, KD:KD + 1, :].to_broadcast(
                [QK, 2, T]), ALU.mult))
            background(1)
            dve.wait(spread, k_ready)
            kj = kT[0:QK, 2 * j:2 * j + 2, :]
            dve.mark(V.tensor_tensor(kj, kj, pair(b)[0:QK], ALU.mult))
            bank_free[b] = [dve.last]
            dve.wait(turned, q_sums)
            dve.mark(V.tensor_tensor(q_sq[0:QK, 2 * j:2 * j + 2, :], pair(b2)[0:QK],
                                     normed[0:QK, KD + 1:KD + 2, :].to_broadcast([QK, 2, T]),
                                     ALU.mult))
            bank_free[b2] = [dve.last]
            dve.wait(dve.last, pool.last)
            dve.mark(V.tensor_tensor(qj, qj, q_sq[0:QK, 2 * j:2 * j + 2, :], ALU.add))
        squares_free[0] = pe.last

        s1 = wide[:, 0:HEADS * T].rearrange("p (h t) -> p h t", h=HEADS)
        s0 = wide[:, HEADS * T:].rearrange("p (h t) -> p h t", h=HEADS)
        mask2 = cst[:, C_MASK:C_MASK + P].rearrange("p (o n) -> p o n", o=1).to_broadcast(
            [P, 2, P])
        top, negative, total = small[:, 48:56], small[:, 56:64], small[:, 64:72]
        scale = float(QK) ** -0.5
        dve.wait(dve.last)
        dve.mark(V.tensor_scalar(roots16, roots16, scale, None, ALU.mult))
        pe.wait(dve.last)
        for t, s in ((0, s0), (1, s1)):
            keys = (t + 1) * P
            for h in range(HEADS):
                b, c = 1 + h // 2, h % 2
                if c == 0:
                    pe.wait(*bank_free[b])
                last = T_.matmul(pair(b)[:, c, 0:keys], qT[0:QK, h, t * P:(t + 1) * P],
                                 kT[0:QK, h, 0:keys], start=True, stop=True)
                if c == 0:
                    continue
                dve.wait(pe.mark(last))
                dve.mark(V.tensor_tensor(s[:, h - 1:h + 1, keys - P:keys],
                                         pair(b)[:, :, keys - P:keys], mask2, ALU.add))
                if t:
                    dve.mark(V.tensor_copy(s[:, h - 1:h + 1, 0:P], pair(b)[:, :, 0:P]))
                bank_free[b] = [dve.last]
            dve.wait(dve.last, act.last)
            dve.mark(V.tensor_reduce(top, s, AX, ALU.max))
            dve.wait(dve.last)
            dve.mark(V.tensor_tensor(negative, top, roots16[:, t * HEADS:(t + 1) * HEADS],
                                     ALU.mult))
            dve.wait(dve.last)
            dve.mark(V.tensor_scalar(negative, negative, -1.0, None, ALU.mult))
            act.wait(dve.last)
            for h in range(HEADS):
                act.mark(S.activation(s[:, h, :], s[:, h, :], ACT.Exp, bias=negative[:, h:h + 1],
                                      scale=roots16[:, t * HEADS + h:t * HEADS + h + 1],
                                      accum_out=total[:, h:h + 1]))
            background(4)
            dve.wait(act.last)
            dve.mark(V.reciprocal(total, total))
            dve.wait(dve.last)
            for h in range(HEADS):
                dve.mark(V.tensor_scalar(s[:, h, :], s[:, h, :], total[:, h:h + 1], None,
                                         ALU.mult))
            pe.wait(dve.last)
            for kt in range(t + 1):
                block = 0 if t == 0 else 1 + kt
                for half in range(2):
                    b = 1 + (2 * kt + half) % 4
                    pe.wait(*bank_free[b])
                    for h in range(4 * half, 4 * half + 4):
                        last = T_.transpose(bank[b][:, (h % 4) * P:(h % 4 + 1) * P],
                                            s[:, h, kt * P:(kt + 1) * P], ident)
                    act.wait(pe.mark(last), kr_ready)
                    at0 = (block * HEADS + 4 * half) * P
                    act.mark(S.activation(p_t[:, at0:at0 + 4 * P], bank[b][:, :], ACT.Copy))
                    bank_free[b] = [act.last]
            background(3)
        pt = p_t.rearrange("p (b h t) -> p b h t", b=3, h=HEADS)

        pe.wait(act.last, v_ready)
        y_points = [None] * KD
        for pair_h in range(HEADS // 2):
            b = 1 + pair_h
            pe.wait(*bank_free[b])
            for c in range(2):
                h = 2 * pair_h + c
                dst = pair(b)[c * VD:(c + 1) * VD, 0, :]
                v0, v1 = (v_tok[:, t, h * VD:(h + 1) * VD] for t in range(TT))
                T_.matmul(dst[:, 0:P], v0, pt[:, 0, h, :], start=True, stop=True,
                          skip_group_check=True)
                T_.matmul(dst[:, P:T], v0, pt[:, 1, h, :], start=False, stop=False,
                          skip_group_check=True)
                last = T_.matmul(dst[:, P:T], v1, pt[:, 2, h, :], start=False, stop=True,
                                 skip_group_check=True)
            dve.wait(pe.mark(last), dve.last)
            done = dve.mark(V.tensor_copy(normed[:, KC + pair_h, :], pair(b)[:, 0, :]))
            bank_free[b] = [done]
            y_points[KC + pair_h] = split_operand(KC + pair_h, normed[:, KC + pair_h, :], [done])
            background(1)
        background(CONV_K)
        modulation_end(8, 16)

        dve.wait(pe.last)
        for c in (2, 3):
            dve.mark(V.tensor_scalar(conv[:, c, :], pair(0)[:, c - 2, :], col("conv_b", c), None,
                                     ALU.add))
        bank_free[0] = [dve.last]
        pe.wait(dve.last, *bank_free[5])
        for c in range(KC):
            last = T_.matmul(pair(5)[:, 0, :], ones[:, :], conv[:, c, :], start=c == 0,
                             stop=c == KC - 1)
        dve.wait(pe.mark(last), dve.last)
        dve.mark(V.tensor_scalar(mean, pair(5)[:, 0, :], 1.0 / CONV_CH, None, ALU.mult))
        bank_free[5] = [dve.last]
        act.wait(pe.last)
        for c in range(KC):
            dve.wait(dve.last)
            dve.mark(V.tensor_tensor(conv[:, c, :], conv[:, c, :], mean, ALU.subtract))
            square(conv, c, dve.last)
        sum_squares(KC, 6)
        for c in range(KC):
            dve.wait(dve.last)
            dve.mark(V.scalar_tensor_tensor(conv[:, c, :], conv[:, c, :], col("conv_ln_g", c),
                                            rstd, ALU.mult, ALU.mult))
            dve.wait(dve.last)
            dve.mark(V.tensor_scalar(conv[:, c, :], conv[:, c, :], col("conv_ln_b", c), None,
                                     ALU.add))
            act.wait(dve.last)
            done = act.mark(S.activation(conv[:, c, :], conv[:, c, :], ACT.Silu))
            y_points[c] = split_operand(c, conv[:, c, :], [done])

        x_points = []
        for j in range(4):
            done = column_product(1 + j, y_points if j == 0 else None)
            dve.wait(done)
            for c in range(2):
                m = 2 * j + c
                x_points.append(dve.mark(V.scalar_tensor_tensor(
                    xT[:, m, :], pair(1 + j)[:, c, :], mod[:, 2 * KD + m:2 * KD + m + 1],
                    xT[:, m, :], ALU.mult, ALU.add)))
            bank_free[1 + j] = [dve.last]
        operand_free[0] = pe.last

        scaled_gain(1, "norm_ffn", 4 * KD)
        h_points = rms_norm(lambda k: gmod[:, 1, k:k + 1], x_points,
                            lambda k: mod[:, 3 * KD + k:3 * KD + k + 1])
        at[0] = 0
        gate_all = scratch(EXPERTS * T).rearrange("p (e t) -> p e t", e=EXPERTS)
        gates_t = scratch(T)
        r_at = at[0]
        NR = GROUPS + EXPERTS
        pe.wait(dve.last, (s_route, 32), *bank_free[1])
        for t in range(TT):
            dst = bank[1][:, t * 64:t * 64 + NR]
            for k in range(KD):
                T_.matmul(dst, normed[:, k, t * P:(t + 1) * P], w_route[:, k, :], start=k == 0,
                          stop=False)
            last = T_.matmul(dst, ones[0:1, 0:P], bias_row, start=False, stop=True)
        dve.wait(pe.mark(last))
        desc = cst[:, C_DESC:C_DESC + EXPERTS]

        def one_hot_of_top(dst, values, n, scr, best):
            dve.wait(dve.last)
            dve.mark(V.tensor_reduce(best, values, AX, ALU.max))
            dve.wait(dve.last)
            dve.mark(V.tensor_scalar(scr, values, best, None, ALU.is_equal))
            dve.wait(dve.last)
            dve.mark(V.tensor_tensor(scr, scr, desc[:, EXPERTS - n:], ALU.mult))
            dve.wait(dve.last)
            dve.mark(V.tensor_reduce(dst[:, 0:1], scr, AX, ALU.max))
            dve.wait(dve.last)
            dve.mark(V.tensor_scalar(scr, desc[:, EXPERTS - n:], dst[:, 0:1], None,
                                     ALU.is_equal))
            dve.wait(dve.last)
            dve.mark(V.tensor_copy(dst, scr))
            dve.wait(dve.last)

        for t in range(TT):
            lg, le, hot_g, hot1, hot2, scr, pr = (
                scratch(n) for n in (GROUPS, EXPERTS, GROUPS, EXPERTS, EXPERTS, EXPERTS, EXPERTS))
            best, neg, s_g, p2, den = (scratch(1) for _ in range(5))
            dve.wait(act.last, pe.last)
            dve.mark(V.tensor_copy(lg, bank[1][:, t * 64:t * 64 + GROUPS]))
            dve.mark(V.tensor_copy(le, bank[1][:, t * 64 + GROUPS:t * 64 + NR]))
            one_hot_of_top(hot_g, lg, GROUPS, scr[:, 0:GROUPS], best)
            dve.mark(V.tensor_scalar(neg, best, -1.0, None, ALU.mult))
            act.wait(dve.last)
            act.mark(S.activation(scr[:, 0:GROUPS], lg, ACT.Exp, bias=neg, accum_out=s_g))
            dve.wait(act.last)
            dve.mark(V.tensor_scalar(hot_g, hot_g, -1.0, 1e30, ALU.add, ALU.mult))
            dve.wait(dve.last)
            for g in range(GROUPS):
                dve.mark(V.tensor_scalar(le[:, g * PER_GROUP:(g + 1) * PER_GROUP],
                                         le[:, g * PER_GROUP:(g + 1) * PER_GROUP],
                                         hot_g[:, g:g + 1], None, ALU.add))
            dve.wait(dve.last)
            dve.mark(V.tensor_reduce(best, le, AX, ALU.max))
            dve.wait(dve.last)
            dve.mark(V.tensor_scalar(neg, best, -1.0, None, ALU.mult))
            act.wait(dve.last)
            act.mark(S.activation(pr, le, ACT.Exp, bias=neg))
            dve.wait(act.last)
            one_hot_of_top(hot1, pr, EXPERTS, scr, best)
            dve.mark(V.scalar_tensor_tensor(pr, hot1, -2.0, pr, ALU.mult, ALU.add))
            one_hot_of_top(hot2, pr, EXPERTS, scr, p2)
            dve.mark(V.tensor_tensor(den, best, p2, ALU.add))
            dve.mark(V.tensor_scalar(hot1, hot1, best, None, ALU.mult))
            dve.wait(dve.last)
            dve.mark(V.tensor_tensor(den, den, s_g, ALU.mult))
            dve.mark(V.scalar_tensor_tensor(hot1, hot2, p2, hot1, ALU.mult, ALU.add))
            dve.wait(dve.last)
            dve.mark(V.reciprocal(den, den))
            dve.wait(dve.last)
            dve.mark(V.tensor_scalar(hot1, hot1, den, None, ALU.mult))
            pe.wait(dve.last, *bank_free[2])
            last = T_.transpose(bank[2][0:EXPERTS, t * P:(t + 1) * P], hot1, ident)
            pe.mark(last)
        bank_free[1] = [dve.last]
        dve.wait(pe.last)
        dve.mark(V.tensor_copy(gates_t[0:EXPERTS, :], bank[2][0:EXPERTS, 0:T]))
        bank_free[2] = [dve.last]
        gates_ready = dve.last

        def finish_routing():
            pe.wait(gates_ready)
            spread_gates()

        def spread_gates():
            for j in range(EXPERTS // 2):
                b = 4 + j % 4
                pe.wait(*bank_free[b])
                for c in range(2):
                    e = 2 * j + c
                    last = T_.matmul(pair(b)[:, c, :],
                                     cst[0:EXPERTS, C_IDENT + e:C_IDENT + e + 1].to_broadcast(
                                         [EXPERTS, P]),
                                     gates_t[0:EXPERTS, :], start=True, stop=True)
                pe.mark(last)
                lane, eng = (act, S) if j % 2 else (dve, V)
                lane.wait(pe.last)
                dst = gate_all[:, 2 * j:2 * j + 2, :]
                if j % 2:
                    act.mark(S.activation(dst, pair(b), ACT.Copy))
                else:
                    dve.mark(V.tensor_copy(dst, pair(b)))
                bank_free[b] = [lane.last]
            dve.wait(act.last)

        done = gated_units(EXPERTS, h_points, False, finish_routing, gate_all)
        x_points = add_banks(lambda m: mod[:, 5 * KD + m:5 * KD + m + 1], done)

        BAND = 3 * P
        at[0] = 0
        s_band = sem("s_band")
        bands = []
        gates_free = (dve.last, pe.last, act.last)

        bands_ready = []

        def load_bands():
            n_band = 0
            pool.wait(*gates_free)
            for name in ("lru_w_a_2", "lru_w_x_2"):
                band = scratch(KR * BAND).rearrange("p (c n) -> p c n", c=KR)
                bands.append(band)
                pool.mark(G.memset(band, 0.0))
                pool.wait(pool.last)
                for h in range(LRU_HEADS):
                    r = h * LRU_DIM
                    while r < (h + 1) * LRU_DIM:
                        c = r // P
                        end = min((h + 1) * LRU_DIM, (c + 1) * P)
                        c0 = h * LRU_DIM - (c - 1) * P
                        G.dma_start(band[r - c * P:end - c * P, c, c0:c0 + LRU_DIM],
                                    a[name][h, r - h * LRU_DIM:end - h * LRU_DIM, :]
                                    ).then_inc(s_band, 16)
                        n_band += 16
                        r = end
            return s_band, n_band

        def ffn(which, layer, x_points, then=None, before_last=None):
            h = scaled(lambda k: col(f"{which}_norm_2", layer * KD + k), x_points)
            if then:
                then()
            return add_banks(0.5, gated_units(D_FF // CW, h, True,
                                              before_last=before_last))

        s_p = sem("s_p")

        p_tok = arena[:, 0:TT * 256].rearrange("p (t d) -> p t d", t=TT)
        pT = arena[:, TT * 256:TT * 256 + 2 * T].rearrange("p (k t) -> p k t", k=2)
        p_points = []

        def load_p(layer):
            pool.wait(dve.last, act.last, pe.last)
            G.dma_start(p_tok, a["p_2"][layer].rearrange("(t p) d -> p t d", p=P)
                        ).then_inc(s_p, 16)

        def turn_p(layer):
            pe.wait((s_p, 16 * (layer + 1)), *bank_free[2])
            for k in range(2):
                for t in range(TT):
                    last = T_.transpose(pair(2)[:, k, t * P:(t + 1) * P],
                                        p_tok[:, t, k * P:(k + 1) * P], ident)
            dve.wait(pe.mark(last), act.last)
            done = dve.mark(V.tensor_copy(pT, pair(2)))
            bank_free[2] = [done]
            p_points[:] = [split_operand(KD + k, pT[:, k, :], [done]) for k in range(2)]

        def per_layer_embedding(layer, x_points):
            sg = arena[:, 1024:1024 + D * TT].rearrange("p (m t) -> p m t", m=KD)
            proj = row_product([a_hi[:, KD, :], a_hi[:, KD + 1, :]],
                               [a_lo[:, KD, :], a_lo[:, KD + 1, :]], True, True, p_points)
            h = scaled(lambda k: col("ple_norm_2", layer * KD + k), x_points)
            points = []
            for j in range(4):
                if j == 0:
                    done = two_column_products(0, 1, h)
                    diagonals = sum_squares_start(KD, 3)
                    done2 = column_product(2, None)
                    sum_squares_end(3, diagonals)
                elif j > 1:
                    done = column_product(3, None) if j == 3 else done2
                g = sg[:, 2 * j:2 * j + 2, :]
                dve.wait(done, dve.last, act.last)
                dve.mark(V.tensor_tensor(g, pair(j), rstd2, ALU.mult))
                bank_free[j] = [dve.last]
                act.wait(dve.last)
                act.mark(S.activation(g, g, ACT.Sigmoid))
                dve.wait(act.last, *proj)
                dve.mark(V.tensor_tensor(g, g, pair(4 + j), ALU.mult))
                bank_free[4 + j] = [dve.last]
                dve.wait(dve.last)
                for c in range(2):
                    points.append(dve.mark(V.tensor_tensor(
                        xT[:, 2 * j + c, :], xT[:, 2 * j + c, :], sg[:, 2 * j + c, :], ALU.add)))
            operand_free[0] = pe.last
            return points

        def lru(x_points):
            base = at[0]
            h = scaled(lambda k: col("mix_norm_2", k), x_points)
            nn, an, _ = vec_at["lru_a_param_2"]
            v, e, z, z2, log_rate = (small[:, 40 + i * KR:40 + (i + 1) * KR] for i in range(5))
            dve.wait(act.last)
            dve.mark(V.tensor_scalar(v, vec[:, nn, an:an + KR], -1.0, None, ALU.mult))
            dve.wait(dve.last)
            dve.mark(V.tensor_tensor(e, v, vec[:, nn, an:an + KR], ALU.max))
            act.wait(dve.last)
            act.mark(S.activation(e, e, ACT.Exp, scale=-1.0))
            dve.wait(act.last)
            dve.mark(V.tensor_scalar(z, e, 2.0, None, ALU.add))
            dve.wait(dve.last)
            dve.mark(V.reciprocal(z, z))
            dve.wait(dve.last)
            dve.mark(V.tensor_tensor(z, z, e, ALU.mult))
            dve.wait(dve.last)
            dve.mark(V.tensor_tensor(z2, z, z, ALU.mult))
            dve.wait(dve.last)
            dve.mark(V.tensor_scalar(log_rate, z2, 1.0 / 17, 1.0 / 15, ALU.mult, ALU.add))
            for n in (13, 11, 9, 7, 5, 3, 1):
                dve.wait(dve.last)
                dve.mark(V.tensor_tensor(log_rate, log_rate, z2, ALU.mult))
                dve.wait(dve.last)
                dve.mark(V.tensor_scalar(log_rate, log_rate, 1.0 / n, None, ALU.add))
            dve.wait(dve.last)
            dve.mark(V.tensor_tensor(log_rate, log_rate, z, ALU.mult))
            dve.wait(dve.last)
            dve.mark(V.tensor_scalar(v, v, 0.0, None, ALU.max))
            dve.wait(dve.last)
            dve.mark(V.scalar_tensor_tensor(log_rate, log_rate, 2.0, v, ALU.mult, ALU.add))
            dve.wait(dve.last)
            dve.mark(V.tensor_scalar(log_rate, log_rate, -LRU_C, None, ALU.mult))
            xb = normed
            gelu = scratch(KR * T).rearrange("p (c t) -> p c t", c=KR)
            xc = scratch(KR * T).rearrange("p (c t) -> p c t", c=KR)

            def evacuate(b, dst, done):
                dve.wait(done, dve.last, act.last)
                dve.mark(V.tensor_tensor(dst, pair(b), rstd2, ALU.mult))
                bank_free[b] = [dve.last]

            def convolve(c):
                dve.wait(dve.last)
                dve.mark(V.tensor_scalar(xc[:, c, :], xb[:, c, :], col("lru_conv_w_2", 3 * KR + c),
                                         col("lru_conv_b_2", c), ALU.mult, ALU.add))
                for k in range(3):
                    shift = 3 - k
                    dve.wait(dve.last)
                    dve.mark(V.scalar_tensor_tensor(
                        xc[:, c, shift:], xb[:, c, 0:T - shift], col("lru_conv_w_2", k * KR + c),
                        xc[:, c, shift:], ALU.mult, ALU.add))

            done01 = two_column_products(0, 1, h)
            diagonals = sum_squares_start(KD, 3)
            done2 = column_product(2, None)
            sum_squares_end(3, diagonals)
            evacuate(0, xb[:, 0:2, :], done01)
            evacuate(1, xb[:, 2:4, :], done01)
            evacuate(2, xb[:, 4:6, :], done2)
            for j in (3, 4):
                evacuate(j % 4, xb[:, 2 * j:2 * j + 2, :], column_product(j % 4, None))
                convolve(2 * j - 6)
                convolve(2 * j - 5)
            for j in range(KR // 2):
                b = (1 + j) % 4
                evacuate(b, gelu[:, 2 * j:2 * j + 2, :], column_product(b, None))
                for c in ((4, 5), (6, 7), (8, 9), (), ())[j]:
                    convolve(c)
            operand_free[0] = pe.last

            def gelu_chunks(c0, c1):
                g, w = gelu[:, c0:c1, :], xb[:, c0:c1, :]
                dve.wait(act.last, dve.last)
                dve.mark(V.tensor_tensor(w, g, g, ALU.mult))
                dve.wait(dve.last)
                dve.mark(V.tensor_scalar(w, w, 0.044715, 1.0, ALU.mult, ALU.add))
                dve.wait(dve.last)
                dve.mark(V.tensor_tensor(w, w, g, ALU.mult))
                act.wait(dve.last)
                act.mark(S.activation(w, w, ACT.Tanh, scale=0.7978845608028654))
                dve.wait(act.last)
                dve.mark(V.tensor_scalar(w, w, 1.0, 0.5, ALU.add, ALU.mult))
                dve.wait(dve.last)
                dve.mark(V.tensor_tensor(g, g, w, ALU.mult))

            HALF = KR // 2
            pe.wait(dve.last, *bands_ready)

            def gate_products(half):
                c0 = half * HALF
                for c in range(c0, c0 + HALF):
                    source = [i for i in (c - 1, c, c + 1) if c0 <= i < c0 + HALF]
                    b = c - c0 + (0, 3)[half]
                    pe.wait(*bank_free[b])
                    for n in range(2):
                        for i in source:
                            last = T_.matmul(pair(b)[:, n, :],
                                             bands[n][:, i, (c - i + 1) * P:(c - i + 2) * P],
                                             xc[:, i, :], start=i == source[0],
                                             stop=i == source[-1])
                    gate_done.append(pe.mark(last))

            def scan_half(half):
                c0 = half * HALF
                chunks = range(c0, c0 + HALF)
                bk = [pair(c - c0 + (0, 3)[half]) for c in chunks]
                log_a = xb[:, c0:c0 + HALF, :]
                xh = xc[:, c0:c0 + HALF, :]
                act.wait(dve.last, gate_done[c0 + HALF - 1])
                for c in chunks:
                    for n, bias in ((0, "lru_b_a_2"), (1, "lru_b_x_2")):
                        act.mark(S.activation(bk[c - c0][:, n, :], bk[c - c0][:, n, :],
                                              ACT.Sigmoid, bias=col(bias, c)))
                    dve.wait(act.last)
                    dve.mark(V.tensor_scalar(xb[:, c, :], bk[c - c0][:, 0, :], log_rate[:, c:c + 1],
                                             None, ALU.mult))
                    dve.mark(V.tensor_tensor(xc[:, c, :], xc[:, c, :], bk[c - c0][:, 1, :],
                                             ALU.mult))
                for c in chunks:
                    act.wait(dve.last)
                    act.mark(S.activation(bk[c - c0][:, 0, :], xb[:, c, :], ACT.Exp))
                    act.mark(S.activation(bk[c - c0][:, 1, :], xb[:, c, :], ACT.Tanh,
                                          scale=-1.0))
                    dve.wait(act.last)
                    dve.mark(V.tensor_copy(xb[:, c, :], bk[c - c0][:, 0, :]))
                    dve.wait(dve.last)
                    dve.mark(V.tensor_tensor(xb[:, c, :], xb[:, c, :], xb[:, c, :], ALU.mult))
                    dve.wait(dve.last)
                    dve.mark(V.scalar_tensor_tensor(xb[:, c, :], xb[:, c, :], 1.0,
                                                    bk[c - c0][:, 1, :], ALU.add, ALU.mult))
                act.wait(dve.last)
                act.mark(S.activation(log_a, log_a, ACT.Sqrt))
                dve.wait(act.last)
                dve.mark(V.tensor_tensor(xh, xh, log_a, ALU.mult))
                dve.wait(dve.last)
                for c in chunks:
                    dve.wait(dve.last)
                    dve.mark(V.tensor_tensor_scan(xb[:, c, :], bk[c - c0][:, 0, :], xc[:, c, :],
                                                  0.0, ALU.mult, ALU.add))
                    bank_free[c - c0 + (0, 3)[half]] = [dve.last]
                    dve.wait(dve.last)
                    done = dve.mark(V.tensor_tensor(gelu[:, c, :], gelu[:, c, :], xb[:, c, :],
                                                    ALU.mult))
                    y_points.append(split_operand(c, gelu[:, c, :], [done]))

            y_points, gate_done = [], []
            gate_products(0)
            gelu_chunks(0, HALF)
            scan_half(0)
            gate_products(1)
            gelu_chunks(HALF, KR)
            scan_half(1)
            for j in range(KR // 2):
                done = row_product([a_hi[:, 2 * j + c, :] for c in range(2)],
                                   [a_lo[:, 2 * j + c, :] for c in range(2)],
                                   j == 0, j == KR // 2 - 1, y_points[2 * j:2 * j + 2])
            operand_free[0] = pe.last
            return add_banks(1.0, done)

        def pooling(x_points):
            rms_norm(lambda k: col("mix_norm_2", KD + k), x_points)
            padded = arena[:, 0:3 * 2 * TW].rearrange("p (b c t) -> p b c t", b=3, c=2)
            pool.wait(dve.last, act.last, pe.last)
            pool.mark(G.memset(padded[:, :, :, 0:PAD], 0.0))
            points = []
            for g, win in enumerate(WINDOWS):
                x, s, s_next = padded[:, 0], padded[:, 1], padded[:, 2]
                dve.wait(pool.last, dve.last, act.last)
                dve.mark(V.tensor_copy(x[:, :, PAD:], normed[:, 2 * g:2 * g + 2, :]))
                src, step = x, 1
                while step < win:
                    dst = s if src is not s else s_next
                    dve.wait(dve.last)
                    dve.mark(V.tensor_tensor(dst[:, :, PAD:], src[:, :, PAD:],
                                             src[:, :, PAD - step:TW - step], ALU.add))
                    src, step = dst, 2 * step
                first = cst[:, C_COUNT + 16 * g:C_COUNT + 16 * g + 16]
                dve.wait(dve.last)
                for c in range(2):
                    dve.mark(V.tensor_tensor(src[:, c, PAD:PAD + 16], src[:, c, PAD:PAD + 16],
                                             first, ALU.mult))
                dve.mark(V.tensor_scalar(src[:, :, PAD + 16:], src[:, :, PAD + 16:], 1.0 / win,
                                         None, ALU.mult))
                dve.wait(dve.last)
                for c in range(2):
                    done = dve.mark(V.tensor_tensor(normed[:, 2 * g + c, :], src[:, c, PAD:],
                                                    x[:, c, PAD:], ALU.subtract))
                for c in range(2):
                    points.append(split_operand(2 * g + c, normed[:, 2 * g + c, :], [done]))
            i = take()
            wh, wl = weights(i)
            out_points = []
            for g in range(len(WINDOWS)):
                pe.wait(*bank_free[g])
                for m in range(2):
                    for k in range(2):
                        j = 2 * g + k
                        pe.wait(points[j])
                        last = product3(pair(g)[:, m, :],
                                        (wh[:, j, m * P:(m + 1) * P], wl[:, j, m * P:(m + 1) * P]),
                                        (a_hi[:, j, :], a_lo[:, j, :]), k == 0, k == 1)
                dve.wait(pe.mark(last), dve.last)
                for m in range(2):
                    c = 2 * g + m
                    dve.mark(V.tensor_scalar(tmp_a, pair(g)[:, m, :], col("pool_b_2", c),
                                             col("pool_scale_2", c), ALU.add, ALU.mult))
                    dve.wait(dve.last)
                    out_points.append(dve.mark(V.tensor_tensor(xT[:, c, :], xT[:, c, :], tmp_a,
                                                               ALU.add)))
                    dve.wait(dve.last)
                bank_free[g] = [dve.last]
            give_back(i, pe.last)
            operand_free[0] = pe.last
            return out_points

        x_points = ffn("ffn1", 0, x_points, lambda: bands_ready.append(load_bands()))
        x_points = lru(x_points)
        x_points = ffn("ffn2", 0, x_points, lambda: load_p(0), lambda: turn_p(0))
        x_points = per_layer_embedding(0, x_points)
        x_points = ffn("ffn1", 1, x_points)
        x_points = pooling(x_points)
        x_points = ffn("ffn2", 1, x_points, lambda: load_p(1), lambda: turn_p(1))
        x_points = per_layer_embedding(1, x_points)

        rms_statistics(xT, KD, 0, x_points)
        y_tok = arena[:, 0:TT * D].rearrange("p (t d) -> p t d", t=TT)
        s_out = sem("s_out")
        for k in range(KD):
            dve.wait(dve.last)
            dve.mark(V.scalar_tensor_tensor(normed[:, k, :], xT[:, k, :], col("final_norm_2", k),
                                            rstd, ALU.mult, ALU.mult))
        pe.wait(dve.last)
        for t in range(TT):
            for half in range(2):
                b = 1 + 2 * t + half
                pe.wait(*bank_free[b])
                for k in range(4):
                    last = T_.transpose(bank[b][:, k * P:(k + 1) * P],
                                        normed[:, 4 * half + k, t * P:(t + 1) * P], ident)
                act.wait(pe.mark(last), dve.last)
                act.mark(S.activation(y_tok[:, t, half * 512:(half + 1) * 512], bank[b][:, :],
                                      ACT.Copy))
            sp.wait(act.last)
            L.dma_start(out[t * P:(t + 1) * P, :], y_tok[:, t, :]).then_inc(s_out, 16)
        L.wait_ge(s_out, 16 * TT)
        assert n_taken == len(entries)


def two_pi_parts():
    import math
    rest, parts = 2 * math.pi, []
    for bits in (8, 8, 8):
        exponent = math.floor(math.log2(rest)) + 1
        unit = 2.0 ** (exponent - bits)
        part = math.floor(rest / unit) * unit
        parts.append(part)
        rest -= part
    return parts + [rest]


def constants():
    import numpy as np
    c = np.zeros((P, C_END), np.float32)
    c[:, C_IDENT:C_IDENT + P] = np.eye(P, dtype=np.float32)
    half = ROPE // 2
    for j in range(half):
        c[NOPE + half + j, C_ROT + NOPE + j] = -1.0
        c[NOPE + j, C_ROT + NOPE + half + j] = 1.0
    c[0:CHUNK, C_MASK + CHUNK:C_MASK + P] = -1e30
    freq = 10000.0 ** (-np.arange(0, ROPE, 2) / ROPE)
    c[NOPE:NOPE + half, C_FREQ] = freq
    c[NOPE + half:QK, C_FREQ] = freq
    for g, win in enumerate(WINDOWS):
        for t in range(16):
            c[:, C_COUNT + 16 * g + t] = 1.0 / min(t + 1, win)
    c[:, C_DESC:C_DESC + EXPERTS] = np.arange(EXPERTS, 0, -1)
    c[0:ROPE, C_SHIFT + NOPE:C_SHIFT + QK] = np.eye(ROPE)
    return c


NAMES = ["x", "positions", "w_ada", "w_in", "w_q_b", "w_kv_b", "w_out", "w_gate_e", "w_up_e",
         "w_down_e", "p_2", "ffn1_w_gate_2", "ffn1_w_up_2", "ffn1_w_down_2", "lru_w_in_2",
         "lru_w_a_2", "lru_w_x_2", "lru_w_out_2", "pool_w_2", "ffn2_w_gate_2", "ffn2_w_up_2",
         "ffn2_w_down_2", "ple_w_gate_2", "ple_w_proj_2"]
KEEP_LEADING = {"positions", "p_2", "ffn1_w_gate_2", "ffn1_w_up_2", "ffn1_w_down_2",
                "ffn2_w_gate_2", "ffn2_w_up_2", "ffn2_w_down_2", "ple_w_gate_2", "ple_w_proj_2"}


def kernel(**inputs):
    import numpy as np
    import concourse.bacc as bacc
    from concourse.bass_utils import run_bass_kernel_spmd

    nc = bacc.Bacc("TRN2", target_bir_lowering=False, num_devices=1)
    arrays, aps = {}, {}
    for name in NAMES:
        array = np.ascontiguousarray(inputs[name])
        if name not in KEEP_LEADING:
            array = array.reshape(array.shape[1:])
        if name == "p_2":
            array = array.reshape(2, T, 256)
        arrays["in_" + name] = array
        aps[name] = nc.dram_tensor("in_" + name, array.shape, mybir.dt.from_np(array.dtype),
                                   kind="ExternalInput").ap()
    vectors = np.zeros((P, 4, P), np.float32)
    for n, group in enumerate((VEC_A, VEC_B, VEC_C, VEC_D)):
        at = 0
        for name, count in group:
            flat = np.ravel(inputs[name])
            rows = vectors[at:at + count, n, :]
            if flat.size == rows.size:
                rows[...] = flat.reshape(count, P)
            else:
                rows[0, :flat.size] = flat
            at += count
    packed = {"vectors": vectors,
              "w_route": np.concatenate([inputs["w_group"][0], inputs["w_expert"][0]], axis=1),
              "b_route": np.concatenate([inputs["b_group"], inputs["b_expert"]], axis=1)}
    for name, array in packed.items():
        arrays["in_" + name] = np.ascontiguousarray(array)
        aps[name] = nc.dram_tensor("in_" + name, array.shape, F32, kind="ExternalInput").ap()
    arrays["in_constants"] = constants()
    consts = nc.dram_tensor("in_constants", (P, C_END), F32, kind="ExternalInput").ap()
    out = nc.dram_tensor("out", (T, D), F32, kind="ExternalOutput").ap()
    build(nc, aps, consts, out)
    result = run_bass_kernel_spmd(nc, [arrays], core_ids=[0])
    return result.results[0]["out"].reshape(1, T, D)
```

```python
from contextlib import ExitStack

import concourse.bass as bass
from concourse import mybir

F32 = mybir.dt.float32
F32R = mybir.dt.float32r
I32 = mybir.dt.int32
ALU = mybir.AluOpType
ACT = mybir.ActivationFunctionType
AX = mybir.AxisListType.X

P = 128
T = 256
TT = T // P
D = 1024
KD = D // P
SLOT = 2048
CW = SLOT // KD
RW = SLOT // D
N_RAW = 4
N_SPLIT = 4
AHEAD = N_SPLIT - 1
EPS = 1e-6
ARENA = 12832

CONV_CH, CONV_K = 512, 31
KC = CONV_CH // P
HEADS, NOPE, ROPE, VD = 8, 64, 32, 64
QK = NOPE + ROPE
GROUPS, PER_GROUP = 4, 8
EXPERTS = GROUPS * PER_GROUP
CHUNK = 64
D_FF = 2816
D_RNN = 1280
KR = D_RNN // P
LRU_HEADS, LRU_DIM = 16, 80
LRU_C = 8.0
WINDOWS = (2, 4, 8, 16)
PAD = 32
TW = PAD + T

C_IDENT = 0
C_ROT = C_IDENT + P
C_MASK = C_ROT + QK
C_FREQ = C_MASK + P
C_COUNT = C_FREQ + 1
C_DESC = C_COUNT + len(WINDOWS) * 16
C_SHIFT = C_DESC + EXPERTS
C_END = C_SHIFT + QK

VEC_A = [("b_ada", 48), ("norm_mix", 8), ("norm_ffn", 8), ("c", 8), ("conv_b", 4),
         ("conv_ln_g", 4), ("conv_ln_b", 4), ("q_a_norm", 2), ("kv_a_norm", 1)]
VEC_B = [("ffn1_norm_2", 16), ("mix_norm_2", 16), ("ffn2_norm_2", 16), ("ple_norm_2", 16),
         ("final_norm_2", 8), ("pool_b_2", 8), ("pool_scale_2", 8),
         ("q_norm", 1), ("k_norm", 1)]
VEC_C = [("conv_w", CONV_K * KC)]
VEC_D = [("lru_conv_w_2", 4 * KR), ("lru_conv_b_2", KR), ("lru_b_a_2", KR), ("lru_b_x_2", KR),
         ("lru_a_param_2", KR)]


class Lane:

    def __init__(self, engine, semaphore):
        self.engine, self.semaphore, self.count, self.seen = engine, semaphore, 0, {}

    def mark(self, instruction):
        instruction.then_inc(self.semaphore, 1)
        self.count += 1
        return self.semaphore, self.count

    @property
    def last(self):
        return self.semaphore, self.count

    def wait(self, *points):
        for semaphore, value in points:
            if value > self.seen.get(id(semaphore), 0):
                self.engine.wait_ge(semaphore, value)
                self.seen[id(semaphore)] = value


def build(nc, a, consts, out):
    ctx = ExitStack()
    with ctx:
        def sb(name, shape, dt=F32):
            return ctx.enter_context(nc.sbuf_tensor(name, shape, dt))

        def sem(name):
            return ctx.enter_context(nc.semaphore(name))

        pe, act = Lane(nc.tensor, sem("pe")), Lane(nc.scalar, sem("act"))
        dve, pool = Lane(nc.vector, sem("dve")), Lane(nc.gpsimd, sem("pool"))
        sp = Lane(nc.sync, sem("sp"))
        T_, V, S, G, L = nc.tensor, nc.vector, nc.scalar, nc.gpsimd, nc.sync

        bank = [ctx.enter_context(nc.psum_tensor(f"bank{b}", [P, 512], F32)) for b in range(8)]
        bank_free = [[] for _ in range(8)]

        def pair(b):
            return bank[b][:, :].rearrange("p (c t) -> p c t", c=2)

        raw = [sb(f"raw{i}", [P, SLOT]) for i in range(N_RAW)]
        w_hi = [sb(f"w_hi{i}", [P, SLOT], F32R) for i in range(N_SPLIT)]
        w_lo = [sb(f"w_lo{i}", [P, SLOT], F32R) for i in range(N_SPLIT)]
        xT = sb("xT", [P, KD, T])
        normed = sb("normed", [P, KR, T])
        a_hi = sb("a_hi", [P, KR, T], F32R)
        a_lo = sb("a_lo", [P, KR, T], F32R)
        hid = sb("hid", [P, 2, 2 * T])
        h_hi = sb("h_hi", [P, 2, 2 * T], F32R)
        h_lo = sb("h_lo", [P, 2, 2 * T], F32R)
        stat = sb("stat", [P, 5, T])
        cst = sb("cst", [P, C_END])
        ones = sb("ones", [P, P])
        vec = sb("vec", [P, 4, P])
        mod = sb("mod", [P, 48])
        gmod = sb("gmod", [P, 2, KD])
        small = sb("small", [P, 96])
        arena = sb("arena", [P, ARENA])
        rows = arena[:, TT * D:TT * D + 4 * P].rearrange("p (n c) -> p n c", n=4)

        cols = vec[:, 3, 80:128]
        roots2, roots16 = vec[:, 0, 88:90], vec[:, 0, 90:106]
        ident = cst[:, C_IDENT:C_IDENT + P]
        rstd, var, tmp_a, tmp_b, mean = (stat[:, i, :] for i in range(5))
        rstd2 = stat[:, 0:1, :].to_broadcast([P, 2, T])
        squares = arena[:, ARENA - KD * T:].rearrange("p (c t) -> p c t", c=KD)

        vec_at = {}
        for n, group in enumerate((VEC_A, VEC_B, VEC_C, VEC_D)):
            at = 0
            for name, count in group:
                vec_at[name] = (n, at, count)
                at += count

        def col(name, j):
            n, at, _ = vec_at[name]
            return vec[:, n, at + j:at + j + 1]

        s_vec, s_pos, s_route, s_x = sem("s_vec"), sem("s_pos"), sem("s_route"), sem("s_x")
        L.dma_start(arena[:, 0:TT * D].rearrange("p (t d) -> p t d", t=TT),
                    a["x"].rearrange("(t p) d -> p t d", p=P)).then_inc(s_x, 16)
        pos_i = arena[0:1, TT * D + 4 * P:TT * D + 4 * P + T].bitcast(I32)
        bias_row = small[0:1, 4:4 + GROUPS + EXPERTS]
        w_route = sb("w_route", [P, KD, GROUPS + EXPERTS])
        S.dma_start(rows, a["vectors"]).then_inc(s_vec, 16)
        S.dma_start(cst[:, :], consts).then_inc(s_vec, 16)
        S.dma_start(pos_i, a["positions"]).then_inc(s_pos, 16)
        S.dma_start(w_route[:, :, :], a["w_route"].rearrange("(k p) n -> p k n", p=P)
                    ).then_inc(s_route, 16)
        S.dma_start(bias_row, a["b_route"]).then_inc(s_route, 16)

        entries = []

        def columns(name, c0, width=CW, split=True, index=None):
            w = a[name] if index is None else a[name][index]
            entries.append((w[:, c0:c0 + width].rearrange("(k p) n -> p k n", p=P),
                            w.shape[0] // P, width, split))

        def row_block(name, r0, split=True, index=None):
            w = a[name] if index is None else a[name][index]
            entries.append((w[r0:r0 + RW * P, :].rearrange("(k p) n -> p k n", p=P), RW, D, split))

        def units(names, n, per_expert, index=None):
            gate, up, down = names
            for u in range(n):
                i, c0 = (u, 0) if per_expert else (index, u * CW)
                columns(gate, c0, index=i)
                columns(up, c0, index=i)
                if u:
                    j, r0 = (u - 1, 0) if per_expert else (index, (u - 1) * CW)
                    row_block(down, r0, index=j)
            j, r0 = (n - 1, 0) if per_expert else (index, (n - 1) * CW)
            row_block(down, r0, index=j)

        def ple_entries(i):
            row_block("ple_w_proj_2", 0, index=i)
            for c0 in range(0, D, CW):
                columns("ple_w_gate_2", c0, index=i)

        for c0 in range(0, 2 * D, CW):
            columns("w_ada", c0, split=False)
        columns("w_in", 1024)
        columns("w_in", 0)
        columns("w_in", 1280, width=160)
        for c0 in range(CW, 1024, CW):
            columns("w_in", c0)
        entries.append((a["w_q_b"].rearrange("(k p) n -> p k n", p=P), 2, HEADS * QK, False))
        entries.append((a["w_kv_b"].rearrange("(k p) n -> p k n", p=P), 1, HEADS * 128, False))
        for c0 in range(2 * D, 6 * D, CW):
            columns("w_ada", c0, split=False)
        for c0 in range(0, D, CW):
            columns("w_out", c0)
        units(("w_gate_e", "w_up_e", "w_down_e"), EXPERTS, True)
        for i in range(2):
            units(("ffn1_w_gate_2", "ffn1_w_up_2", "ffn1_w_down_2"), D_FF // CW, False, i)
            if i == 0:
                for c0 in list(range(D_RNN, 2 * D_RNN, CW)) + list(range(0, D_RNN, CW)):
                    columns("lru_w_in_2", c0)
                for r0 in range(0, D_RNN, RW * P):
                    row_block("lru_w_out_2", r0)
            else:
                entries.append((a["pool_w_2"].rearrange("g (k p) n -> p (g k) n", p=P), 8, CW,
                                True))
            units(("ffn2_w_gate_2", "ffn2_w_up_2", "ffn2_w_down_2"), D_FF // CW, False, i)
            ple_entries(i)

        s_raw = [sem(f"s_raw{i}") for i in range(N_RAW)]
        n_loaded = n_split = n_taken = 0
        raw_free = [[] for _ in range(N_RAW)]
        split_free = [None] * N_SPLIT
        where = {}
        ready = {}
        n_splits = n_returned = 0

        released = [False] * len(entries)

        def load_more():
            nonlocal n_loaded
            while n_loaded < len(entries) and (n_loaded < N_RAW or released[n_loaded - N_RAW]):
                src, k, width, _ = entries[n_loaded]
                slot = n_loaded % N_RAW
                sp.wait(*raw_free[slot])
                L.dma_start(raw[slot][:, 0:k * width].rearrange("p (k n) -> p k n", k=k),
                            src).then_inc(s_raw[slot], 16)
                n_loaded += 1

        def release(i, points):
            raw_free[i % N_RAW] = points
            released[i] = True
            load_more()

        def loaded(i):
            return s_raw[i % N_RAW], 16 * (i // N_RAW + 1)

        def split_next():
            nonlocal n_split, n_splits
            i = n_split
            n_split += 1
            _, k, width, split = entries[i]
            load_more()
            assert n_loaded > i
            if not split:
                ready[i] = [loaded(i)]
                return
            s, n, size = i % N_RAW, n_splits % N_SPLIT, k * width
            n_splits += 1
            where[i] = n
            act.wait(loaded(i))
            if split_free[n]:
                act.wait(split_free[n])
                dve.wait(split_free[n])
            hi = act.mark(S.activation(w_hi[n][:, 0:size], raw[s][:, 0:size], ACT.Copy))
            dve.wait(loaded(i), hi)
            lo = dve.mark(V.tensor_tensor(w_lo[n][:, 0:size], raw[s][:, 0:size],
                                          w_hi[n][:, 0:size].bitcast(F32), ALU.subtract))
            ready[i] = [hi, lo]
            release(i, [hi, lo])

        def take(lane=pe, ahead=True):
            nonlocal n_taken
            i = n_taken
            n_taken += 1
            while n_split <= i:
                split_next()
            if ahead:
                look_ahead(i)
            lane.wait(*ready[i])
            return i

        def look_ahead(i):
            while (n_split < n_loaded and n_split <= i + AHEAD
                   and (not entries[n_split][3] or n_splits - n_returned < N_SPLIT)):
                split_next()

        def give_back(i, point, ahead=True):
            nonlocal n_returned
            if entries[i][3]:
                split_free[where[i]] = point
                n_returned += 1
            else:
                release(i, [point])
            if ahead:
                look_ahead(i)

        def weights(i):
            _, k, width, split = entries[i]
            if not split:
                return raw[i % N_RAW][:, 0:k * width].rearrange("p (k n) -> p k n", k=k)
            n = where[i]
            return tuple(w[n][:, 0:k * width].rearrange("p (k n) -> p k n", k=k)
                         for w in (w_hi, w_lo))

        def product3(dst, w, x, first, last, check=True):
            (wh, wl), (xh, xl) = w, x
            T_.matmul(dst, wh, xh, start=first, stop=False, skip_group_check=not check)
            T_.matmul(dst, wh, xl, start=False, stop=False, skip_group_check=not check)
            return T_.matmul(dst, wl, xh, start=False, stop=last, skip_group_check=not check)

        def column_product(b, x_ready, chunks=KD, width=CW, x0=0):
            i = take()
            wh, wl = weights(i)
            pe.wait(*bank_free[b])
            m0 = 0
            while m0 < width:
                m = min(P, width - m0)
                for k in range(chunks):
                    if x_ready and m0 == 0:
                        pe.wait(x_ready[k])
                    last = product3(pair(b)[0:m, m0 // P, :],
                                    (wh[:, k, m0:m0 + m], wl[:, k, m0:m0 + m]),
                                    (a_hi[:, x0 + k, :], a_lo[:, x0 + k, :]),
                                    k == 0, k == chunks - 1)
                m0 += m
            point = pe.mark(last)
            give_back(i, point)
            return point

        def row_product(x_hi, x_lo, first, last, x_ready):
            i = take()
            wh, wl = weights(i)
            pe.wait(*x_ready)
            if first:
                for b in range(4, 8):
                    pe.wait(*bank_free[b])
            points = []
            for m in range(KD):
                for k in range(RW):
                    ins = product3(pair(4 + m // 2)[:, m % 2, :],
                                   (wh[:, k, m * P:(m + 1) * P], wl[:, k, m * P:(m + 1) * P]),
                                   (x_hi[k], x_lo[k]),
                                   first and k == 0 and m % 2 == 0, last and k == RW - 1, False)
                if last and m % 2:
                    points.append(pe.mark(ins))
            give_back(i, pe.last if last else pe.mark(ins))
            return points or [pe.last]

        operand_free = [None]

        def operand_hi(k, src, src_ready):
            act.wait(*src_ready)
            if operand_free[0]:
                act.wait(operand_free[0])
            return act.mark(S.activation(a_hi[:, k, :], src, ACT.Copy))

        def operand_lo(k, src, hi):
            if operand_free[0]:
                dve.wait(operand_free[0])
            dve.wait(hi)
            return dve.mark(V.tensor_tensor(a_lo[:, k, :], src, a_hi[:, k, :].bitcast(F32),
                                            ALU.subtract))

        def split_operand(k, src, src_ready):
            return operand_lo(k, src, operand_hi(k, src, src_ready))

        def split_stream(n, produce):
            hi, points = [], []
            for k in range(n + 1):
                if k < n:
                    hi.append(operand_hi(k, normed[:, k, :], [produce(k)]))
                if k:
                    points.append(operand_lo(k - 1, normed[:, k - 1, :], hi[k - 1]))
            return points

        squares_free, squares_ready = [None], [None]

        def square(src, k, x_ready):
            act.wait(x_ready)
            if k == 0 and squares_free[0]:
                act.wait(squares_free[0])
            done = act.mark(S.activation(squares[:, k, :], src[:, k, :], ACT.Square))
            pool.wait(done)
            if k > 1:
                pool.wait(pool.last)
            if k:
                done = pool.mark(G.tensor_tensor(squares[:, 0, :], squares[:, 0, :],
                                                 squares[:, k, :], ALU.add))
            squares_ready[0] = done

        def token_roots(total, n, roots):
            w = total.shape[-1]
            v, ta, tb = (cols[:, 16 * i:16 * i + w] for i in range(3))
            dve.wait(dve.last)
            dve.mark(V.tensor_scalar(v, total, 1.0 / n, EPS, ALU.mult, ALU.add))
            act.wait(dve.last)
            act.mark(S.activation(ta, v, ACT.Sqrt))
            dve.wait(act.last)
            dve.mark(V.reciprocal(tb, ta))
            dve.wait(dve.last)
            dve.mark(V.tensor_tensor(roots, tb, tb, ALU.mult))
            dve.wait(dve.last)
            dve.mark(V.tensor_tensor(roots, roots, v, ALU.mult))
            dve.wait(dve.last)
            dve.mark(V.tensor_scalar(roots, roots, -0.5, 1.5, ALU.mult, ALU.add))
            dve.wait(dve.last)
            return dve.mark(V.tensor_tensor(roots, roots, tb, ALU.mult))

        def as_diagonals(values, dst):
            for t in range(TT):
                dve.wait(dve.last)
                done = dve.mark(V.tensor_scalar(dst[:, t * P:(t + 1) * P], ident,
                                                values[:, t:t + 1], None, ALU.mult))
            return done

        def sum_squares_start(n_chunks, b, at=0, roots=roots2, diagonals=tmp_a):
            pe.wait(consts_ready, *bank_free[b])
            pe.wait(squares_ready[0])
            for t in range(TT):
                last = T_.matmul(bank[b][:, t:t + 1], squares[:, at, t * P:(t + 1) * P],
                                 ones[:, 0:1], start=True, stop=True)
            dve.wait(pe.mark(last))
            squares_free[0] = pe.last
            token_roots(bank[b][:, 0:TT], n_chunks * P, roots)
            bank_free[b] = [dve.last]
            return as_diagonals(roots, diagonals)

        def sum_squares_end(b, ready, diagonals=tmp_a, dst=rstd):
            pe.wait(ready, *bank_free[b])
            dve.wait(pe.mark(T_.matmul(pair(b)[:, 0, :], ones[:, :], diagonals, start=True,
                                       stop=True)), dve.last, act.last)
            point = dve.mark(V.tensor_copy(dst, pair(b)[:, 0, :]))
            bank_free[b] = [point]
            return point

        def sum_squares(n_chunks, b):
            return sum_squares_end(b, sum_squares_start(n_chunks, b))

        def rms_statistics(src, n_chunks, b, x_ready):
            for k in range(n_chunks):
                square(src, k, x_ready[k])
            return sum_squares(n_chunks, b)

        def rms_norm(gain, x_ready, shift=None):
            rms_statistics(xT, KD, 0, x_ready)

            def produce(k):
                if k == 0:
                    dve.wait(dve.last)
                done = dve.mark(V.scalar_tensor_tensor(normed[:, k, :], xT[:, k, :], gain(k),
                                                       rstd, ALU.mult, ALU.mult))
                if shift is not None:
                    dve.wait(done)
                    done = dve.mark(V.tensor_scalar(normed[:, k, :], normed[:, k, :], shift(k),
                                                    None, ALU.add))
                return done

            return split_stream(KD, produce)

        def scaled(gain, x_ready):
            def produce(k):
                dve.wait(x_ready[k])
                done = dve.mark(V.tensor_scalar(normed[:, k, :], xT[:, k, :], gain(k), None,
                                                ALU.mult))
                square(xT, k, x_ready[k])
                return done

            return split_stream(KD, produce)

        def two_column_products(b0, b1, x_ready, order=tuple(range(KD)), halfway=None):
            entries_ = [take(ahead=halfway is None) for _ in range(2)]
            ws = [weights(i) for i in entries_]
            pe.wait(*bank_free[b0], *bank_free[b1])
            for k in order:
                if halfway and k == order[KD // 2]:
                    halfway()
                pe.wait(x_ready[k])
                for b, (wh, wl) in zip((b0, b1), ws):
                    for m in range(2):
                        last = product3(pair(b)[:, m, :],
                                        (wh[:, k, m * P:(m + 1) * P], wl[:, k, m * P:(m + 1) * P]),
                                        (a_hi[:, k, :], a_lo[:, k, :]), k == order[0] and m == 0,
                                        k == order[-1], False)
            point = pe.mark(last)
            for i in entries_:
                give_back(i, point)
            return point

        def gated_units(n, x_ready, statistics=False, after_second=None, expert_gates=None,
                        before_last=None):
            hidden = [None] * n
            down_done = [None] * n
            products = [None] * n

            def product(u):
                s = u % 2
                if u == 0:
                    products[u] = two_column_products(0, 1, x_ready)
                else:
                    if u == 1 and statistics:
                        diagonals = sum_squares_start(KD, 4)
                    column_product(2 * s, None)
                    if u == 1 and statistics:
                        sum_squares_end(4, diagonals)
                        hide(0)
                    products[u] = column_product(2 * s + 1, None)

            def hide(u):
                s = u % 2
                gate_b, up_b = 2 * s, 2 * s + 1
                h = hid[:, s, :].rearrange("p (c t) -> p c t", c=2)
                act.wait(products[u])
                if u >= 2:
                    act.wait(hidden[u - 2])
                    dve.wait(hidden[u - 2])
                if expert_gates is None:
                    dve.wait(products[u], dve.last)
                    dve.mark(V.tensor_tensor(h, pair(gate_b), rstd2, ALU.mult))
                    act.wait(dve.last)
                    act.mark(S.activation(h, h, ACT.Silu))
                    bank_free[gate_b] = [dve.last]
                else:
                    act.mark(S.activation(h, pair(gate_b), ACT.Silu))
                    bank_free[gate_b] = [act.last]
                dve.wait(act.last, products[u])
                dve.mark(V.tensor_tensor(h, h, pair(up_b), ALU.mult))
                bank_free[up_b] = [dve.last]
                dve.wait(dve.last)
                scale = rstd2 if expert_gates is None else expert_gates[:, u:u + 1, :].to_broadcast(
                    [P, 2, T])
                dve.mark(V.tensor_tensor(h, h, scale, ALU.mult))
                act.wait(dve.last)
                if u >= 2:
                    act.wait(*down_done[u - 2])
                    dve.wait(*down_done[u - 2])
                act.mark(S.activation(h_hi[:, s, :], hid[:, s, :], ACT.Copy))
                dve.wait(act.last)
                hidden[u] = dve.mark(V.tensor_tensor(h_lo[:, s, :], hid[:, s, :],
                                                     h_hi[:, s, :].bitcast(F32), ALU.subtract))

            def down(u):
                s = u % 2
                hi, lo = (h[:, s, :].rearrange("p (c t) -> p c t", c=2) for h in (h_hi, h_lo))
                down_done[u] = row_product([hi[:, 0, :], hi[:, 1, :]], [lo[:, 0, :], lo[:, 1, :]],
                                           u == 0, u == n - 1, [hidden[u]])

            product(0)
            if after_second:
                product(1)
                after_second()
                hide(0)
                hide(1)
                down(0)
            else:
                product(1)
                hide(1)
                down(0)
            for u in range(2, n):
                product(u)
                hide(u)
                down(u - 1)
            if before_last:
                before_last()
            down(n - 1)
            operand_free[0] = pe.last
            return down_done[n - 1]

        def add_banks(factor, done):
            points = []
            for m in range(KD):
                dve.wait(done[m // 2])
                f = factor(m) if callable(factor) else factor
                points.append(dve.mark(V.scalar_tensor_tensor(
                    xT[:, m, :], pair(4 + m // 2)[:, m % 2, :], f, xT[:, m, :],
                    ALU.mult, ALU.add)))
                bank_free[4 + m // 2] = [dve.last]
            return points

        pool.mark(G.memset(ones[:, :], 1.0))
        consts_ready = pool.last

        def turn_vectors(groups, b):
            pe.wait((s_vec, 32), *bank_free[b])
            sizes = [sum(count for _, count in (VEC_A, VEC_B, VEC_C, VEC_D)[n]) for n in groups]
            for n, r in zip(groups, sizes):
                last = T_.transpose(bank[b][:, n * P:n * P + r], rows[0:r, n, :],
                                    ident[0:r, 0:r])
            dve.wait(pe.mark(last))
            for n, r in zip(groups, sizes):
                done = dve.mark(V.tensor_copy(vec[:, n, 0:r], bank[b][:, n * P:n * P + r]))
            bank_free[b] = [done]
            return done

        vectors = turn_vectors((0,), 0)
        c_act = small[:, 40:40 + KD]
        n, at, _ = vec_at["c"]
        act.wait(vectors)
        c_ready = act.mark(S.activation(c_act, vec[:, n, at:at + KD], ACT.Silu))

        partial = [var, tmp_b, rstd]
        partial_free, summed, n_partial = [None] * 3, [], [0]

        def sum_partials(keep=0):
            while len(summed) > keep:
                j, n, point = summed.pop(0)
                pe.wait(point, consts_ready, *bank_free[7])
                for m in range(2):
                    last = T_.matmul(bank[7][:, 2 * j + m:2 * j + m + 1],
                                     partial[n][:, m * P:(m + 1) * P], ones[:, 0:1],
                                     start=True, stop=True)
                partial_free[n] = pe.mark(last)

        def modulation_slots(first, count, both=False):
            dve.wait(c_ready, dve.last)
            for j in range(first, first + count):
                if both and j % 2 == 0:
                    i = take(pe, False)
                    w = weights(i)
                    pe.wait(c_ready, *bank_free[7])
                    for m in range(2):
                        for k in range(KD):
                            last = T_.matmul(bank[7][:, 2 * j + m:2 * j + m + 1],
                                             w[:, k, m * P:(m + 1) * P], c_act[:, k:k + 1],
                                             start=k == 0, stop=k == KD - 1)
                    give_back(i, pe.mark(last), False)
                    continue
                if not both and j % 3 == 1:
                    lane, n = pool, 2
                    i = take(act, False)
                    w, acc = weights(i), partial[n]
                    act.wait(c_ready)
                    for k in range(KD):
                        act.mark(S.activation(w[:, k, :], w[:, k, :], ACT.Copy,
                                              scale=c_act[:, k:k + 1]))
                    pool.wait(act.last)
                    for half in (4, 2):
                        pool.mark(G.tensor_tensor(w[:, 0:half, :], w[:, 0:half, :],
                                                  w[:, half:2 * half, :], ALU.add))
                        pool.wait(pool.last)
                    if partial_free[n]:
                        pool.wait(partial_free[n])
                    pool.mark(G.tensor_tensor(acc, w[:, 0, :], w[:, 1, :], ALU.add))
                else:
                    lane, n = dve, n_partial[0] % 2
                    n_partial[0] += 1
                    i = take(dve, False)
                    w, acc = weights(i), partial[n]
                    if partial_free[n]:
                        dve.wait(partial_free[n])
                    dve.mark(V.tensor_scalar(acc, w[:, 0, :], c_act[:, 0:1], None, ALU.mult))
                    for k in range(1, KD):
                        dve.wait(dve.last)
                        dve.mark(V.scalar_tensor_tensor(acc, w[:, k, :], c_act[:, k:k + 1], acc,
                                                        ALU.mult, ALU.add))
                give_back(i, lane.last, False)
                summed.append((j, n, lane.last))
                sum_partials(1 if both else 2)

        def modulation_end(first, count):
            sum_partials()
            dve.wait(pe.last, vectors)
            nb, ab, _ = vec_at["b_ada"]
            lo, hi = 2 * first, 2 * (first + count)
            dve.mark(V.tensor_tensor(mod[:, lo:hi], bank[7][:, lo:hi], vec[:, nb, ab + lo:ab + hi],
                                     ALU.add))
            bank_free[7] = [dve.last]

        def scaled_gain(row, name, at_scale):
            nn, an, _ = vec_at[name]
            dve.wait(dve.last)
            dve.mark(V.scalar_tensor_tensor(gmod[:, row, :], mod[:, at_scale:at_scale + KD], 1.0,
                                            vec[:, nn, an:an + KD], ALU.add, ALU.mult))
            dve.wait(dve.last)

        x_tok = arena[:, 0:TT * D].rearrange("p (t d) -> p t d", t=TT)
        pe.wait((s_x, 16))
        x_points = []
        for k in range(KD):
            b = 1 + k // 2
            for t in range(TT):
                last = T_.transpose(pair(b)[:, k % 2, t * P:(t + 1) * P],
                                    x_tok[:, t, k * P:(k + 1) * P], ident)
            if k % 2:
                dve.wait(pe.mark(last))
                x_points += 2 * [dve.mark(V.tensor_copy(xT[:, k - 1:k + 1, :], pair(b)))]
                bank_free[b] = [dve.last]
                square(xT, k - 1, dve.last)
                square(xT, k, dve.last)
        modulation_slots(0, 2, True)
        sum_squares(KD, 0)
        for k in range(0, KD, 2):
            dve.wait(dve.last)
            dve.mark(V.tensor_tensor(normed[:, k:k + 2, :], xT[:, k:k + 2, :], rstd2, ALU.mult))

        cosT, sinT = normed[:, KD, :], normed[:, KD + 1, :]
        pos_row = stat[0:1, 4, :]
        dve.wait((s_pos, 16))
        dve.mark(V.tensor_copy(pos_row, pos_i))
        pe.wait(dve.last, *bank_free[6])
        last = T_.matmul(pair(6)[0:QK, 0, :], ones[0:1, 0:QK], pos_row, start=True, stop=True)
        dve.wait(pe.mark(last))
        ang = cosT[0:QK, :]
        turn = tmp_a[0:QK, :]
        dve.mark(V.tensor_scalar(ang, pair(6)[0:QK, 0, :], cst[0:QK, C_FREQ:C_FREQ + 1], None,
                                 ALU.mult))
        bank_free[6] = [dve.last]
        MAGIC = 12582912.0
        for scalar, op in ((1.0 / 6.283185307179586, ALU.mult), (MAGIC, ALU.add),
                           (-MAGIC, ALU.add)):
            dve.wait(dve.last)
            dve.mark(V.tensor_scalar(turn, ang if op == ALU.mult else turn, scalar, None, op))
        for part in two_pi_parts():
            dve.wait(dve.last)
            dve.mark(V.scalar_tensor_tensor(ang, turn, -part, ang, ALU.mult, ALU.add))
        PI = 3.1415925
        dve.wait(dve.last)
        dve.mark(V.tensor_scalar(ang, ang, PI, -PI, ALU.min, ALU.max))
        act.wait(dve.last)
        act.mark(S.activation(sinT[0:QK, :], ang, ACT.Sin))
        dve.wait(dve.last)
        dve.mark(V.tensor_scalar(turn, ang, -1.0, None, ALU.mult))
        dve.wait(dve.last)
        dve.mark(V.tensor_tensor(turn, turn, ang, ALU.max))
        dve.wait(dve.last)
        dve.mark(V.tensor_scalar(turn, turn, -1.0, 1.5707963267948966, ALU.mult, ALU.add))
        act.wait(dve.last, act.last)
        rope_ready = act.mark(S.activation(cosT[0:QK, :], turn, ACT.Sin))

        modulation_slots(2, 6, True)
        look_ahead(n_taken)
        modulation_end(0, 8)
        scaled_gain(0, "norm_mix", KD)
        h_points = split_stream(KD, lambda k: dve.mark(V.tensor_scalar(
            normed[:, k, :], normed[:, k, :], gmod[:, 0, k:k + 1], mod[:, k:k + 1],
            ALU.mult, ALU.add)))

        at = [0]

        def scratch(size):
            x = arena[:, at[0]:at[0] + size]
            at[0] += size
            assert at[0] <= ARENA
            return x

        u_pad = scratch(KC * TW).rearrange("p (c t) -> p c t", c=KC)
        qk = scratch(2 * HEADS * T).rearrange("p (s h t) -> p s h t", s=2, h=HEADS)
        v_tok = scratch(TT * HEADS * VD).rearrange("p (t n) -> p t n", t=TT)
        wide = scratch(HEADS * T + HEADS * P)
        p_t = scratch(3 * HEADS * P)
        cq = p_t[:, 0:2 * T].rearrange("p (c t) -> p c t", c=2)
        ckv = p_t[:, 2 * T:3 * T].rearrange("p (c t) -> p c t", c=1)
        k_rope, k_rope_sq = p_t[0:ROPE, 3 * T:4 * T], p_t[0:ROPE, 4 * T:5 * T]
        conv = hid[:, :, :].rearrange("p s (c t) -> p (s c) t", c=2)
        qT, kT = qk[:, 0, :, :], qk[:, 1, :, :]

        turn_vectors((1, 2, 3), 6)
        vectors_ready = dve.last
        pool.wait(pe.last, dve.last)
        pad_ready = pool.mark(G.memset(u_pad[:, :, 0:PAD], 0.0))
        cq_done = two_column_products(1, 5, h_points)
        kv_done = column_product(2, None, width=160)
        act.wait(cq_done, squares_free[0], vectors_ready)
        act.mark(S.activation(cq[:, :, :], pair(1), ACT.Copy))
        bank_free[1] = [act.last]
        act.wait(act.last)
        cq_sq = act.mark(S.activation(squares[:, 0:2, :], cq[:, :, :], ACT.Square))
        pool.wait(cq_sq)
        squares_ready[0] = pool.mark(G.tensor_tensor(squares[:, 0, :], squares[:, 0, :],
                                                     squares[:, 1, :], ALU.add))
        act.wait(kv_done)
        act.mark(S.activation(ckv[:, 0, :], pair(2)[:, 0, :], ACT.Copy))
        kv_ready = act.mark(S.activation(k_rope, pair(2)[0:ROPE, 1, :], ACT.Copy))
        bank_free[2] = [kv_ready]
        act.wait(kv_ready)
        act.mark(S.activation(squares[:, 2, :], ckv[:, 0, :], ACT.Square))
        ckv_sq = act.mark(S.activation(k_rope_sq, k_rope, ACT.Square))

        val23 = column_product(6, None)
        cq_diagonals = sum_squares_start(2, 3)
        squares_ready[0] = ckv_sq
        ckv_diagonals = sum_squares_start(1, 4, 2, roots16[:, 0:TT], tmp_b)
        gate01 = column_product(7, None)
        sum_squares_end(3, cq_diagonals)
        sum_squares_end(4, ckv_diagonals, tmp_b, var)
        for k in range(2):
            dve.wait(dve.last)
            cq_ready = dve.mark(V.scalar_tensor_tensor(cq[:, k, :], cq[:, k, :],
                                                       col("q_a_norm", k), rstd,
                                                       ALU.mult, ALU.mult))
        ckv_ready = dve.mark(V.scalar_tensor_tensor(ckv[:, 0, :], ckv[:, 0, :],
                                                    col("kv_a_norm", 0), var,
                                                    ALU.mult, ALU.mult))
        gate23 = column_product(0, None)
        operand_free[0] = pe.last

        q_sq = normed[:, 0:HEADS, :]
        k_sq = wide[:, 0:HEADS * T].rearrange("p (h t) -> p h t", h=HEADS)
        i = take()
        w = weights(i)
        pe.wait(cq_ready)
        for h in range(HEADS):
            b = (1, 2, 3, 1)[h // 2]
            if h % 2 == 0:
                pe.wait(*bank_free[b])
            for k in range(2):
                last = T_.matmul(pair(b)[0:QK, h % 2, :], w[:, k, h * QK:(h + 1) * QK],
                                 cq[:, k, :], start=k == 0, stop=k == 1)
            if h % 2:
                act.wait(pe.mark(last))
                act.mark(S.activation(q_sq[0:QK, h - 1:h + 1, :], pair(b)[0:QK], ACT.Square))
                act.mark(S.activation(qT[0:QK, h - 1:h + 1, :], pair(b)[0:QK], ACT.Copy,
                                      scale=col("q_norm", 0)[0:QK]))
                bank_free[b] = [act.last]
        give_back(i, pe.last)
        q_ready = act.last

        for j, gate_done in enumerate((gate01, gate23)):
            act.wait(gate_done)
            act.mark(S.activation(conv[:, 2 * j:2 * j + 2, :], pair((7, 0)[j]), ACT.Sigmoid))
            bank_free[(7, 0)[j]] = [act.last]
            dve.wait(act.last, cq_done if j == 0 else val23)
            dve.mark(V.tensor_tensor(u_pad[:, 2 * j:2 * j + 2, PAD:], pair(5 + j),
                                     conv[:, 2 * j:2 * j + 2, :], ALU.mult))
            bank_free[5 + j] = [dve.last]
        u_ready = dve.last
        pe.wait(u_ready, pad_ready)

        i = take()
        w = weights(i)
        pe.wait(ckv_ready)
        for h in range(HEADS):
            b = (2, 3, 5, 6)[h // 2]
            if h % 2 == 0:
                pe.wait(*bank_free[b])
            last = T_.matmul(pair(b)[0:NOPE, h % 2, :], w[:, 0, h * 128:h * 128 + NOPE],
                             ckv[:, 0, :], start=True, stop=True)
            if h % 2:
                act.wait(pe.mark(last))
                act.mark(S.activation(k_sq[0:NOPE, h - 1:h + 1, :], pair(b)[0:NOPE], ACT.Square))
                act.mark(S.activation(kT[0:NOPE, h - 1:h + 1, :], pair(b)[0:NOPE], ACT.Copy,
                                      scale=col("k_norm", 0)[0:NOPE]))
                bank_free[b] = [act.last]
        k_ready = act.last
        wv = w[:, 0, :].rearrange("p (h s) -> p h s", s=128)[:, :, NOPE:128]
        for t in range(TT):
            pe.wait(*bank_free[1 + t])
            last = T_.matmul(bank[1 + t][:, :], ckv[:, 0, t * P:(t + 1) * P], wv, start=True,
                             stop=True)
            act.wait(pe.mark(last))
            v_ready = act.mark(S.activation(v_tok[:, t, :], bank[1 + t][:, :], ACT.Copy))
            bank_free[1 + t] = [act.last]
        give_back(i, pe.last)

        ring = [hid[:, n, :].rearrange("p (c m) -> p c m", c=KC) for n in range(2)]
        ring_free = [u_ready, u_ready]
        CONV_BANK = (6, 6, 0, 0)

        def tap_diagonals(k):
            group, first, _ = vec_at["conv_w"]
            w = vec[:, group, first + k * KC:first + (k + 1) * KC].rearrange(
                "p (c o) -> p c o", o=1).to_broadcast([P, KC, P])
            pool.wait(ring_free[k % 2])
            return pool.mark(G.tensor_tensor(
                ring[k % 2], ident.rearrange("p (o m) -> p o m", o=1).to_broadcast([P, KC, P]),
                w, ALU.mult))

        def convolution():
            diagonals = [tap_diagonals(0)]
            for k in range(CONV_K):
                start = PAD - (CONV_K - 1) + k
                if k + 1 < CONV_K:
                    diagonals.append(tap_diagonals(k + 1))
                if k == 0:
                    pe.wait(*bank_free[0], *bank_free[6])
                pe.wait(diagonals[k])
                for c in range(KC):
                    last = T_.matmul(pair(CONV_BANK[c])[:, c % 2, :], ring[k % 2][:, c, :],
                                     u_pad[:, c, start:start + T],
                                     start=k == 0 and c % 2 == 0, stop=k == CONV_K - 1,
                                     skip_group_check=True)
                ring_free[k % 2] = pe.mark(last)
                if k % 2 == 0:
                    modulation_slots(8 + k // 2, 1)
                yield

        steps = convolution()

        def background(n):
            for _ in range(n):
                next(steps, None)

        kr = mean[0:QK, :]
        pe.wait(kv_ready, *bank_free[3])
        last = T_.matmul(pair(3)[0:QK, 0, :], cst[0:ROPE, C_SHIFT:C_SHIFT + QK], k_rope,
                         start=True, stop=True)
        dve.wait(pe.mark(last))
        dve.mark(V.tensor_scalar(kr, pair(3)[0:QK, 0, :], col("k_norm", 0)[0:QK], None, ALU.mult))
        pe.wait(q_ready, k_ready, consts_ready, *bank_free[4])
        for t in range(TT):
            for h in range(HEADS):
                c = t * HEADS + h
                last = T_.matmul(bank[4][:, c:c + 1], q_sq[0:QK, h, t * P:(t + 1) * P],
                                 ones[0:QK, 0:1], start=True, stop=True)
        q_sums = pe.mark(last)
        pe.wait(dve.last)
        last = T_.matmul(pair(3)[0:QK, 1, :], cst[0:QK, C_ROT:C_ROT + QK], kr, start=True,
                         stop=True)
        kr_turned = pe.mark(last)
        pe.wait(*bank_free[5])
        for t in range(TT):
            for h in range(HEADS):
                c = t * HEADS + h
                T_.matmul(bank[5][:, c:c + 1], k_sq[0:NOPE, h, t * P:(t + 1) * P],
                          ones[0:NOPE, 0:1], start=True, stop=True)
            c = TT * HEADS + t
            last = T_.matmul(bank[5][:, c:c + 1], k_rope_sq[:, t * P:(t + 1) * P],
                             ones[0:ROPE, 0:1], start=True, stop=True)
        k_sums = pe.mark(last)
        background(3)
        dve.wait(kr_turned, rope_ready, dve.last)
        dve.mark(V.tensor_tensor(tmp_a[0:QK, :], pair(3)[0:QK, 1, :], sinT[0:QK, :], ALU.mult))
        bank_free[3] = [dve.last]
        dve.mark(V.tensor_tensor(kr, kr, cosT[0:QK, :], ALU.mult))
        dve.wait(dve.last)
        dve.mark(V.tensor_tensor(kr, kr, tmp_a[0:QK, :], ALU.add))
        dve.wait(dve.last)
        kr_ready = dve.mark(V.tensor_copy(
            kT[NOPE:QK, :, :], stat[NOPE:QK, 4:5, :].to_broadcast([ROPE, HEADS, T])))
        roots_k = small[:, 72:88]
        dve.wait(q_sums)
        token_roots(bank[4][:, 0:2 * HEADS], QK, roots16)
        bank_free[4] = [dve.last]
        dve.wait(k_sums, dve.last)
        sums_k, rope_sums = cols[:, 0:2 * HEADS], roots_k[:, 0:TT]
        dve.mark(V.tensor_copy(rope_sums, bank[5][:, TT * HEADS:TT * HEADS + TT]))
        dve.wait(dve.last)
        dve.mark(V.tensor_tensor(
            sums_k.rearrange("p (t h) -> p t h", t=TT),
            bank[5][:, 0:TT * HEADS].rearrange("p (t h) -> p t h", t=TT),
            rope_sums.rearrange("p (t o) -> p t o", o=1).to_broadcast([P, TT, HEADS]), ALU.add))
        token_roots(sums_k, QK, roots_k)
        bank_free[5] = [dve.last]
        for j in range(HEADS // 2):
            dve.wait(dve.last, squares_free[0])
            for h in (2 * j, 2 * j + 1):
                for t in range(TT):
                    c = t * HEADS + h
                    dve.mark(V.tensor_scalar(squares[:, h, t * P:(t + 1) * P], ident,
                                             roots_k[:, c:c + 1], None, ALU.mult))
            b = (1, 2)[j % 2]
            pe.wait(dve.last, *bank_free[b])
            spread = pe.mark(T_.matmul(pair(b)[0:QK], ones[:, 0:QK],
                                       squares[:, 2 * j:2 * j + 2, :], start=True, stop=True))
            b2 = (3, 4)[j % 2]
            pe.wait(*bank_free[b2])
            qj = qT[0:QK, 2 * j:2 * j + 2, :]
            turned = pe.mark(T_.matmul(pair(b2)[0:QK], cst[0:QK, C_ROT:C_ROT + QK], qj,
                                       start=True, stop=True))
            pool.wait(turned, rope_ready)
            pool.mark(G.tensor_tensor(qj, qj, normed[0:QK, KD:KD + 1, :].to_broadcast(
                [QK, 2, T]), ALU.mult))
            background(1)
            dve.wait(spread, k_ready)
            kj = kT[0:QK, 2 * j:2 * j + 2, :]
            dve.mark(V.tensor_tensor(kj, kj, pair(b)[0:QK], ALU.mult))
            bank_free[b] = [dve.last]
            dve.wait(turned, q_sums)
            dve.mark(V.tensor_tensor(q_sq[0:QK, 2 * j:2 * j + 2, :], pair(b2)[0:QK],
                                     normed[0:QK, KD + 1:KD + 2, :].to_broadcast([QK, 2, T]),
                                     ALU.mult))
            bank_free[b2] = [dve.last]
            dve.wait(dve.last, pool.last)
            dve.mark(V.tensor_tensor(qj, qj, q_sq[0:QK, 2 * j:2 * j + 2, :], ALU.add))
        squares_free[0] = pe.last

        s1 = wide[:, 0:HEADS * T].rearrange("p (h t) -> p h t", h=HEADS)
        s0 = wide[:, HEADS * T:].rearrange("p (h t) -> p h t", h=HEADS)
        mask2 = cst[:, C_MASK:C_MASK + P].rearrange("p (o n) -> p o n", o=1).to_broadcast(
            [P, 2, P])
        top, negative, total = small[:, 48:56], small[:, 56:64], small[:, 64:72]
        scale = float(QK) ** -0.5
        dve.wait(dve.last)
        dve.mark(V.tensor_scalar(roots16, roots16, scale, None, ALU.mult))
        pe.wait(dve.last)
        for t, s in ((0, s0), (1, s1)):
            keys = (t + 1) * P
            for h in range(HEADS):
                b, c = 1 + h // 2, h % 2
                if c == 0:
                    pe.wait(*bank_free[b])
                last = T_.matmul(pair(b)[:, c, 0:keys], qT[0:QK, h, t * P:(t + 1) * P],
                                 kT[0:QK, h, 0:keys], start=True, stop=True)
                if c == 0:
                    continue
                dve.wait(pe.mark(last))
                dve.mark(V.tensor_tensor(s[:, h - 1:h + 1, keys - P:keys],
                                         pair(b)[:, :, keys - P:keys], mask2, ALU.add))
                if t:
                    dve.mark(V.tensor_copy(s[:, h - 1:h + 1, 0:P], pair(b)[:, :, 0:P]))
                bank_free[b] = [dve.last]
            dve.wait(dve.last, act.last)
            dve.mark(V.tensor_reduce(top, s, AX, ALU.max))
            dve.wait(dve.last)
            dve.mark(V.tensor_tensor(negative, top, roots16[:, t * HEADS:(t + 1) * HEADS],
                                     ALU.mult))
            dve.wait(dve.last)
            dve.mark(V.tensor_scalar(negative, negative, -1.0, None, ALU.mult))
            act.wait(dve.last)
            for h in range(HEADS):
                act.mark(S.activation(s[:, h, :], s[:, h, :], ACT.Exp, bias=negative[:, h:h + 1],
                                      scale=roots16[:, t * HEADS + h:t * HEADS + h + 1],
                                      accum_out=total[:, h:h + 1]))
            background(6)
            dve.wait(act.last)
            dve.mark(V.reciprocal(total, total))
            dve.wait(dve.last)
            for h in range(HEADS):
                dve.mark(V.tensor_scalar(s[:, h, :], s[:, h, :], total[:, h:h + 1], None,
                                         ALU.mult))
            pe.wait(dve.last)
            for kt in range(t + 1):
                block = 0 if t == 0 else 1 + kt
                for half in range(2):
                    b = 1 + (2 * kt + half) % 4
                    pe.wait(*bank_free[b])
                    for h in range(4 * half, 4 * half + 4):
                        last = T_.transpose(bank[b][:, (h % 4) * P:(h % 4 + 1) * P],
                                            s[:, h, kt * P:(kt + 1) * P], ident)
                    act.wait(pe.mark(last), kr_ready)
                    at0 = (block * HEADS + 4 * half) * P
                    act.mark(S.activation(p_t[:, at0:at0 + 4 * P], bank[b][:, :], ACT.Copy))
                    bank_free[b] = [act.last]
            background(4)
        pt = p_t.rearrange("p (b h t) -> p b h t", b=3, h=HEADS)

        pe.wait(act.last, v_ready)
        y_points = [None] * KD
        for pair_h in range(HEADS // 2):
            b = 1 + pair_h
            pe.wait(*bank_free[b])
            for c in range(2):
                h = 2 * pair_h + c
                dst = pair(b)[c * VD:(c + 1) * VD, 0, :]
                v0, v1 = (v_tok[:, t, h * VD:(h + 1) * VD] for t in range(TT))
                T_.matmul(dst[:, 0:P], v0, pt[:, 0, h, :], start=True, stop=True,
                          skip_group_check=True)
                T_.matmul(dst[:, P:T], v0, pt[:, 1, h, :], start=False, stop=False,
                          skip_group_check=True)
                last = T_.matmul(dst[:, P:T], v1, pt[:, 2, h, :], start=False, stop=True,
                                 skip_group_check=True)
            dve.wait(pe.mark(last), dve.last)
            done = dve.mark(V.tensor_copy(normed[:, KC + pair_h, :], pair(b)[:, 0, :]))
            bank_free[b] = [done]
            y_points[KC + pair_h] = split_operand(KC + pair_h, normed[:, KC + pair_h, :], [done])
            background(1)
        background(CONV_K)
        modulation_end(8, 16)

        dve.wait(pe.last)
        for c in range(KC):
            dve.mark(V.tensor_scalar(conv[:, c, :], pair(CONV_BANK[c])[:, c % 2, :],
                                     col("conv_b", c), None, ALU.add))
        bank_free[0] = bank_free[6] = [dve.last]
        pe.wait(dve.last, *bank_free[5])
        for c in range(KC):
            last = T_.matmul(pair(5)[:, 0, :], ones[:, :], conv[:, c, :], start=c == 0,
                             stop=c == KC - 1)
        dve.wait(pe.mark(last), dve.last)
        dve.mark(V.tensor_scalar(mean, pair(5)[:, 0, :], 1.0 / CONV_CH, None, ALU.mult))
        bank_free[5] = [dve.last]

        def convolution_norm():
            act.wait(pe.last)
            for c in range(KC):
                dve.wait(dve.last)
                dve.mark(V.tensor_tensor(conv[:, c, :], conv[:, c, :], mean, ALU.subtract))
                square(conv, c, dve.last)
            sum_squares(KC, 6)
            dve.wait(dve.last)
            for c in range(KC):
                dve.mark(V.scalar_tensor_tensor(conv[:, c, :], conv[:, c, :], col("conv_ln_g", c),
                                                rstd, ALU.mult, ALU.mult))
            hi = []
            for c in range(KC):
                act.wait(dve.last)
                done = act.mark(S.activation(conv[:, c, :], conv[:, c, :], ACT.Silu,
                                             bias=col("conv_ln_b", c)))
                hi.append(operand_hi(c, conv[:, c, :], [done]))
            for c in range(KC):
                y_points[c] = operand_lo(c, conv[:, c, :], hi[c])

        x_points = []
        done01 = two_column_products(1, 2, y_points, (4, 5, 6, 7, 0, 1, 2, 3), convolution_norm)
        for j in range(4):
            done = done01 if j < 2 else column_product(1 + j, None)
            dve.wait(done)
            for c in range(2):
                m = 2 * j + c
                x_points.append(dve.mark(V.scalar_tensor_tensor(
                    xT[:, m, :], pair(1 + j)[:, c, :], mod[:, 2 * KD + m:2 * KD + m + 1],
                    xT[:, m, :], ALU.mult, ALU.add)))
            bank_free[1 + j] = [dve.last]
        operand_free[0] = pe.last

        scaled_gain(1, "norm_ffn", 4 * KD)
        h_points = rms_norm(lambda k: gmod[:, 1, k:k + 1], x_points,
                            lambda k: mod[:, 3 * KD + k:3 * KD + k + 1])
        at[0] = 0
        gate_all = scratch(EXPERTS * T).rearrange("p (e t) -> p e t", e=EXPERTS)
        gates_t = scratch(T)
        NR = GROUPS + EXPERTS
        pe.wait(dve.last, (s_route, 32), *bank_free[1])
        for t in range(TT):
            dst = bank[1][:, t * 64:t * 64 + NR]
            for k in range(KD):
                T_.matmul(dst, normed[:, k, t * P:(t + 1) * P], w_route[:, k, :], start=k == 0,
                          stop=False)
            last = T_.matmul(dst, ones[0:1, 0:P], bias_row, start=False, stop=True)
        dve.wait(pe.mark(last))
        desc = cst[:, C_DESC:C_DESC + EXPERTS]

        def wide_as(x, n):
            return x.to_broadcast([P, TT, n])

        def one_hot_of_top(dst, values, n, scr, best):
            order = desc[:, EXPERTS - n:].rearrange("p (o n) -> p o n", o=1).to_broadcast(
                [P, TT, n])
            dve.wait(dve.last)
            dve.mark(V.tensor_reduce(best, values, AX, ALU.max))
            dve.wait(dve.last)
            dve.mark(V.tensor_tensor(scr, values, wide_as(best, n), ALU.is_equal))
            dve.wait(dve.last)
            dve.mark(V.tensor_tensor(scr, scr, order, ALU.mult))
            dve.wait(dve.last)
            dve.mark(V.tensor_reduce(first_hit, scr, AX, ALU.max))
            dve.wait(dve.last)
            dve.mark(V.tensor_tensor(dst, order, wide_as(first_hit, n), ALU.is_equal))
            dve.wait(dve.last)

        lg, hot_g, scr_g, le, hot1, hot2, scr, pr = (
            scratch(TT * n).rearrange("p (t n) -> p t n", t=TT)
            for n in 3 * [GROUPS] + 5 * [EXPERTS])
        best, s_g, p2, den, first_hit = (scratch(TT).rearrange("p (t n) -> p t n", t=TT)
                                         for _ in range(5))
        logits = bank[1][:, 0:TT * 64].rearrange("p (t n) -> p t n", t=TT)
        dve.wait(act.last)
        dve.mark(V.tensor_copy(lg, logits[:, :, 0:GROUPS]))
        dve.mark(V.tensor_copy(le, logits[:, :, GROUPS:NR]))
        bank_free[1] = [dve.last]
        one_hot_of_top(hot_g, lg, GROUPS, scr_g, best)
        dve.mark(V.tensor_tensor(lg, lg, wide_as(best, GROUPS), ALU.subtract))
        act.wait(dve.last)
        act.mark(S.activation(lg, lg, ACT.Exp))
        dve.mark(V.tensor_scalar(hot_g, hot_g, -1.0, 1e30, ALU.add, ALU.mult))
        dve.wait(dve.last)
        for g in range(GROUPS):
            e0 = g * PER_GROUP
            dve.mark(V.tensor_tensor(le[:, :, e0:e0 + PER_GROUP], le[:, :, e0:e0 + PER_GROUP],
                                     wide_as(hot_g[:, :, g:g + 1], PER_GROUP), ALU.add))
        dve.wait(dve.last)
        dve.mark(V.tensor_reduce(best, le, AX, ALU.max))
        dve.wait(dve.last)
        dve.mark(V.tensor_tensor(le, le, wide_as(best, EXPERTS), ALU.subtract))
        act.wait(dve.last)
        act.mark(S.activation(pr, le, ACT.Exp))
        dve.wait(act.last)
        dve.mark(V.tensor_reduce(s_g, lg, AX, ALU.add))
        one_hot_of_top(hot1, pr, EXPERTS, scr, best)
        dve.mark(V.scalar_tensor_tensor(pr, hot1, -2.0, pr, ALU.mult, ALU.add))
        one_hot_of_top(hot2, pr, EXPERTS, scr, p2)
        dve.mark(V.tensor_tensor(den, best, p2, ALU.add))
        dve.mark(V.tensor_tensor(hot1, hot1, wide_as(best, EXPERTS), ALU.mult))
        dve.mark(V.tensor_tensor(hot2, hot2, wide_as(p2, EXPERTS), ALU.mult))
        dve.wait(dve.last)
        dve.mark(V.tensor_tensor(den, den, s_g, ALU.mult))
        dve.mark(V.tensor_tensor(hot1, hot1, hot2, ALU.add))
        dve.wait(dve.last)
        dve.mark(V.reciprocal(den, den))
        dve.wait(dve.last)
        gates_ready = dve.mark(V.tensor_tensor(hot1, hot1, wide_as(den, EXPERTS), ALU.mult))

        def finish_routing():
            pe.wait(gates_ready, *bank_free[4])
            for t in range(TT):
                last = T_.transpose(bank[4][0:EXPERTS, t * P:(t + 1) * P], hot1[:, t, :], ident)
            dve.wait(pe.mark(last))
            bank_free[4] = [dve.mark(V.tensor_copy(gates_t[0:EXPERTS, :],
                                                   bank[4][0:EXPERTS, 0:T]))]
            pe.wait(dve.last)
            spread_gates()

        def spread_gates():
            for j in range(EXPERTS // 2):
                b = 5 + j % 3
                pe.wait(*bank_free[b])
                for c in range(2):
                    e = 2 * j + c
                    last = T_.matmul(pair(b)[:, c, :],
                                     cst[0:EXPERTS, C_IDENT + e:C_IDENT + e + 1].to_broadcast(
                                         [EXPERTS, P]),
                                     gates_t[0:EXPERTS, :], start=True, stop=True)
                pe.mark(last)
                lane, eng = (act, S) if j % 2 else (dve, V)
                lane.wait(pe.last)
                dst = gate_all[:, 2 * j:2 * j + 2, :]
                if j % 2:
                    act.mark(S.activation(dst, pair(b), ACT.Copy))
                else:
                    dve.mark(V.tensor_copy(dst, pair(b)))
                bank_free[b] = [lane.last]
            dve.wait(act.last)

        done = gated_units(EXPERTS, h_points, False, finish_routing, gate_all)
        x_points = add_banks(lambda m: mod[:, 5 * KD + m:5 * KD + m + 1], done)

        BAND = 3 * P
        at[0] = 0
        s_band = sem("s_band")
        bands = []
        gates_free = (dve.last, pe.last, act.last)

        bands_ready = []

        def load_bands():
            n_band = 0
            pool.wait(*gates_free)
            for name in ("lru_w_a_2", "lru_w_x_2"):
                band = scratch(KR * BAND).rearrange("p (c n) -> p c n", c=KR)
                bands.append(band)
                pool.mark(G.memset(band, 0.0))
                pool.wait(pool.last)
                for h in range(LRU_HEADS):
                    r = h * LRU_DIM
                    while r < (h + 1) * LRU_DIM:
                        c = r // P
                        end = min((h + 1) * LRU_DIM, (c + 1) * P)
                        c0 = h * LRU_DIM - (c - 1) * P
                        G.dma_start(band[r - c * P:end - c * P, c, c0:c0 + LRU_DIM],
                                    a[name][h, r - h * LRU_DIM:end - h * LRU_DIM, :]
                                    ).then_inc(s_band, 16)
                        n_band += 16
                        r = end
            return s_band, n_band

        def ffn(which, layer, x_points, then=None, before_last=None):
            h = scaled(lambda k: col(f"{which}_norm_2", layer * KD + k), x_points)
            if then:
                then()
            return add_banks(0.5, gated_units(D_FF // CW, h, True,
                                              before_last=before_last))

        s_p = sem("s_p")

        p_tok = arena[:, 0:TT * 256].rearrange("p (t d) -> p t d", t=TT)
        pT = arena[:, TT * 256:TT * 256 + 2 * T].rearrange("p (k t) -> p k t", k=2)
        p_points = []

        def load_p(layer):
            pool.wait(dve.last, act.last, pe.last)
            G.dma_start(p_tok, a["p_2"][layer].rearrange("(t p) d -> p t d", p=P)
                        ).then_inc(s_p, 16)

        def turn_p(layer):
            pe.wait((s_p, 16 * (layer + 1)), *bank_free[2])
            for k in range(2):
                for t in range(TT):
                    last = T_.transpose(pair(2)[:, k, t * P:(t + 1) * P],
                                        p_tok[:, t, k * P:(k + 1) * P], ident)
            dve.wait(pe.mark(last), act.last)
            done = dve.mark(V.tensor_copy(pT, pair(2)))
            bank_free[2] = [done]
            p_points[:] = [split_operand(KD + k, pT[:, k, :], [done]) for k in range(2)]

        def per_layer_embedding(layer, x_points):
            sg = arena[:, 1024:1024 + D * TT].rearrange("p (m t) -> p m t", m=KD)
            proj = row_product([a_hi[:, KD, :], a_hi[:, KD + 1, :]],
                               [a_lo[:, KD, :], a_lo[:, KD + 1, :]], True, True, p_points)
            h = scaled(lambda k: col("ple_norm_2", layer * KD + k), x_points)
            points = []

            def start(j, done):
                g = sg[:, 2 * j:2 * j + 2, :]
                dve.wait(done, dve.last)
                dve.mark(V.tensor_tensor(g, pair(j), rstd2, ALU.mult))
                bank_free[j] = [dve.last]
                act.wait(dve.last)
                return act.mark(S.activation(g, g, ACT.Sigmoid))

            def end(j, sigmoid):
                g = sg[:, 2 * j:2 * j + 2, :]
                dve.wait(sigmoid, *proj)
                dve.mark(V.tensor_tensor(g, g, pair(4 + j), ALU.mult))
                bank_free[4 + j] = [dve.last]
                dve.wait(dve.last)
                x2 = xT[:, 2 * j:2 * j + 2, :]
                points.extend(2 * [dve.mark(V.tensor_tensor(x2, x2, g, ALU.add))])

            done01 = two_column_products(0, 1, h)
            diagonals = sum_squares_start(KD, 3)
            done2 = column_product(2, None)
            sum_squares_end(3, diagonals)
            done = [done01, done01, done2, None]
            dve.wait(act.last)
            for j in range(4):
                if j == 3:
                    done[j] = column_product(3, None)
                sigmoid = start(j, done[j])
                if j:
                    end(j - 1, before)
                before = sigmoid
            end(3, before)
            operand_free[0] = pe.last
            return points

        def lru(x_points):
            h = scaled(lambda k: col("mix_norm_2", k), x_points)
            nn, an, _ = vec_at["lru_a_param_2"]
            v, e, z, z2, log_rate = (small[:, 40 + i * KR:40 + (i + 1) * KR] for i in range(5))
            minus_log_rate = z
            dve.wait(act.last)
            dve.mark(V.tensor_scalar(v, vec[:, nn, an:an + KR], -1.0, None, ALU.mult))
            dve.wait(dve.last)
            dve.mark(V.tensor_tensor(e, v, vec[:, nn, an:an + KR], ALU.max))
            act.wait(dve.last)
            act.mark(S.activation(e, e, ACT.Exp, scale=-1.0))
            dve.wait(act.last)
            dve.mark(V.tensor_scalar(z, e, 2.0, None, ALU.add))
            dve.wait(dve.last)
            dve.mark(V.reciprocal(z, z))
            dve.wait(dve.last)
            dve.mark(V.tensor_tensor(z, z, e, ALU.mult))
            dve.wait(dve.last)
            dve.mark(V.tensor_tensor(z2, z, z, ALU.mult))
            dve.wait(dve.last)
            dve.mark(V.tensor_scalar(log_rate, z2, 1.0 / 17, 1.0 / 15, ALU.mult, ALU.add))
            for n in (13, 11, 9, 7, 5, 3, 1):
                dve.wait(dve.last)
                dve.mark(V.tensor_tensor(log_rate, log_rate, z2, ALU.mult))
                dve.wait(dve.last)
                dve.mark(V.tensor_scalar(log_rate, log_rate, 1.0 / n, None, ALU.add))
            dve.wait(dve.last)
            dve.mark(V.tensor_tensor(log_rate, log_rate, z, ALU.mult))
            dve.wait(dve.last)
            dve.mark(V.tensor_scalar(v, v, 0.0, None, ALU.max))
            dve.wait(dve.last)
            dve.mark(V.scalar_tensor_tensor(log_rate, log_rate, 2.0, v, ALU.mult, ALU.add))
            dve.wait(dve.last)
            dve.mark(V.tensor_scalar(minus_log_rate, log_rate, LRU_C, None, ALU.mult))
            dve.mark(V.tensor_scalar(log_rate, log_rate, -LRU_C, None, ALU.mult))
            xb = normed
            gelu = scratch(KR * T).rearrange("p (c t) -> p c t", c=KR)
            xc = scratch(KR * T).rearrange("p (c t) -> p c t", c=KR)

            def evacuate(b, dst, done):
                dve.wait(done, dve.last, act.last)
                dve.mark(V.tensor_tensor(dst, pair(b), rstd2, ALU.mult))
                bank_free[b] = [dve.last]

            def convolve(c):
                dve.wait(dve.last)
                dve.mark(V.tensor_scalar(xc[:, c, :], xb[:, c, :], col("lru_conv_w_2", 3 * KR + c),
                                         col("lru_conv_b_2", c), ALU.mult, ALU.add))
                for k in range(3):
                    shift = 3 - k
                    dve.wait(dve.last)
                    dve.mark(V.scalar_tensor_tensor(
                        xc[:, c, shift:], xb[:, c, 0:T - shift], col("lru_conv_w_2", k * KR + c),
                        xc[:, c, shift:], ALU.mult, ALU.add))
                convolved[c] = dve.last

            def gelu_pair(j):
                g = gelu[:, 2 * j:2 * j + 2, :]
                w = hid[:, j % 2, :].rearrange("p (c t) -> p c t", c=2)
                act.wait(dve.last)
                act.mark(S.activation(w, g, ACT.Square))
                act.wait(act.last)
                act.mark(S.activation(w, w, ACT.Copy, scale=0.044715, bias=1.0))
                dve.wait(act.last)
                dve.mark(V.tensor_tensor(w, w, g, ALU.mult))
                act.wait(dve.last)
                act.mark(S.activation(w, w, ACT.Tanh, scale=0.7978845608028654))

                def end():
                    dve.wait(tanh_done)
                    dve.mark(V.scalar_tensor_tensor(g, w, 1.0, g, ALU.add, ALU.mult))

                tanh_done = act.last
                return end

            HALF = KR // 2
            convolved, gate_done, y_points = [None] * KR, [None] * KR, []
            gate_bank = 2 * [3, 4, 5, 6, 7]
            a_of, i_of = (band[:, :, 0:T] for band in bands)

            def gate_products(c):
                half = c // HALF
                source = [i for i in (c - 1, c, c + 1) if i // HALF == half and i >= 0]
                b = gate_bank[c]
                pe.wait(*[convolved[i] for i in source], *bank_free[b])
                for n in range(2):
                    for i in source:
                        last = T_.matmul(pair(b)[:, n, :],
                                         bands[n][:, i, (c - i + 1) * P:(c - i + 2) * P],
                                         xc[:, i, :], start=i == source[0], stop=i == source[-1])
                gate_done[c] = pe.mark(last)

            def scan_gates(half):
                for c in range(half * HALF, (half + 1) * HALF):
                    bk = pair(gate_bank[c])
                    served = gate_done[min(c + 1, (half + 1) * HALF - 1)]
                    act.wait(served, convolved[c])
                    act.mark(S.activation(xb[:, c, :], bk[:, 0, :], ACT.Sigmoid,
                                          bias=col("lru_b_a_2", c)))
                    act.mark(S.activation(i_of[:, c, :], bk[:, 1, :], ACT.Sigmoid,
                                          bias=col("lru_b_x_2", c)))
                    bank_free[gate_bank[c]] = [act.last]
                    dve.wait(act.last, served)
                    dve.mark(V.tensor_tensor(xc[:, c, :], xc[:, c, :], i_of[:, c, :], ALU.mult))

            def scan_half(half):
                chunks = range(half * HALF, (half + 1) * HALF)
                root = xb[:, half * HALF:(half + 1) * HALF, :]
                act.wait(act.last, dve.last)
                for c in chunks:
                    act.mark(S.activation(a_of[:, c, :], xb[:, c, :], ACT.Exp,
                                          scale=log_rate[:, c:c + 1]))
                    act.mark(S.activation(i_of[:, c, :], xb[:, c, :], ACT.Tanh,
                                          scale=minus_log_rate[:, c:c + 1]))
                    act.wait(act.last)
                    act.mark(S.activation(xb[:, c, :], a_of[:, c, :], ACT.Square))
                    dve.wait(act.last)
                    dve.mark(V.scalar_tensor_tensor(xb[:, c, :], xb[:, c, :], 1.0, i_of[:, c, :],
                                                    ALU.add, ALU.mult))
                act.wait(dve.last)
                act.mark(S.activation(root, root, ACT.Sqrt))
                dve.wait(act.last)
                for c in chunks:
                    dve.mark(V.tensor_tensor(xc[:, c, :], xc[:, c, :], xb[:, c, :], ALU.mult))
                    dve.wait(dve.last)
                    dve.mark(V.tensor_tensor_scan(xb[:, c, :], a_of[:, c, :], xc[:, c, :],
                                                  0.0, ALU.mult, ALU.add))
                    dve.wait(dve.last)
                    done = dve.mark(V.scalar_tensor_tensor(gelu[:, c, :], gelu[:, c, :], 0.5,
                                                           xb[:, c, :], ALU.mult, ALU.mult))
                    if c > chunks[0]:
                        y_points.append(operand_lo(c - 1, gelu[:, c - 1, :], hi))
                    hi = operand_hi(c, gelu[:, c, :], [done])
                y_points.append(operand_lo(c, gelu[:, c, :], hi))

            done01 = two_column_products(0, 1, h)
            diagonals = sum_squares_start(KD, 3)
            done2 = column_product(2, None)
            sum_squares_end(3, diagonals)
            evacuate(0, xb[:, 0:2, :], done01)
            evacuate(1, xb[:, 2:4, :], done01)
            convolve(0)
            convolve(1)
            evacuate(2, xb[:, 4:6, :], done2)
            done = column_product(3, None)
            convolve(2)
            convolve(3)
            evacuate(3, xb[:, 6:8, :], done)
            done = column_product(0, None)
            convolve(4)
            evacuate(0, xb[:, 8:10, :], done)
            gelu_end = []
            done = column_product(1, None)
            convolve(5)
            evacuate(1, gelu[:, 0:2, :], done)
            gelu_end.append(gelu_pair(0))
            pe.wait(*bands_ready)
            for c in range(HALF):
                gate_products(c)
            convolve(6)
            done = column_product(2, None)
            scan_gates(0)
            evacuate(2, gelu[:, 2:4, :], done)
            gelu_end.append(gelu_pair(1))
            convolve(7)
            convolve(8)
            for end in gelu_end:
                end()
            done = column_product(0, None)
            convolve(9)
            evacuate(0, gelu[:, 4:6, :], done)
            gelu_pair(2)()
            for c in range(HALF, KR):
                gate_products(c)
            done3 = column_product(1, None)
            scan_gates(1)
            evacuate(1, gelu[:, 6:8, :], done3)
            gelu_end = [gelu_pair(3)]
            done4 = column_product(2, None)
            evacuate(2, gelu[:, 8:10, :], done4)
            gelu_end.append(gelu_pair(4))
            operand_free[0] = pe.last
            scan_half(0)
            for end in gelu_end:
                end()
            scan_half(1)
            for j in range(KR // 2):
                done = row_product([a_hi[:, 2 * j + c, :] for c in range(2)],
                                   [a_lo[:, 2 * j + c, :] for c in range(2)],
                                   j == 0, j == KR // 2 - 1, y_points[2 * j:2 * j + 2])
            operand_free[0] = pe.last
            return add_banks(1.0, done)

        def pooling(x_points):
            rms_norm(lambda k: col("mix_norm_2", KD + k), x_points)
            padded = arena[:, 0:3 * 2 * TW].rearrange("p (b c t) -> p b c t", b=3, c=2)
            pool.wait(dve.last, act.last, pe.last)
            pool.mark(G.memset(padded[:, :, :, 0:PAD], 0.0))
            points = []
            for g, win in enumerate(WINDOWS):
                x, s, s_next = padded[:, 0], padded[:, 1], padded[:, 2]
                dve.wait(pool.last, dve.last, act.last)
                dve.mark(V.tensor_copy(x[:, :, PAD:], normed[:, 2 * g:2 * g + 2, :]))
                src, step = x, 1
                while step < win:
                    dst = s if src is not s else s_next
                    dve.wait(dve.last)
                    dve.mark(V.tensor_tensor(dst[:, :, PAD:], src[:, :, PAD:],
                                             src[:, :, PAD - step:TW - step], ALU.add))
                    src, step = dst, 2 * step
                first = cst[:, C_COUNT + 16 * g:C_COUNT + 16 * g + 16]
                dve.wait(dve.last)
                for c in range(2):
                    dve.mark(V.tensor_tensor(src[:, c, PAD:PAD + 16], src[:, c, PAD:PAD + 16],
                                             first, ALU.mult))
                dve.mark(V.tensor_scalar(src[:, :, PAD + 16:], src[:, :, PAD + 16:], 1.0 / win,
                                         None, ALU.mult))
                dve.wait(dve.last)
                for c in range(2):
                    done = dve.mark(V.tensor_tensor(normed[:, 2 * g + c, :], src[:, c, PAD:],
                                                    x[:, c, PAD:], ALU.subtract))
                for c in range(2):
                    points.append(split_operand(2 * g + c, normed[:, 2 * g + c, :], [done]))
            i = take()
            wh, wl = weights(i)
            out_points = []
            for g in range(len(WINDOWS)):
                pe.wait(*bank_free[g])
                for m in range(2):
                    for k in range(2):
                        j = 2 * g + k
                        pe.wait(points[j])
                        last = product3(pair(g)[:, m, :],
                                        (wh[:, j, m * P:(m + 1) * P], wl[:, j, m * P:(m + 1) * P]),
                                        (a_hi[:, j, :], a_lo[:, j, :]), k == 0, k == 1)
                dve.wait(pe.mark(last), dve.last)
                for m in range(2):
                    c = 2 * g + m
                    dve.mark(V.tensor_scalar(tmp_a, pair(g)[:, m, :], col("pool_b_2", c),
                                             col("pool_scale_2", c), ALU.add, ALU.mult))
                    dve.wait(dve.last)
                    out_points.append(dve.mark(V.tensor_tensor(xT[:, c, :], xT[:, c, :], tmp_a,
                                                               ALU.add)))
                    dve.wait(dve.last)
                bank_free[g] = [dve.last]
            give_back(i, pe.last)
            operand_free[0] = pe.last
            return out_points

        x_points = ffn("ffn1", 0, x_points, lambda: bands_ready.append(load_bands()))
        x_points = lru(x_points)
        x_points = ffn("ffn2", 0, x_points, lambda: load_p(0), lambda: turn_p(0))
        x_points = per_layer_embedding(0, x_points)
        x_points = ffn("ffn1", 1, x_points)
        x_points = pooling(x_points)
        x_points = ffn("ffn2", 1, x_points, lambda: load_p(1), lambda: turn_p(1))
        x_points = per_layer_embedding(1, x_points)

        rms_statistics(xT, KD, 0, x_points)
        y_tok = arena[:, 0:TT * D].rearrange("p (t d) -> p t d", t=TT)
        s_out = sem("s_out")
        for k in range(KD):
            dve.wait(dve.last)
            dve.mark(V.scalar_tensor_tensor(normed[:, k, :], xT[:, k, :], col("final_norm_2", k),
                                            rstd, ALU.mult, ALU.mult))
        pe.wait(dve.last)
        for t in range(TT):
            for half in range(2):
                b = 1 + 2 * t + half
                pe.wait(*bank_free[b])
                for k in range(4):
                    last = T_.transpose(bank[b][:, k * P:(k + 1) * P],
                                        normed[:, 4 * half + k, t * P:(t + 1) * P], ident)
                act.wait(pe.mark(last), dve.last)
                act.mark(S.activation(y_tok[:, t, half * 512:(half + 1) * 512], bank[b][:, :],
                                      ACT.Copy))
            sp.wait(act.last)
            L.dma_start(out[t * P:(t + 1) * P, :], y_tok[:, t, :]).then_inc(s_out, 16)
        L.wait_ge(s_out, 16 * TT)
        assert n_taken == len(entries)


def two_pi_parts():
    import math
    rest, parts = 2 * math.pi, []
    for bits in (8, 8, 8):
        exponent = math.floor(math.log2(rest)) + 1
        unit = 2.0 ** (exponent - bits)
        part = math.floor(rest / unit) * unit
        parts.append(part)
        rest -= part
    return parts + [rest]


def constants():
    import numpy as np
    c = np.zeros((P, C_END), np.float32)
    c[:, C_IDENT:C_IDENT + P] = np.eye(P, dtype=np.float32)
    half = ROPE // 2
    for j in range(half):
        c[NOPE + half + j, C_ROT + NOPE + j] = -1.0
        c[NOPE + j, C_ROT + NOPE + half + j] = 1.0
    c[0:CHUNK, C_MASK + CHUNK:C_MASK + P] = -1e30
    freq = 10000.0 ** (-np.arange(0, ROPE, 2) / ROPE)
    c[NOPE:NOPE + half, C_FREQ] = freq
    c[NOPE + half:QK, C_FREQ] = freq
    for g, win in enumerate(WINDOWS):
        for t in range(16):
            c[:, C_COUNT + 16 * g + t] = 1.0 / min(t + 1, win)
    c[:, C_DESC:C_DESC + EXPERTS] = np.arange(EXPERTS, 0, -1)
    c[0:ROPE, C_SHIFT + NOPE:C_SHIFT + QK] = np.eye(ROPE)
    return c


NAMES = ["x", "positions", "w_ada", "w_in", "w_q_b", "w_kv_b", "w_out", "w_gate_e", "w_up_e",
         "w_down_e", "p_2", "ffn1_w_gate_2", "ffn1_w_up_2", "ffn1_w_down_2", "lru_w_in_2",
         "lru_w_a_2", "lru_w_x_2", "lru_w_out_2", "pool_w_2", "ffn2_w_gate_2", "ffn2_w_up_2",
         "ffn2_w_down_2", "ple_w_gate_2", "ple_w_proj_2"]
KEEP_LEADING = {"positions", "p_2", "ffn1_w_gate_2", "ffn1_w_up_2", "ffn1_w_down_2",
                "ffn2_w_gate_2", "ffn2_w_up_2", "ffn2_w_down_2", "ple_w_gate_2", "ple_w_proj_2"}


def kernel(**inputs):
    import numpy as np
    import concourse.bacc as bacc
    from concourse.bass_utils import run_bass_kernel_spmd

    nc = bacc.Bacc("TRN2", target_bir_lowering=False, num_devices=1)
    arrays, aps = {}, {}
    for name in NAMES:
        array = np.ascontiguousarray(inputs[name])
        if name not in KEEP_LEADING:
            array = array.reshape(array.shape[1:])
        if name == "p_2":
            array = array.reshape(2, T, 256)
        arrays["in_" + name] = array
        aps[name] = nc.dram_tensor("in_" + name, array.shape, mybir.dt.from_np(array.dtype),
                                   kind="ExternalInput").ap()
    vectors = np.zeros((P, 4, P), np.float32)
    for n, group in enumerate((VEC_A, VEC_B, VEC_C, VEC_D)):
        at = 0
        for name, count in group:
            flat = np.ravel(inputs[name])
            rows = vectors[at:at + count, n, :]
            if flat.size == rows.size:
                rows[...] = flat.reshape(count, P)
            else:
                rows[0, :flat.size] = flat
            at += count
    packed = {"vectors": vectors,
              "w_route": np.concatenate([inputs["w_group"][0], inputs["w_expert"][0]], axis=1),
              "b_route": np.concatenate([inputs["b_group"], inputs["b_expert"]], axis=1)}
    for name, array in packed.items():
        arrays["in_" + name] = np.ascontiguousarray(array)
        aps[name] = nc.dram_tensor("in_" + name, array.shape, F32, kind="ExternalInput").ap()
    arrays["in_constants"] = constants()
    consts = nc.dram_tensor("in_constants", (P, C_END), F32, kind="ExternalInput").ap()
    out = nc.dram_tensor("out", (T, D), F32, kind="ExternalOutput").ap()
    build(nc, aps, consts, out)
    result = run_bass_kernel_spmd(nc, [arrays], core_ids=[0])
    return result.results[0]["out"].reshape(1, T, D)
```
